# Optimizing a Trainium2 kernel written in Bass

```python
import jax
import jax.numpy as jnp
from jax import lax
import numpy as np

D_MODEL = 1024
BATCH = 1
SEQ = 256
DEPTH = 2

GRID_W = 64
CTX_LEN = 256

FNET_GROUPS = 4
FNET_CH = 64
D_FNET = FNET_GROUPS * FNET_CH

MLA_HEADS = 6
MLA_Q_RANK = 256
MLA_KV_RANK = 128
MLA_NOPE = 64
MLA_ROPE = 32
MLA_QK = MLA_NOPE + MLA_ROPE
MLA_V = 64

SWA_HEADS = 6
SWA_KV_HEADS = 2
SWA_HEAD_DIM = 64
WINDOW = 128
BLOCK = 128
Q_BLOCK = 128

D_MIX = D_FNET + MLA_HEADS * MLA_V + SWA_HEADS * SWA_HEAD_DIM
IN_SIZES = (D_FNET, MLA_Q_RANK, MLA_KV_RANK, MLA_ROPE,
            SWA_HEADS * SWA_HEAD_DIM, SWA_KV_HEADS * SWA_HEAD_DIM, SWA_KV_HEADS * SWA_HEAD_DIM)
D_IN = sum(IN_SIZES)
IN_SPLITS = tuple(int(v) for v in np.cumsum(IN_SIZES)[:-1])

N_EXPERTS = 16
N_EXPERT_GROUPS = 4
EXPERTS_PER_GROUP = N_EXPERTS // N_EXPERT_GROUPS
TOP_K = 2
D_EXPERT = 512

ROPE_THETA = 10000.0
EPS = 1e-6

kernel_name = "hybrid_dit_fnet_mla_swa_moe"

def rmsnorm(x, g):
    xf = x.astype(jnp.float32)
    y = xf * lax.rsqrt(jnp.mean(xf * xf, axis=-1, keepdims=True) + EPS)
    return (y * g.astype(jnp.float32)).astype(x.dtype)

def axial_rope_table(rows, cols, d_rot):
    d_axis = d_rot // 2
    inv = ROPE_THETA ** (-jnp.arange(0, d_axis, 2, dtype=jnp.float32) / d_axis)
    ar = rows.astype(jnp.float32)[:, None] * inv
    ac = cols.astype(jnp.float32)[:, None] * inv
    ang = jnp.concatenate([ar, ar, ac, ac], axis=-1)
    return jnp.cos(ang)[:, None, :], jnp.sin(ang)[:, None, :]

def apply_axial_rope(x, cos, sin):
    a1, a2, b1, b2 = jnp.split(x, 4, axis=-1)
    rot = jnp.concatenate([-a2, a1, -b2, b1], axis=-1)
    return (x * cos + rot * sin).astype(x.dtype)

def rope_tail(x, cos, sin):
    return jnp.concatenate([x[..., :MLA_NOPE], apply_axial_rope(x[..., MLA_NOPE:], cos, sin)], axis=-1)

def mixer_inputs(h, w_in, cq_g, ckv_g, w_uq, w_uk, w_uv, mq_g, mk_g, sq_g, sk_g, rope, with_queries=True):
    B, N, _ = h.shape
    p = h @ w_in
    u_f, cq, ckv, k_r, q_s, k_s, v_s = jnp.split(p, IN_SPLITS, axis=-1)
    ckv = rmsnorm(ckv, ckv_g)
    k_nope = (ckv @ w_uk).reshape(B, N, MLA_HEADS, MLA_NOPE)
    v_m = (ckv @ w_uv).reshape(B, N, MLA_HEADS, MLA_V)
    k_rope = jnp.broadcast_to(k_r[:, :, None, :], (B, N, MLA_HEADS, MLA_ROPE))
    k_m = rmsnorm(jnp.concatenate([k_nope, k_rope], axis=-1), mk_g)
    k_s = rmsnorm(k_s.reshape(B, N, SWA_KV_HEADS, SWA_HEAD_DIM), sk_g)
    v_s = v_s.reshape(B, N, SWA_KV_HEADS, SWA_HEAD_DIM)
    if rope is not None:
        cos_m, sin_m, cos_s, sin_s = rope
        k_m = rope_tail(k_m, cos_m, sin_m)
        k_s = apply_axial_rope(k_s, cos_s, sin_s)
    if not with_queries:
        return None, None, k_m, v_m, None, k_s, v_s
    q_m = rmsnorm((rmsnorm(cq, cq_g) @ w_uq).reshape(B, N, MLA_HEADS, MLA_QK), mq_g)
    q_s = rmsnorm(q_s.reshape(B, N, SWA_HEADS, SWA_HEAD_DIM), sq_g)
    if rope is not None:
        q_m = rope_tail(q_m, cos_m, sin_m)
        q_s = apply_axial_rope(q_s, cos_s, sin_s)
    return u_f, q_m, k_m, v_m, q_s, k_s, v_s

def fourier_mix(u, w):
    B, N, _ = u.shape
    ug = u.reshape(B, N, FNET_GROUPS, FNET_CH).astype(jnp.float32)
    f = jnp.fft.fft2(ug, axes=(1, 3), norm='ortho').real.astype(u.dtype)
    return jnp.einsum('bngc,gce->bnge', f, w).reshape(B, N, D_FNET)

def dense_attend_blocks(q, k, v):
    B, S, H, d = q.shape
    nb = S // Q_BLOCK
    qb = jnp.moveaxis(q.reshape(B, nb, Q_BLOCK, H, d), 1, 0)
    scale = d ** -0.5

    def one_block(qi):
        s = jnp.einsum('bqhd,bkhd->bhqk', qi, k, preferred_element_type=jnp.float32) * scale
        p = jax.nn.softmax(s, axis=-1).astype(v.dtype)
        return jnp.einsum('bhqk,bkhd->bqhd', p, v)

    out = lax.map(one_block, qb)
    return jnp.moveaxis(out, 0, 1).reshape(B, S, H * v.shape[-1])

def window_attend(q, k, v, k_ctx, v_ctx, sink):
    B, S, H, d = q.shape
    kvh = k.shape[2]
    g = H // kvh
    nb = S // BLOCK
    qb = q.reshape(B, nb, BLOCK, kvh, g, d)

    def band(t):
        tp = jnp.pad(t, ((0, 0), (BLOCK, BLOCK), (0, 0), (0, 0)))
        tb = tp.reshape(B, nb + 2, BLOCK, kvh, d)
        return jnp.concatenate([tb[:, :-2], tb[:, 1:-1], tb[:, 2:]], axis=2)

    kb, vb = band(k), band(v)
    scale = d ** -0.5
    s_loc = jnp.einsum('bnqkgd,bnjkd->bnkgqj', qb, kb, preferred_element_type=jnp.float32) * scale
    kpos = jnp.arange(3 * BLOCK) - BLOCK
    rel = kpos[None, :] - jnp.arange(BLOCK)[:, None]
    kabs = jnp.arange(nb)[:, None, None] * BLOCK + kpos[None, None, :]
    valid = (jnp.abs(rel) <= WINDOW)[None] & (kabs >= 0) & (kabs < S)
    s_loc = jnp.where(valid[None, :, None, None], s_loc, -jnp.inf)
    s_ctx = jnp.einsum('bnqkgd,bjkd->bnkgqj', qb, k_ctx, preferred_element_type=jnp.float32) * scale
    s_sink = jnp.broadcast_to(sink.astype(jnp.float32).reshape(1, 1, kvh, g, 1, 1), s_loc.shape[:-1] + (1,))
    p = jax.nn.softmax(jnp.concatenate([s_loc, s_ctx, s_sink], axis=-1), axis=-1).astype(v.dtype)
    n_loc = 3 * BLOCK
    n_ctx = k_ctx.shape[1]
    out = (jnp.einsum('bnkgqj,bnjkd->bnqkgd', p[..., :n_loc], vb)
           + jnp.einsum('bnkgqj,bjkd->bnqkgd', p[..., n_loc:n_loc + n_ctx], v_ctx))
    return out.reshape(B, S, H * d)

def context_gqa_attend(q, k, v, sink):
    B, C, H, d = q.shape
    kvh = k.shape[2]
    g = H // kvh
    qg = q.reshape(B, C, kvh, g, d)
    s = jnp.einsum('bqkgd,bjkd->bkgqj', qg, k, preferred_element_type=jnp.float32) * d ** -0.5
    s_sink = jnp.broadcast_to(sink.astype(jnp.float32).reshape(1, kvh, g, 1, 1), s.shape[:-1] + (1,))
    p = jax.nn.softmax(jnp.concatenate([s, s_sink], axis=-1), axis=-1).astype(v.dtype)
    out = jnp.einsum('bkgqj,bjkd->bqkgd', p[..., :k.shape[1]], v)
    return out.reshape(B, C, H * d)

def moe_ffn(h, router_w, router_b, w_gate, w_up, w_down):
    T = h.shape[0]
    aff = jax.nn.sigmoid(jnp.einsum('td,de->te', h, router_w, preferred_element_type=jnp.float32))
    sel = aff + router_b.astype(jnp.float32)
    gscore = lax.top_k(sel.reshape(T, N_EXPERT_GROUPS, EXPERTS_PER_GROUP), TOP_K)[0].sum(-1)
    gbest = jnp.argmax(gscore, axis=-1)
    in_group = (jnp.arange(N_EXPERTS) // EXPERTS_PER_GROUP)[None, :] == gbest[:, None]
    _, idx = lax.top_k(jnp.where(in_group, sel, -jnp.inf), TOP_K)
    wsel = jnp.take_along_axis(aff, idx, axis=-1)
    wsel = wsel / jnp.sum(wsel, axis=-1, keepdims=True)
    gates = jnp.einsum('tk,tke->te', wsel, jax.nn.one_hot(idx, N_EXPERTS, dtype=jnp.float32)).astype(h.dtype)
    y = jnp.zeros_like(h)
    for e in range(N_EXPERTS):
        a = jax.nn.silu(h @ w_gate[e]) * (h @ w_up[e])
        y = y + gates[:, e:e + 1] * (a @ w_down[e])
    return y

def setup_inputs(seed: int = 0) -> dict:
    key = jax.random.key(seed)
    ks = jax.random.split(key, 26)
    f32 = jnp.float32

    def nrm(k, shape, fan_in, mult=1.0):
        return jax.random.normal(k, shape, f32) * (mult * fan_in ** -0.5)

    def gain(k, shape):
        return 1.0 + 0.1 * jax.random.normal(k, shape, f32)

    return {
        'x': jax.random.normal(ks[0], (BATCH, SEQ, D_MODEL), f32),
        'c': jax.random.normal(ks[1], (BATCH, D_MODEL), f32),
        'ctx': jax.random.normal(ks[2], (BATCH, CTX_LEN, D_MODEL), f32),
        'c_ctx': jax.random.normal(ks[3], (D_MODEL,), f32),
        'ada_w': nrm(ks[4], (DEPTH, D_MODEL, 6 * D_MODEL), D_MODEL, 0.5),
        'ada_b': 0.02 * jax.random.normal(ks[5], (DEPTH, 6 * D_MODEL), f32),
        'norm1_g': gain(ks[6], (DEPTH, D_MODEL)),
        'norm2_g': gain(ks[7], (DEPTH, D_MODEL)),
        'w_in': nrm(ks[8], (DEPTH, D_MODEL, D_IN), D_MODEL),
        'fnet_w': nrm(ks[9], (DEPTH, FNET_GROUPS, FNET_CH, FNET_CH), FNET_CH),
        'mla_cq_g': gain(ks[10], (DEPTH, MLA_Q_RANK)),
        'mla_ckv_g': gain(ks[11], (DEPTH, MLA_KV_RANK)),
        'mla_w_uq': nrm(ks[12], (DEPTH, MLA_Q_RANK, MLA_HEADS * MLA_QK), MLA_Q_RANK),
        'mla_w_uk': nrm(ks[13], (DEPTH, MLA_KV_RANK, MLA_HEADS * MLA_NOPE), MLA_KV_RANK),
        'mla_w_uv': nrm(ks[14], (DEPTH, MLA_KV_RANK, MLA_HEADS * MLA_V), MLA_KV_RANK),
        'mla_q_g': gain(ks[15], (DEPTH, MLA_QK)),
        'mla_k_g': gain(ks[16], (DEPTH, MLA_QK)),
        'swa_q_g': gain(ks[17], (DEPTH, SWA_HEAD_DIM)),
        'swa_k_g': gain(ks[18], (DEPTH, SWA_HEAD_DIM)),
        'swa_sink': 0.5 * jax.random.normal(ks[19], (DEPTH, SWA_HEADS), f32),
        'w_out': nrm(ks[20], (DEPTH, D_MIX, D_MODEL), D_MIX),
        'router_w': nrm(ks[21], (D_MODEL, N_EXPERTS), D_MODEL),
        'router_b': 0.01 * jax.random.normal(ks[22], (N_EXPERTS,), f32),
        'exp_w_gate': nrm(ks[23], (DEPTH, N_EXPERTS, D_MODEL, D_EXPERT), D_MODEL),
        'exp_w_up': nrm(ks[24], (DEPTH, N_EXPERTS, D_MODEL, D_EXPERT), D_MODEL),
        'exp_w_down': nrm(ks[25], (DEPTH, N_EXPERTS, D_EXPERT, D_MODEL), D_EXPERT),
    }

def reference(x, c, ctx, c_ctx, ada_w, ada_b, norm1_g, norm2_g, w_in, fnet_w,
              mla_cq_g, mla_ckv_g, mla_w_uq, mla_w_uk, mla_w_uv, mla_q_g, mla_k_g,
              swa_q_g, swa_k_g, swa_sink, w_out, router_w, router_b,
              exp_w_gate, exp_w_up, exp_w_down):
    B, S, D = x.shape
    C = ctx.shape[1]
    ROWS = S // GRID_W
    rows = jnp.repeat(jnp.arange(ROWS), GRID_W)
    cols = jnp.arange(ROWS * GRID_W) % GRID_W
    rope = axial_rope_table(rows, cols, MLA_ROPE) + axial_rope_table(rows, cols, SWA_HEAD_DIM)
    silu_c = jax.nn.silu(c)
    silu_cc = jax.nn.silu(c_ctx)

    for l in range(DEPTH):
        last = l == DEPTH - 1
        sh1, sc1, g1, sh2, sc2, g2 = jnp.split((silu_c @ ada_w[l] + ada_b[l])[:, None, :], 6, axis=-1)
        csh1, csc1, cg1, csh2, csc2, cg2 = jnp.split(silu_cc @ ada_w[l] + ada_b[l], 6, axis=-1)
        mix_w = (w_in[l], mla_cq_g[l], mla_ckv_g[l], mla_w_uq[l], mla_w_uk[l], mla_w_uv[l],
                 mla_q_g[l], mla_k_g[l], swa_q_g[l], swa_k_g[l])

        hx = rmsnorm(x, norm1_g[l]) * (1.0 + sc1) + sh1
        hc = rmsnorm(ctx, norm1_g[l]) * (1.0 + csc1) + csh1
        fx, qmx, kmx, vmx, qsx, ksx, vsx = mixer_inputs(hx, *mix_w, rope=rope)
        fc, qmc, kmc, vmc, qsc, ksc, vsc = mixer_inputs(hc, *mix_w, rope=None, with_queries=not last)
        out_x = jnp.concatenate([
            fourier_mix(fx, fnet_w[l]),
            dense_attend_blocks(qmx, jnp.concatenate([kmx, kmc], axis=1), jnp.concatenate([vmx, vmc], axis=1)),
            window_attend(qsx, ksx, vsx, ksc, vsc, swa_sink[l]),
        ], axis=-1)
        x = x + g1 * (out_x @ w_out[l])
        if not last:
            out_c = jnp.concatenate([
                fourier_mix(fc, fnet_w[l]),
                dense_attend_blocks(qmc, kmc, vmc),
                context_gqa_attend(qsc, ksc, vsc, swa_sink[l]),
            ], axis=-1)
            ctx = ctx + cg1 * (out_c @ w_out[l])

        moe_w = (router_w, router_b, exp_w_gate[l], exp_w_up[l], exp_w_down[l])
        h2x = (rmsnorm(x, norm2_g[l]) * (1.0 + sc2) + sh2).reshape(B * S, D)
        if last:
            x = x + g2 * moe_ffn(h2x, *moe_w).reshape(B, S, D)
        else:
            h2c = (rmsnorm(ctx, norm2_g[l]) * (1.0 + csc2) + csh2).reshape(B * C, D)
            y = moe_ffn(jnp.concatenate([h2x, h2c], axis=0), *moe_w)
            x = x + g2 * y[:B * S].reshape(B, S, D)
            ctx = ctx + cg2 * y[B * S:].reshape(B, C, D)
    return x


_drawn_inputs = setup_inputs


def setup_inputs(seed=0):
    import zlib

    import numpy as np

    out = dict(_drawn_inputs(seed))
    spreads = {}
    factors = {'mla_cq_g': 5.393,
     'mla_q_g': 4.294,
     'mla_k_g': 3.991,
     'swa_q_g': 4.523,
     'swa_k_g': 2.816,
     'swa_sink': 64.0}
    for name, (base, spread) in spreads.items():
        noise = np.random.default_rng([zlib.crc32(name.encode()), seed]).standard_normal(out[name].shape)
        drawn = base * np.exp(spread * noise) if base else spread * noise
        out[name] = jnp.asarray(drawn.astype(out[name].dtype))
    for name, factor in factors.items():
        out[name] = (out[name] * factor).astype(out[name].dtype)
    return out
```

```python
from contextlib import ExitStack

import concourse.bass as bass
from concourse import mybir

F32 = mybir.dt.float32
F32R = mybir.dt.float32r
BF16 = mybir.dt.bfloat16
F16 = mybir.dt.float16
I32 = mybir.dt.int32
ALU = mybir.AluOpType
ACT = mybir.ActivationFunctionType
AX = mybir.AxisListType

P = 128
D = 1024
KT = D // P
DEPTH = 2
SEQ = 256
XT = SEQ // P
NTILES = 4
CQ, CKV, KR, QS, KS, VS, D_IN = 256, 512, 640, 672, 1056, 1184, 1312
NH, QKD, HD, KVH = 6, 96, 64, 2
VM = CQ
NE, GROUP = 16, 4
EPS = 1e-6
BIG = 1 << 20
SLOTS = 128

RAW = 4
SPL = 3
CHUNK = 512
ADA_CHUNKS = 6 * D // CHUNK
ADA_BODY = 6
IN_UNITS, OUT_UNITS, EXP_UNITS = 6, 4, 6
LAYER_UNITS = IN_UNITS + OUT_UNITS + NE * EXP_UNITS
IN_WIDTH = (512, 512, 288)

C_ID, C_DFT, C_CHAN, C_ROPE, C_IOTA, C_LT, C_DIAG, C_INVN, C_HALF = (
    0, 128, 1152, 1408, 1792, 1920, 1936, 1952, 1962)
C_TOK = 1976
CONST_W = 1984
N_SMALL = 14
B_ID, B_MASK, B_TRI, B_ONE = 0, 128, 640, 768
CONST_B = 896
G_CQ, G_CKV, G_MQ, G_MK, G_SQ, G_SK, G_W = 0, 256, 384, 480, 576, 640, 704


class Stage:

    def __init__(self, sem, items=()):
        self.sem = sem
        self.count = {item: n + 1 for n, item in enumerate(items)}

    def after(self, item):
        return self.count[item]


def u_in(l):
    return DEPTH * 2 * ADA_CHUNKS + l * LAYER_UNITS


def u_out(l):
    return u_in(l) + IN_UNITS


def u_exp(l):
    return u_out(l) + OUT_UNITS


def stream(t):
    return 0 if t < XT else 1


def plus(n, times, i):
    return n if i is None else i * times + n


def in_tiles(l, chunk):
    return [2, 3, 0, 1] if l == 0 or chunk else [0, 1]


def out_tiles(l):
    return [2, 3, 0, 1] if l == 0 else [0, 1]


def jobs(l):
    return [1, 0] if l == 0 else [0]


def prep_uses(l, t):
    q = l == 0 or t < XT
    return (["c"] + ["q0", "q1"] * q + ["k", "v"] + ["tq0", "tq1"] * q + ["tk0", "tk1"] + ["sq"] * q + ["sk"])


def build(nc, x, c, ctx, c_ctx, ada_w, ada_b, norm1_g, norm2_g, w_in, fnet_w, mla_cq_g, mla_ckv_g,
          mla_w_uq, mla_w_uk, mla_w_uv, mla_q_g, mla_k_g, swa_q_g, swa_k_g, swa_sink, w_out, router_w,
          router_b, exp_w_gate, exp_w_up, exp_w_down, consts, consts_b, out):
    es = ExitStack()

    def sem(name):
        return es.enter_context(nc.semaphore(name))

    def sb(name, shape, dt=F32):
        return es.enter_context(nc.sbuf_tensor(name, shape, dt))

    ps = es.enter_context(nc.psum_tensor("ps", [P, 8, 512], F32))

    raw = [sb(f"raw{i}", [P, 4, 512]) for i in range(RAW)]
    whi = [sb(f"whi{i}", [P, 4, 512], F32R) for i in range(SPL)]
    wlo = [sb(f"wlo{i}", [P, 4, 512], F32R) for i in range(SPL)]
    t_hi = sb("t_hi", [P, KT, NTILES * P], F32R)
    t_lo = sb("t_lo", [P, KT, NTILES * P], F32R)
    cst = sb("cst", [P, CONST_W])
    cstb = sb("cstb", [P, CONST_B], BF16)
    w_uq = sb("w_uq", [P, 2, NH * QKD])
    w_ukv = sb("w_ukv", [P, 2, NH * HD])
    gains = sb("gains", [P, G_W])
    sinks = sb("sinks", [P, 2, NH])
    wbd = sb("wbd", [P, 2, P])
    mch = sb("mch", [P, 2, 2, P])
    rwf = sb("rwf", [P, KT, NE])
    rw_hi = sb("rw_hi", [P, KT, NE], F32R)
    rw_lo = sb("rw_lo", [P, KT, NE], F32R)
    rb = sb("rb", [P, NE])
    ss = sb("ss", [P, 4])
    ms = sb("ms", [P, 4])
    rstd = sb("rstd", [P, 4])
    ss2 = sb("ss2", [P, 16])
    rs2 = sb("rs2", [P, 16])

    KIB = 1024
    region = es.enter_context(nc.sbuf_tensor("region", [P, 71 * KIB // 4], F32))
    r_base = nc.lookup_mloc(region).addr

    def at(name, off, shape, dt=F32):
        return nc.alloc_sbuf_tensor_at(name, shape, dt, offset=r_base + off)

    xs = at("xs", 0, [P, NTILES, D])
    gb = at("gb", 16 * KIB, [P, 2, D])
    xn = at("xn", 24 * KIB, [P, 2, D])
    hg = at("hg", 24 * KIB, [P, 2, D])
    s_act = at("s_act", 32 * KIB, [P, 512])
    a_act = at("a_act", 34 * KIB, [P, 512])
    at_hi = at("at_hi", 36 * KIB, [P, 4, P], F32R)
    at_lo = at("at_lo", 38 * KIB, [P, 4, P], F32R)
    yb = at("yb", 40 * KIB, [P, 2, D])
    otmp = at("otmp", 40 * KIB, [P, 2, CHUNK])
    junk = at("junk", 44 * KIB, [P, D])
    hgt_hi = at("hgt_hi", 48 * KIB, [P, 2, KT, P], F32R)
    hgt_lo = at("hgt_lo", 56 * KIB, [P, 2, KT, P], F32R)
    ab = at("ab", 48 * KIB, [P, 2, 2, D])
    yy = at("yy", 48 * KIB, [P, 2, 2, D])
    rt_off = 64 * KIB
    rt_names = {}

    def rt(name, shape, dt=F32, size=4):
        nonlocal rt_off
        n = 1
        for s in shape[1:]:
            n *= s
        t = at(name, rt_off, shape, dt)
        rt_off += (n * size + 31) // 32 * 32
        assert rt_off <= 71 * KIB
        return t

    aff = rt("aff", [P, 4, NE])
    sel = rt("sel", [P, 4, NE])
    pair = at("pair", 34 * KIB, [P, 16, 4, 4])
    pair2 = at("pair2", 35 * KIB, [P, 16, 4, 4])
    gsc = rt("gsc", [P, 4, 4])
    gcnt = rt("gcnt", [P, 4, 4])
    best = rt("best", [P, 4, 4])
    cnt = rt("cnt", [P, 4, NE])
    msk = rt("msk", [P, 4, NE])
    mskb = rt("mskb", [P, 4, NE], BF16, 2)
    den = rt("den", [P, 8])
    gate = rt("gate", [P, 4, NE])
    gres = rt("gres", [P, 4, NE])
    posm = rt("posm", [P, 4, NE], F16, 2)
    posf = rt("posf", [P, 4, NE])
    iota16 = rt("iota16", [P, P], F16, 2)
    pay = rt("pay", [P, 4, NE, 8], BF16, 2)
    oh = at("oh", 32 * KIB, [P, 2, 4, P], BF16)
    info = rt("info", [P, NE, 8])
    tokf = rt("tokf", [P, NE])
    oobf = rt("oobf", [P, NE])
    gate_s = rt("gate_s", [P, NE])
    idxg = rt("idxg", [P, NE], I32)
    idxs = rt("idxs", [P, NE], I32)
    cur_g = rt("cur_g", [P, 2], I32)
    cur_s = rt("cur_s", [P, 2], I32)
    most = rt("most", [P, 1], I32)
    info_o = rt("info_o", [P, 8])
    calc_o = rt("calc_o", [P, 4])
    idx_o = rt("idx_o", [P, 2], I32)
    tick = rt("tick", [P, 1])

    c_raw = at("c_raw", 24 * KIB, [P, KT, 2])
    c_act = at("c_act", 25 * KIB, [P, KT, 2])
    c_st = at("c_st", 28 * KIB, [P, KT, P], F32R)
    rowp = at("rowp", 32 * KIB, [4, 2, 512])
    row2 = at("row2", 36 * KIB, [2, 2, 512])
    bias2 = at("bias2", 40 * KIB, [2, 2, 512])
    comb = at("comb", 44 * KIB, [4, P])
    cb_raw = at("cb_raw", 60 * KIB, [P, CONST_B])

    pr = at("pr", 0, [P, NTILES, D_IN])
    o = NTILES * D_IN * 4
    qk = at("qk", o, [P, 2 * NH, QKD]); o += 2 * NH * QKD * 4
    sq = at("sq", o, [P, 2 * NH * QKD]); o += 2 * NH * QKD * 4
    cn = at("cn", o, [P, 384]); o += 384 * 4
    ct = at("ct", o, [P, 3, P]); o += 384 * 4
    kdup = at("kdup", o, [P, 2, 2, HD]); o += 256 * 4
    qt_m = at("qt_m", o, [QKD, NH, 256]); o += NH * 256 * 4
    qt_s = at("qt_s", o, [P, 3, 256]); o += 3 * 256 * 4
    kt_m = at("kt_m", o, [QKD, NH, 512]); o += NH * 512 * 4
    kt_s = at("kt_s", o, [P, KVH, 512]); o += KVH * 512 * 4
    pb = at("pb", o, [P, 2, 512]); o += 1024 * 4
    ptb = at("ptb", o, [P, 2, 4, 256]); o += 2048 * 4
    fab = at("fab", o - 4096, [P, 2, 2, 256])
    mx = at("mx", o, [P, 2]); o += 32
    nb = at("nb", o, [P, 2]); o += 32
    sm = at("sm", o, [P, 2]); o += 32
    esk = at("esk", o, [P, 2]); o += 32
    ri = at("ri", o, [P, 2]); o += 32
    assert o <= 71 * KIB, o

    ada_d = nc.dram_tensor("ada_rows", (2, DEPTH * 6 * D), F32).ap()
    h2_d = nc.dram_tensor("h2_rows", (NTILES * P, D), F32).ap()
    y_d = nc.dram_tensor("y_rows", (NTILES * P * 2, D), F32).ap()
    x_d = nc.dram_tensor("x_rows", (SEQ, D), F32).ap()

    identf = cst[:, C_ID:C_ID + P]
    identb = cstb[:, B_ID:B_ID + P]
    dft = cst[:, C_DFT:C_DFT + 1024].rearrange("p (k n) -> p k n", k=2)
    chan = cst[:, C_CHAN:C_CHAN + 256].rearrange("p (s n) -> p s n", s=2)
    rope = cst[:, C_ROPE:C_ROPE + 384].rearrange("p (t n) -> p t n", t=2)
    half = cst[:, C_HALF:C_HALF + 12]
    maskb = cstb[:, B_MASK:B_MASK + 512].rearrange("p (t n) -> p t n", t=2)

    L = range(DEPTH)
    const_in, small_in, x_in = sem("const_in"), sem("small_in"), sem("x_in")
    w_landed = [sem(f"w_landed{i}") for i in range(RAW)]
    w_hi, w_lo, w_used = sem("w_hi"), sem("w_lo"), sem("w_used")
    setup_dve, setup_act = sem("setup_dve"), sem("setup_act")
    dve_chain, act_chain, pool_chain = sem("dve_chain"), sem("act_chain"), sem("pool_chain")
    ada_copied, ada_comb, ada_row = sem("ada_copied"), sem("ada_comb"), sem("ada_row")
    ada_bias_in = [sem(f"ada_bias_in{i}") for i in range(2)]
    ada_stored = [sem(f"ada_stored{i}") for i in range(2)]
    ab_in, gb_in = sem("ab_in"), sem("gb_in")
    norms = [(l, w) for l in L for w in (1, 2)]

    def norm_tiles(l, w):
        return [2, 3, 0, 1] if w == 1 else out_tiles(l)

    tile_items = [(l, w, t) for l, w in norms for t in norm_tiles(l, w)]
    ab_ready = Stage(sem("ab_ready"), norms)
    sumsq = Stage(sem("sumsq"), tile_items)
    mean_ready = Stage(sem("mean_ready"), tile_items)
    rstd_ready = Stage(sem("rstd_ready"), tile_items)
    h_ready = Stage(sem("h_ready"), tile_items)
    ht_full = Stage(sem("ht_full"), tile_items)
    ht_hi = Stage(sem("ht_hi"), tile_items)
    ht_split = Stage(sem("ht_split"), tile_items)
    h2_items = [i for i in tile_items if i[1] == 2]
    h2_stored = [sem(f"h2_stored{i}") for i in range(2)]

    p_items = [(l, ch, t) for l in L for ch in range(3) for t in in_tiles(l, ch)]
    p_full = Stage(sem("p_full"), [i for i in p_items if i[2] != in_tiles(i[0], i[1])[-1]])
    p_act = Stage(sem("p_act"), [i for i in p_items if i[2] >= XT])
    p_dve = Stage(sem("p_dve"), [i for i in p_items if i[2] < XT])

    ring_items = []
    for l in L:
        ring_items.append((l, "m"))
        for s in jobs(l) if l == 0 else [1, 0]:
            for t in (2, 3) if s else (0, 1):
                ring_items += [(l, t, u) for u in prep_uses(l, t)]
            if s in jobs(l):
                ring_items += [(l, s, "f0"), (l, s, "f1"), (l, s, "fy")]
    ring_pos = {it: n for n, it in enumerate(ring_items)}
    ring_full = Stage(sem("ring_full"), ring_items)
    ring_free = Stage(sem("ring_free"), ring_items)
    fm_items = [(l, s) for l in L for s in jobs(l)]
    fmix_hi = Stage(sem("fmix_hi"), fm_items)
    fmix_lo = Stage(sem("fmix_lo"), fm_items)
    prep_items = [(l, t) for l in L for t in (2, 3, 0, 1)]
    c_mean, c_rstd, cn_ready, sw_done = (Stage(sem(n), prep_items) for n in ("c_mean", "c_rstd", "cn_ready", "sw_done"))
    qk_mean, qk_rstd, qk_done = (Stage(sem(n), prep_items) for n in ("qk_mean", "qk_rstd", "qk_done"))
    m_ready = sem("m_ready")

    units = [(l, s, h, q) for l in L for s in jobs(l) for h in range(2 * NH) for q in range(2)]
    unit_pos = {u: n for n, u in enumerate(units)}
    heads = [(l, s, h) for l in L for s in jobs(l) for h in range(2 * NH)]
    s_full, nb_ready, exp_done, r_ready, p_norm, pt_full, pt_copied = (
        Stage(sem(n), units) for n in ("s_full", "nb_ready", "exp_done", "r_ready", "p_norm", "pt_full", "pt_copied"))
    o_full, mix_hi, mix_lo = (Stage(sem(n), heads) for n in ("o_full", "mix_hi", "mix_lo"))

    out_items = [(l, ch, t) for l in L for ch in range(2) for t in out_tiles(l)]
    op_scaled, x_upd = (Stage(sem(n), out_items) for n in ("op_scaled", "x_upd"))
    op_full = Stage(sem("op_full"), [i for i in out_items if i[2] != out_tiles(i[0])[-1]])

    def await_p(eng, l, ch, t):
        if t == in_tiles(l, ch)[-1]:
            eng.wait_ge(w_used, u_in(l) + 2 * ch + 2)
        else:
            eng.wait_ge(p_full.sem, p_full.after((l, ch, t)))

    def await_op(eng, l, ch, t):
        if t == out_tiles(l)[-1]:
            eng.wait_ge(w_used, u_out(l) + 2 * ch + 2)
        else:
            eng.wait_ge(op_full.sem, op_full.after((l, ch, t)))

    lg_full, aff_ready, msk_ready, pos_full, info_full, idx_ready = (
        sem(n) for n in ("lg_full", "aff_ready", "msk_ready", "pos_full", "info_full", "idx_ready"))
    oh_ready, oh_used = sem("oh_ready"), sem("oh_used")
    gathered = [sem(f"gathered{i}") for i in range(2)]
    scattered = [sem(f"scattered{i}") for i in range(2)]
    silu_done, a_ready, ta_full, at_hi_done, at_split = (
        sem(n) for n in ("silu_done", "a_ready", "ta_full", "at_hi_done", "at_split"))
    y_ready, tg_full, hgt_hi_done, hgt_split, cur_g_ready, cur_s_ready = (
        sem(n) for n in ("y_ready", "tg_full", "hgt_hi_done", "hgt_split", "cur_g_ready", "cur_s_ready"))
    y_in = [sem(f"y_in{i}") for i in range(2)]
    fin_items = [(l, t) for l in L for t in out_tiles(l)]
    y_sum = Stage(sem("y_sum"), fin_items)
    x_fin = Stage(sem("x_fin"), fin_items)
    x_stored = sem("x_stored")

    def layer_sems(name):
        return [sem(f"{name}_{l}") for l in L]

    v_turn, v_oh, v_info, v_idx, v_step, v_gathered, v_scattered = (layer_sems(n) for n in (
        "v_turn", "v_oh", "v_info", "v_idx", "v_step", "v_gathered", "v_scattered"))
    v_rows_full, v_rows_hi, v_rows_lo, v_silu, v_act, v_act_full, v_act_hi, v_act_lo, v_y = (layer_sems(n) for n in (
        "v_rows_full", "v_rows_hi", "v_rows_lo", "v_silu", "v_act", "v_act_full", "v_act_hi", "v_act_lo", "v_y"))
    v_landed = [[sem(f"v_landed{j}_{l}") for j in range(SPL)] for l in L]
    v_hi, v_lo, v_used, v_shift = (layer_sems(n) for n in ("v_hi", "v_lo", "v_used", "v_shift"))

    def more_rounds(l):
        return len(out_tiles(l)) * P // SLOTS - 1

    def overflow(eng, l, one_round, each=None):
        eng.wait_ge(idx_ready, l + 1)
        biggest = eng.value_load(most[0:1, 0:1], min_val=0, max_val=NTILES * P)
        with eng.If(biggest > SLOTS):
            with eng.Fori(0, more_rounds(l)) as c:
                if each is not None:
                    each(c)
                with eng.Fori(0, NE) as e:
                    n = c * NE + e
                    eng.wait_ge(v_turn[l], n + 1)
                    if each is not None:
                        eng.wait_ge(v_shift[l], c + 1)
                    one_round(e, n)
            eng.wait_ge(v_turn[l], more_rounds(l) * NE + 1)

    N_CONST = 7

    def make_chain(eng, s):
        n = [0]

        def link(ins):
            n[0] += 1
            ins.then_inc(s, 1)
            eng.wait_ge(s, n[0])
        return link

    def load_unit(sp, u, src, i=None, width=512):
        if u >= RAW:
            sp.wait_ge(w_lo, plus(u - RAW + 1, 12, i))
        sp.dma_start(raw[u % RAW][:, :, 0:width], src).then_inc(w_landed[u % RAW], 16)

    def split_hi(act, u, i=None, width=512):
        act.wait_ge(w_landed[u % RAW], plus(16 * (u // RAW + 1), 48, i))
        if u >= SPL:
            act.wait_ge(w_used, plus(u - SPL + 1, 12, i))
        nc.scalar.activation(whi[u % SPL][:, :, 0:width], raw[u % RAW][:, :, 0:width], ACT.Copy).then_inc(w_hi, 1)

    def split_lo(dve, u, i=None, width=512):
        dve.wait_ge(w_hi, plus(u + 1, 12, i))
        nc.vector.tensor_tensor(wlo[u % SPL][:, :, 0:width], raw[u % RAW][:, :, 0:width],
                                whi[u % SPL][:, :, 0:width].bitcast(F32), ALU.subtract).then_inc(w_lo, 1)

    def await_unit(pe, u, i=None):
        pe.wait_ge(w_lo, plus(u + 1, 12, i))

    def product3(out_, hi, lo, whi_, wlo_, first, last):
        nc.tensor.matmul(out_, hi, whi_, start=first, stop=False)
        nc.tensor.matmul(out_, hi, wlo_, start=False, stop=False)
        return nc.tensor.matmul(out_, lo, whi_, start=False, stop=last)

    def ada_src(l, i, j, kh):
        v = ada_w[l].rearrange("(kh kk p) n -> kh p kk n", kh=2, p=P)
        return v[kh][:, :, bass.ds(i * (ADA_BODY * CHUNK) + j * CHUNK, CHUNK)]

    def in_src(l, ch, kh):
        return w_in[l].rearrange("(kh kk p) n -> kh p kk n", kh=2, p=P)[kh][:, :, ch * 512:ch * 512 + IN_WIDTH[ch]]

    def out_src(l, ch, kh):
        return w_out[l].rearrange("(kh kk p) n -> kh p kk n", kh=2, p=P)[kh][:, :, ch * 512:(ch + 1) * 512]

    def e_src(w, l, e, part):
        we = w[l][bass.ds(e, 1)]
        if part < 2:
            return we.rearrange("e (kh kk p) n -> kh p (e kk) n", kh=2, p=P)[part]
        return we.rearrange("e (kk p) n -> p (e kk) n", p=P)[:, :, (part - 2) * 512:(part - 1) * 512]

    def after_turn(l, e):
        return u_exp(l) + 6 * e + 4

    def e_base(l, e_s):
        return u_exp(l) + (0 if e_s == 0 else 4 + 6 * (e_s - 1))

    def ada_pass(eng, body):
        body(0, 0, None, 0)
        body(0, ADA_BODY, None, 1)
        with eng.Fori(0, 2) as i:
            body(1, 2 * ADA_BODY, i, i)

    def ab_src(s, l, k):
        off = (l * 6 + k) * D
        return ada_d[s, off:off + D].partition_broadcast(P)

    def row_bc(v, l, n):
        return v[l, 0:n].partition_broadcast(P)

    block = es.enter_context(nc.Block())

    @block.sync
    def _(sp):
        sp.dma_start(cst[:], consts[:, 0:CONST_W]).then_inc(const_in, 16)
        sp.dma_start(comb[:], consts[0:4, CONST_W:CONST_W + P]).then_inc(const_in, 16)
        sp.dma_start(cb_raw[:], consts_b).then_inc(const_in, 16)
        with nc.allow_non_contiguous_dma(reason="two vectors, once"):
            sp.dma_start(c_raw[:, :, 0:1], c.rearrange("a (k p) -> p k a", p=P)).then_inc(const_in, 16)
            sp.dma_start(c_raw[:, :, 1:2], c_ctx.rearrange("(k p a) -> p k a", p=P, a=1)).then_inc(const_in, 16)
        sp.dma_start(rwf[:], router_w.rearrange("(k p) e -> p k e", p=P)).then_inc(const_in, 16)
        sp.dma_start(rb[:], router_b.partition_broadcast(P)).then_inc(const_in, 16)

        def ada_loads(l, g, i, col):
            for j in range(ADA_BODY):
                for kh in range(2):
                    load_unit(sp, 2 * (g + j) + kh, ada_src(l, col, j, kh), i)
        ada_pass(sp, ada_loads)
        for l in L:
            for ch in range(3):
                for kh in range(2):
                    load_unit(sp, u_in(l) + 2 * ch + kh, in_src(l, ch, kh), width=IN_WIDTH[ch])
            for ch in range(2):
                for kh in range(2):
                    load_unit(sp, u_out(l) + 2 * ch + kh, out_src(l, ch, kh))

            def turn(e, e_s, i, first=False):
                b = e_base(l, e_s)
                for kh in range(2):
                    load_unit(sp, b + kh, e_src(exp_w_gate, l, e, kh), i)
                n = 2
                if not first:
                    for ch in range(2):
                        load_unit(sp, b + 2 + ch, e_src(exp_w_down, l, e - 1, 2 + ch), i)
                    n = 4
                for kh in range(2):
                    load_unit(sp, b + n + kh, e_src(exp_w_up, l, e, kh), i)

            turn(0, 0, None, True)
            with sp.Fori(0, 7) as i:
                turn(i * 2 + 1, 1, i)
                turn(i * 2 + 2, 2, i)
            turn(15, 15, None)
            for ch in range(2):
                load_unit(sp, e_base(l, 16) + ch, e_src(exp_w_down, l, 15, 2 + ch))

            def one_round(e, n):
                for j in range(EXP_UNITS):
                    if j >= SPL:
                        sp.wait_ge(v_lo[l], n * EXP_UNITS + (j - SPL + 1))
                    w = (exp_w_gate, exp_w_up, exp_w_down)[j // 2]
                    sp.dma_start(raw[j % SPL][:], e_src(w, l, e, j % 2 + 2 * (j >= 4))).then_inc(v_landed[l][j % SPL], 16)
            overflow(sp, l, one_round)

    @block.tensor
    def _(pe):
        def ada(l, g0, i, col):
            for j in range(ADA_BODY):
                g = g0 + j
                if g >= 2:
                    pe.wait_ge(ada_copied, plus(g - 1, ADA_BODY, i))
                for kh in range(2):
                    u = 2 * g + kh
                    await_unit(pe, u, i)
                    for kk in range(4):
                        k = 4 * kh + kk
                        nc.tensor.matmul(ps[:, g % 2, :], c_st[:, k, :], whi[u % SPL][:, kk, :], start=k == 0, stop=False)
                        mm = nc.tensor.matmul(ps[:, g % 2, :], c_st[:, k, :], wlo[u % SPL][:, kk, :], start=False, stop=k == KT - 1)
                    mm.then_inc(w_used, 1)
                if g >= 1:
                    combine(g - 1, i)

        def combine(g, i):
            pe.wait_ge(ada_copied, plus(g + 1, ADA_BODY, i))
            if g >= 2:
                pe.wait_ge(ada_row, plus(g - 1, ADA_BODY, i))
            nc.tensor.matmul(ps[:, 2 + g % 2, :], comb[:], rowp[0:4, g % 2, :],
                             start=True, stop=True).then_inc(ada_comb, 1)

        pe.wait_ge(const_in, 16 * N_CONST)
        pe.wait_ge(setup_dve, 5)
        ada_pass(pe, ada)
        combine(2 * ADA_CHUNKS - 1, None)

        def norm(l, w):
            tiles = norm_tiles(l, w)
            if w == 2:
                pe.wait_ge(op_scaled.sem, op_scaled.after((l, 1, tiles[-1])))
            elif l:
                pe.wait_ge(y_ready, NE * l)
            else:
                pe.wait_ge(ada_row, 2 * ADA_CHUNKS)
            for n, t in enumerate(tiles):
                pe.wait_ge(h_ready.sem, h_ready.after((l, w, t)))
                if n >= 2:
                    pe.wait_ge(ht_split.sem, ht_split.after((l, w, tiles[n - 2])))
                for k in range(KT):
                    mm = nc.tensor.transpose(ps[:, 2 * (n % 2) + k // 4, k % 4 * P:(k % 4 + 1) * P],
                                             xn[:, n % 2, k * P:(k + 1) * P], identf)
                mm.then_inc(ht_full.sem, 1)

        def in_proj(l):
            pe.wait_ge(ht_split.sem, ht_split.after((l, 1, norm_tiles(l, 1)[-1])))
            for ch in range(3):
                n = IN_WIDTH[ch]
                bank = 4 if ch % 2 == 0 else 0
                if ch == 2:
                    pe.wait_ge(p_dve.sem, p_dve.after((l, 0, 1)))
                    if l == 0:
                        pe.wait_ge(p_act.sem, p_act.after((l, 0, 3)))
                tiles = in_tiles(l, ch)
                for kh in range(2):
                    u = u_in(l) + 2 * ch + kh
                    await_unit(pe, u)
                    for t in tiles:
                        for kk in range(4):
                            k = 4 * kh + kk
                            mm = product3(ps[:, bank + t, 0:n], t_hi[:, k, t * P:(t + 1) * P], t_lo[:, k, t * P:(t + 1) * P],
                                          whi[u % SPL][:, kk, 0:n], wlo[u % SPL][:, kk, 0:n], k == 0, k == KT - 1)
                        if kh == 1 and t != tiles[-1]:
                            mm.then_inc(p_full.sem, 1)
                    mm.then_inc(w_used, 1)

        def ring(item):
            n = ring_pos[item]
            if n >= 3:
                pe.wait_ge(ring_free.sem, n - 2)
            return n % 3

        def channel_mix(l):
            pe.wait_ge(small_in, 16 * N_SMALL * (l + 1))
            b = ring((l, "m"))
            for pr_ in range(2):
                for cs in range(2):
                    o_ = (2 * pr_ + cs) * P
                    mm = nc.tensor.matmul(ps[:, b, o_:o_ + P], chan[:, cs, :], wbd[:, pr_, :], start=True, stop=True)
            mm.then_inc(ring_full.sem, 1)

        def prep(l, t):
            q = l == 0 or t < XT
            pe.wait_ge(cn_ready.sem, cn_ready.after((l, t)))
            b = ring((l, t, "c"))
            for n in range(3) if q else [2]:
                mm = nc.tensor.transpose(ps[:, b, n * P:(n + 1) * P], cn[:, n * P:(n + 1) * P], identf)
            mm.then_inc(ring_full.sem, 1)
            pe.wait_ge(ring_free.sem, ring_free.after((l, t, "c")))
            if q:
                for n in range(2):
                    b = ring((l, t, f"q{n}"))
                    for k in range(2):
                        mm = nc.tensor.matmul(ps[:, b, 0:288], ct[:, k, :], w_uq[:, k, n * 288:(n + 1) * 288],
                                              start=k == 0, stop=k == 1)
                    mm.then_inc(ring_full.sem, 1)
            for n, what in enumerate("kv"):
                b = ring((l, t, what))
                nc.tensor.matmul(ps[:, b, 0:384], ct[:, 2, :], w_ukv[:, n, :], start=True, stop=True).then_inc(ring_full.sem, 1)
            pe.wait_ge(qk_done.sem, qk_done.after((l, t)))
            for what, h0 in (("tq", 0), ("tk", NH)):
                if what == "tq" and not q:
                    continue
                for n in range(2):
                    b = ring((l, t, f"{what}{n}"))
                    for h in range(4 * n, min(4 * n + 4, NH)):
                        mm = nc.tensor.transpose(ps[0:QKD, b, (h - 4 * n) * P:(h - 4 * n + 1) * P], qk[:, h0 + h, :], identf)
                    mm.then_inc(ring_full.sem, 1)
            pe.wait_ge(sw_done.sem, sw_done.after((l, t)))
            if q:
                b = ring((l, t, "sq"))
                for n in range(3):
                    mm = nc.tensor.transpose(ps[:, b, n * P:(n + 1) * P], pr[:, t, QS + n * P:QS + (n + 1) * P], identf)
                mm.then_inc(ring_full.sem, 1)
            b = ring((l, t, "sk"))
            for n in range(KVH):
                mm = nc.tensor.transpose(ps[:, b, n * P:(n + 1) * P], kdup[:, n, :, :].rearrange("p a d -> p (a d)"), identf)
            mm.then_inc(ring_full.sem, 1)

        def fourier(l, s):
            for ch in range(2):
                b = ring((l, s, f"f{ch}"))
                for k in range(XT):
                    mm = nc.tensor.matmul(ps[:, b, :], pr[:, 2 * s + k, ch * P:(ch + 1) * P], dft[:, k, :],
                                          start=k == 0, stop=k == XT - 1)
                mm.then_inc(ring_full.sem, 1)
            pe.wait_ge(ring_free.sem, ring_free.after((l, s, "f1")))
            b = ring((l, s, "fy"))
            for ch in range(2):
                for cs in range(2):
                    mm = nc.tensor.matmul(ps[:, b, ch * 256:(ch + 1) * 256], mch[:, ch, cs, :], fab[:, ch, cs, :],
                                          start=cs == 0, stop=cs == 1)
            mm.then_inc(ring_full.sem, 1)

        def attend(l, s):
            us = [(l, s, h, q) for h in range(2 * NH) for q in range(2)]
            nk = 4 if s == 0 else 2
            key0 = 0 if s == 0 else 256
            if unit_pos[us[0]] == 0:
                pe.wait_ge(ring_free.sem, ring_free.after((l, s, "fy")))

            def scores(n):
                _, _, h, q = u = us[n]
                g = unit_pos[u]
                if g >= 2:
                    pe.wait_ge(exp_done.sem, g - 1)
                b = 4 + g % 2
                cols = slice(q * P, (q + 1) * P)
                if h < NH:
                    mm = nc.tensor.matmul(ps[:, b, 0:nk * P], qt_m[:, h, cols], kt_m[:, h, key0:key0 + nk * P],
                                          start=True, stop=True)
                else:
                    r = 64 * ((h - NH) % 2)
                    for k0 in range(0, nk * P, 256):
                        masked = s == 0 and k0 == 0
                        mm = nc.tensor.matmul(ps[:, b, k0:k0 + 256], qt_s[r:r + 64, (h - NH) // 2, cols],
                                              kt_s[r:r + 64, (h - NH) // 3, key0 + k0:key0 + k0 + 256],
                                              start=True, stop=not masked)
                        if masked:
                            mm = nc.tensor.matmul(ps[:, b, 0:256], identb, maskb[:, q, :], start=False, stop=True)
                mm.then_inc(s_full.sem, 1)

            def turn_probs(n):
                u = us[n]
                g = unit_pos[u]
                pe.wait_ge(p_norm.sem, p_norm.after(u))
                if g >= 2:
                    pe.wait_ge(pt_copied.sem, g - 1)
                for j in range(nk):
                    mm = nc.tensor.transpose(ps[:, 6 + g % 2, j * P:(j + 1) * P], pb[:, g % 2, j * P:(j + 1) * P], identf)
                mm.then_inc(pt_full.sem, 1)

            def values(h):
                pe.wait_ge(pt_copied.sem, pt_copied.after((l, s, h, 1)))
                hn = heads.index((l, s, h))
                if hn:
                    pe.wait_ge(mix_lo.sem, hn)
                col = 256 + HD * h
                r = col % P
                for j in range(nk):
                    kt = j if s == 0 else 2 + j
                    v0 = VM + HD * h if h < NH else VS + HD * ((h - NH) // 3)
                    mm = nc.tensor.matmul(ps[r:r + 64, 3, 0:256], pr[:, kt, v0:v0 + HD], ptb[:, h % 2, j, :],
                                          start=j == 0, stop=j == nk - 1)
                mm.then_inc(o_full.sem, 1)

            for n in range(len(us) + 3):
                if n < len(us):
                    scores(n)
                if n >= 4 and n % 2 == 0:
                    values((n - 4) // 2)
                if 2 <= n < len(us) + 2:
                    turn_probs(n - 2)

        def out_proj(l):
            pe.wait_ge(mix_lo.sem, mix_lo.after((l, 0, 2 * NH - 1)))
            pe.wait_ge(fmix_lo.sem, fmix_lo.after((l, 0)))
            for ch in range(2):
                bank = 4 if ch == 0 else 0
                tiles = out_tiles(l)
                for kh in range(2):
                    u = u_out(l) + 2 * ch + kh
                    await_unit(pe, u)
                    for t in tiles:
                        for kk in range(4):
                            k = 4 * kh + kk
                            mm = product3(ps[:, bank + t, :], t_hi[:, k, t * P:(t + 1) * P], t_lo[:, k, t * P:(t + 1) * P],
                                          whi[u % SPL][:, kk, :], wlo[u % SPL][:, kk, :], k == 0, k == KT - 1)
                        if kh == 1 and t != tiles[-1]:
                            mm.then_inc(op_full.sem, 1)
                    mm.then_inc(w_used, 1)

        def route(l):
            tiles = out_tiles(l)
            nt = len(tiles)
            pe.wait_ge(ht_split.sem, ht_split.after((l, 2, tiles[-1])))
            for t in tiles:
                for k in range(KT):
                    mm = product3(ps[:, 4, t * NE:(t + 1) * NE], t_hi[:, k, t * P:(t + 1) * P], t_lo[:, k, t * P:(t + 1) * P],
                                  rw_hi[:, k, :], rw_lo[:, k, :], k == 0, k == KT - 1)
            mm.then_inc(lg_full, 1)
            pe.wait_ge(msk_ready, l + 1)
            for t in range(nt + 1):
                last = min(t, nt - 1)
                for t2 in range(last + 1):
                    mm = nc.tensor.matmul(ps[:, 5, t * NE:(t + 1) * NE], cstb[:, (B_TRI if t2 == t else B_ONE):][:, 0:P],
                                          mskb[:, t2, :], start=t2 == 0, stop=t2 == last)
            mm.then_inc(pos_full, 1)
            for e in range(NE):
                pe.wait_ge(oh_ready, l * NE + e + 1)
                for t in range(nt):
                    mm = nc.tensor.matmul(ps[:, 6, e * 8:(e + 1) * 8], oh[:, e % 2, t, :], pay[:, t, e, :],
                                          start=t == 0, stop=t == nt - 1)
                mm.then_inc(oh_used, 1)

        def turn_rows(l, e, par, i):
            pe.wait_ge(gathered[par], plus(16 * (l * 8 + e // 2 + 1), 16, i))
            if l or e:
                pe.wait_ge(hgt_split, plus(l * NE + e, 2, i))
            for k in range(KT):
                mm = nc.tensor.transpose(ps[:, k // 4, k % 4 * P:(k % 4 + 1) * P], hg[:, par, k * P:(k + 1) * P], identf)
            mm.then_inc(tg_full, 1)

        def experts_half(bank, par, kh, u, i):
            await_unit(pe, u, i)
            for kk in range(4):
                k = 4 * kh + kk
                mm = product3(ps[:, bank, :], hgt_hi[:, par, k, :], hgt_lo[:, par, k, :],
                              whi[u % SPL][:, kk, :], wlo[u % SPL][:, kk, :], k == 0, k == KT - 1)
            mm.then_inc(w_used, 1)

        def turn_act(l, e, i):
            pe.wait_ge(a_ready, plus(l * NE + e + 1, 2, i))
            if l or e or i is not None:
                pe.wait_ge(at_split, plus(l * NE + e, 2, i))
            for k in range(4):
                mm = nc.tensor.transpose(ps[:, 4, k * P:(k + 1) * P], a_act[:, k * P:(k + 1) * P], identf)
            mm.then_inc(ta_full, 1)

        def down(l, e, b, i):
            pe.wait_ge(at_split, plus(l * NE + e + 1, 2, i))
            for ch in range(2):
                u = b + ch
                await_unit(pe, u, i)
                if ch == 0 and (l or e or i is not None):
                    pe.wait_ge(y_ready, plus(l * NE + e, 2, i))
                for k in range(4):
                    mm = product3(ps[:, 5 + ch, :], at_hi[:, k, :], at_lo[:, k, :],
                                  whi[u % SPL][:, k, :], wlo[u % SPL][:, k, :], k == 0, k == 3)
                mm.then_inc(w_used, 1)

        def experts(l):
            def turn(e, i):
                b = e_base(l, e)
                par = e % 2
                pe.wait_ge(hgt_split, plus(l * NE + e + 1, 2, i))
                if e:
                    pe.wait_ge(silu_done, plus(l * NE + e, 2, i))
                experts_half(2, par, 0, b, i)
                if e:
                    turn_act(l, e - 1, i)
                experts_half(2, par, 1, b + 1, i)
                if e:
                    down(l, e - 1, b + 2, i)
                if e < NE - 1:
                    turn_rows(l, e + 1, 1 - par, i)
                b = b + (4 if e else 2)
                experts_half(3, par, 0, b, i)
                experts_half(3, par, 1, b + 1, i)

            turn_rows(l, 0, 0, None)
            turn(0, None)
            with pe.Fori(0, 7) as i:
                turn(1, i)
                turn(2, i)
            turn(NE - 1, None)
            turn_act(l, NE - 1, None)
            down(l, NE - 1, e_base(l, NE), None)

            def one_round(e, n):
                nt = len(out_tiles(l))
                pe.wait_ge(v_oh[l], n + 1)
                for t in range(nt):
                    mm = nc.tensor.matmul(ps[:, 7, 0:8], oh[:, 0, t, :], pay[:, t, bass.ds(e, 1), :].rearrange("p a n -> p (a n)"),
                                          start=t == 0, stop=t == nt - 1)
                mm.then_inc(v_info[l], 1)
                pe.wait_ge(v_gathered[l], n * 16 + 16)
                for k in range(KT):
                    mm = nc.tensor.transpose(ps[:, k // 4, k % 4 * P:(k % 4 + 1) * P], hg[:, 0, k * P:(k + 1) * P], identf)
                mm.then_inc(v_rows_full[l], 1)
                pe.wait_ge(v_rows_lo[l], n + 1)
                for j in range(4):
                    pe.wait_ge(v_lo[l], n * EXP_UNITS + (j + 1))
                    for kk in range(4):
                        k = 4 * (j % 2) + kk
                        mm = product3(ps[:, 2 + j // 2, :], hgt_hi[:, 0, k, :], hgt_lo[:, 0, k, :],
                                      whi[j % SPL][:, kk, :], wlo[j % SPL][:, kk, :], k == 0, k == KT - 1)
                    mm.then_inc(v_used[l], 1)
                pe.wait_ge(v_act[l], n + 1)
                for k in range(4):
                    mm = nc.tensor.transpose(ps[:, 4, k * P:(k + 1) * P], a_act[:, k * P:(k + 1) * P], identf)
                mm.then_inc(v_act_full[l], 1)
                pe.wait_ge(v_act_lo[l], n + 1)
                for j in range(4, EXP_UNITS):
                    pe.wait_ge(v_lo[l], n * EXP_UNITS + (j + 1))
                    for k in range(4):
                        mm = product3(ps[:, 1 + j, :], at_hi[:, k, :], at_lo[:, k, :],
                                      whi[j % SPL][:, k, :], wlo[j % SPL][:, k, :], k == 0, k == 3)
                    mm.then_inc(v_used[l], 1)
            overflow(pe, l, one_round)

        for l in L:
            norm(l, 1)
            in_proj(l)
            channel_mix(l)
            for s in [1, 0]:
                for t in (2 * s, 2 * s + 1):
                    if l == 0 or s == 0 or True:
                        prep(l, t)
                if s in jobs(l):
                    fourier(l, s)
                    attend(l, s)
            out_proj(l)
            norm(l, 2)
            route(l)
            experts(l)

    @block.scalar
    def _(act):
        link = make_chain(act, act_chain)

        def ada(l, g0, i, col):
            for j in range(ADA_BODY):
                g = g0 + j
                for kh in range(2):
                    split_hi(act, 2 * g + kh, i)
                if g >= 1:
                    copy_rows(g - 1, i)

        def copy_rows(g, i):
            act.wait_ge(w_used, plus(2 * g + 2, 12, i))
            if g >= 2:
                act.wait_ge(ada_comb, plus(g - 1, ADA_BODY, i))
            nc.scalar.activation(rowp[0:4, g % 2, :], ps[0:4, g % 2, :], ACT.Copy).then_inc(ada_copied, 1)

        act.wait_ge(const_in, 16 * N_CONST)
        link(nc.scalar.activation(c_act[:], c_raw[:], ACT.Silu))
        act.wait_ge(setup_dve, 1)
        nc.scalar.activation(c_st[:, :, 0:2], c_act[:], ACT.Copy).then_inc(setup_act, 1)
        nc.scalar.activation(rw_hi[:], rwf[:], ACT.Copy).then_inc(setup_act, 1)
        ada_pass(act, ada)
        copy_rows(2 * ADA_CHUNKS - 1, None)

        def norm(l, w):
            tiles = norm_tiles(l, w)
            if (l, w) == (0, 1):
                act.wait_ge(x_in, 32)
                act.wait_ge(ada_row, 2 * ADA_CHUNKS)
                act.wait_ge(ada_comb, 2 * ADA_CHUNKS)
            for n, t in enumerate(tiles):
                if w == 2:
                    act.wait_ge(x_upd.sem, x_upd.after((l, 1, t)))
                elif l:
                    act.wait_ge(x_fin.sem, x_fin.after((l - 1, t)))
                if n:
                    act.wait_ge(sumsq.sem, sumsq.after((l, w, tiles[n - 1])))
                nc.scalar.activation(junk[:], xs[:, t, :], ACT.Square, accum_out=ss[:, t:t + 1]).then_inc(sumsq.sem, 1)
            if w == 2:
                act.wait_ge(w_used, u_out(l) + OUT_UNITS)
            for t in tiles:
                act.wait_ge(ht_full.sem, ht_full.after((l, w, t)))
                b = 2 * (tiles.index(t) % 2)
                nc.scalar.activation(t_hi[:, :, t * P:(t + 1) * P],
                                     ps[:, b:b + 2, :].rearrange("p b (k t) -> p (b k) t", t=P), ACT.Copy).then_inc(ht_hi.sem, 1)

        def in_proj(l):
            if l:
                act.wait_ge(x_stored, 32)
            for ch in range(3):
                for kh in range(2):
                    split_hi(act, u_in(l) + 2 * ch + kh, width=IN_WIDTH[ch])
                    if kh == 0 and ch:
                        evacuate(l, ch - 1)
            split_hi(act, u_out(l))
            evacuate(l, 2)

        def evacuate(l, ch):
            n = IN_WIDTH[ch]
            for t in in_tiles(l, ch):
                if t >= XT:
                    await_p(act, l, ch, t)
                    nc.scalar.activation(pr[:, t, ch * 512:ch * 512 + n], ps[:, (4 if ch % 2 == 0 else 0) + t, 0:n],
                                         ACT.Copy).then_inc(p_act.sem, 1)

        def take(item):
            act.wait_ge(ring_full.sem, ring_full.after(item))
            return ring_pos[item] % 3

        def prep(l, t):
            q = l == 0 or t < XT
            cols = slice((t % 2) * P, (t % 2 + 1) * P)
            keys = slice(t * P, (t + 1) * P)

            def copy(out_, in_):
                return nc.scalar.activation(out_, in_, ACT.Copy)

            c0 = 0 if q else 2
            b = take((l, t, "c"))
            copy(ct[:, c0:3, :], ps[:, b, c0 * P:384].rearrange("p (k t) -> p k t", t=P)).then_inc(ring_free.sem, 1)
            if q:
                for n in range(2):
                    b = take((l, t, f"q{n}"))
                    copy(qk[:, 3 * n:3 * n + 3, :], ps[:, b, 0:288].rearrange("p (h d) -> p h d", d=QKD)).then_inc(ring_free.sem, 1)
            b = take((l, t, "k"))
            copy(qk[:, NH:2 * NH, HD:QKD], pr[:, t, KR:QS].unsqueeze(1).to_broadcast([P, NH, QKD - HD]))
            copy(qk[:, NH:2 * NH, 0:HD], ps[:, b, 0:384].rearrange("p (h d) -> p h d", d=HD)).then_inc(ring_free.sem, 1)
            b = take((l, t, "v"))
            copy(pr[:, t, VM:VM + 384], ps[:, b, 0:384]).then_inc(ring_free.sem, 1)
            for what, dst, at_ in (("tq", qt_m, cols), ("tk", kt_m, keys)):
                if what == "tq" and not q:
                    continue
                for n in range(2):
                    b = take((l, t, f"{what}{n}"))
                    h1 = min(4 * n + 4, NH)
                    copy(dst[:, 4 * n:h1, at_], ps[0:QKD, b, 0:(h1 - 4 * n) * P].rearrange("p (h t) -> p h t", t=P)).then_inc(ring_free.sem, 1)
            if q:
                b = take((l, t, "sq"))
                copy(qt_s[:, :, cols], ps[:, b, 0:384].rearrange("p (h t) -> p h t", t=P)).then_inc(ring_free.sem, 1)
            b = take((l, t, "sk"))
            copy(kt_s[:, :, keys], ps[:, b, 0:256].rearrange("p (h t) -> p h t", t=P)).then_inc(ring_free.sem, 1)

        def fourier(l, s):
            for ch in range(2):
                b = take((l, s, f"f{ch}"))
                nc.scalar.activation(fab[:, ch, :, :].rearrange("p a t -> p (a t)"), ps[:, b, :], ACT.Copy).then_inc(ring_free.sem, 1)
            b = take((l, s, "fy"))
            src = ps[:, b, :].rearrange("p (c t) -> p c t", c=2)
            nc.scalar.activation(t_hi[:, 0:2, s * 256:(s + 1) * 256], src, ACT.Copy).then_inc(fmix_hi.sem, 1)
            nc.scalar.activation(fab[:, 0, :, :], src, ACT.Copy).then_inc(ring_free.sem, 1)

        def attend(l, s):
            us = [(l, s, h, q) for h in range(2 * NH) for q in range(2)]
            nk = 4 if s == 0 else 2
            act.wait_ge(small_in, 16 * N_SMALL * (l + 1))

            def probs(n):
                _, _, h, q = u = us[n]
                g = unit_pos[u]
                act.wait_ge(nb_ready.sem, nb_ready.after(u))
                if n >= 2:
                    act.wait_ge(pt_full.sem, g - 1)
                    act.wait_ge(r_ready.sem, g - 1)
                else:
                    act.wait_ge(fmix_lo.sem, fmix_lo.after((l, s)))
                par = g % 2
                e = nc.scalar.activation(pb[:, par, 0:nk * P], ps[:, 4 + par, 0:nk * P], ACT.Exp, bias=nb[:, par:par + 1],
                                         scale=HD ** -0.5 if h >= NH else QKD ** -0.5, accum_out=sm[:, par:par + 1])
                if h >= NH:
                    e = nc.scalar.activation(esk[:, par:par + 1], sinks[:, 0, h - NH:h - NH + 1], ACT.Exp, bias=nb[:, par:par + 1])
                e.then_inc(exp_done.sem, 1)

            def mixed(h):
                act.wait_ge(o_full.sem, o_full.after((l, s, h)))
                row = 256 + HD * h
                r = row % P
                nc.scalar.activation(t_hi[r:r + 64, row // P, s * 256:(s + 1) * 256], ps[r:r + 64, 3, 0:256], ACT.Copy).then_inc(mix_hi.sem, 1)

            for n in range(len(us) + 3):
                if n < len(us):
                    probs(n)
                if n >= 4 and n % 2 == 0:
                    mixed((n - 4) // 2)

        def out_proj(l):
            for u in range(u_out(l) + 1, u_out(l) + OUT_UNITS):
                split_hi(act, u)

        def route(l):
            nt = len(out_tiles(l))
            act.wait_ge(lg_full, l + 1)
            nc.scalar.activation(aff[:, 0:nt, :], ps[:, 4, 0:nt * NE].rearrange("p (t e) -> p t e", e=NE), ACT.Sigmoid).then_inc(aff_ready, 1)

        def experts(l):
            def rows_hi(e, par, i):
                act.wait_ge(tg_full, plus(l * NE + e + 1, 2, i))
                if e >= 2:
                    act.wait_ge(w_used, plus(after_turn(l, e - 2), 12, i))
                nc.scalar.activation(hgt_hi[:, par, :, :], ps[:, 0:2, :].rearrange("p b (k t) -> p (b k) t", t=P),
                                     ACT.Copy).then_inc(hgt_hi_done, 1)

            def act_hi(e, i):
                act.wait_ge(ta_full, plus(l * NE + e + 1, 2, i))
                act.wait_ge(w_used, plus(after_turn(l, e) - 2, 12, i))
                nc.scalar.activation(at_hi[:], ps[:, 4, :].rearrange("p (k t) -> p k t", t=P), ACT.Copy).then_inc(at_hi_done, 1)

            def silu(e, i):
                act.wait_ge(w_used, plus(e_base(l, e) + 2, 12, i))
                if l or e:
                    act.wait_ge(a_ready, plus(l * NE + e, 2, i))
                nc.scalar.activation(s_act[:], ps[:, 2, :], ACT.Silu).then_inc(silu_done, 1)

            def gated(e, par, b, i, ei):
                act.wait_ge(w_used, plus(b + 2, 12, i))
                if l or e >= 2 or i is not None:
                    act.wait_ge(scattered[par], plus(16 * (l * 8 + e // 2), 16, i))
                for ch in range(2):
                    y = nc.scalar.activation(yb[:, par, ch * 512:(ch + 1) * 512], ps[:, 5 + ch, :], ACT.Copy,
                                             scale=gate_s[:, bass.ds(ei, 1)])
                y.then_inc(y_ready, 1)

            def turn(e, i):
                b = e_base(l, e)
                par = e % 2
                split_hi(act, b, i)
                split_hi(act, b + 1, i)
                if e:
                    act_hi(e - 1, i)
                    split_hi(act, b + 2, i)
                    split_hi(act, b + 3, i)
                if e < NE - 1:
                    rows_hi(e + 1, 1 - par, i)
                silu(e, i)
                split_hi(act, b + (4 if e else 2), i)
                if e:
                    gated(e - 1, 1 - par, b + 2, i, plus(e - 1, 2, i))
                split_hi(act, b + (5 if e else 3), i)

            act.wait_ge(idx_ready, l + 1)
            rows_hi(0, 0, None)
            turn(0, None)
            with act.Fori(0, 7) as i:
                turn(1, i)
                turn(2, i)
            turn(NE - 1, None)
            b = e_base(l, NE)
            split_hi(act, b)
            split_hi(act, b + 1)
            act_hi(NE - 1, None)
            gated(NE - 1, 1, b, None, NE - 1)

            def one_round(e, n):
                def hi(j):
                    act.wait_ge(v_landed[l][j % SPL], n * 32 + (16 + 16 * (j // SPL)))
                    if j >= SPL:
                        act.wait_ge(v_used[l], n * EXP_UNITS + (j - SPL + 1))
                    nc.scalar.activation(whi[j % SPL][:], raw[j % SPL][:], ACT.Copy).then_inc(v_hi[l], 1)

                for j in range(SPL):
                    hi(j)
                act.wait_ge(v_rows_full[l], n + 1)
                nc.scalar.activation(hgt_hi[:, 0, :, :], ps[:, 0:2, :].rearrange("p b (k t) -> p (b k) t", t=P),
                                     ACT.Copy).then_inc(v_rows_hi[l], 1)
                act.wait_ge(v_used[l], n * EXP_UNITS + 2)
                nc.scalar.activation(s_act[:], ps[:, 2, :], ACT.Silu).then_inc(v_silu[l], 1)
                for j in range(SPL, EXP_UNITS):
                    hi(j)
                act.wait_ge(v_act_full[l], n + 1)
                nc.scalar.activation(at_hi[:], ps[:, 4, :].rearrange("p (k t) -> p k t", t=P), ACT.Copy).then_inc(v_act_hi[l], 1)
                act.wait_ge(v_used[l], n * EXP_UNITS + EXP_UNITS)
                for ch in range(2):
                    y = nc.scalar.activation(yb[:, 0, ch * 512:(ch + 1) * 512], ps[:, 5 + ch, :], ACT.Copy, scale=calc_o[:, 2:3])
                y.then_inc(v_y[l], 1)
            overflow(act, l, one_round)

        for l in L:
            norm(l, 1)
            in_proj(l)
            act.wait_ge(ring_full.sem, ring_full.after((l, "m")))
            nc.scalar.activation(mch[:].rearrange("p a b n -> p (a b n)"), ps[:, ring_pos[(l, "m")] % 3, :], ACT.Copy).then_inc(ring_free.sem, 1)
            for s in [1, 0]:
                for t in (2 * s, 2 * s + 1):
                    prep(l, t)
                if s in jobs(l):
                    fourier(l, s)
                    attend(l, s)
            out_proj(l)
            norm(l, 2)
            route(l)
            experts(l)

    @block.vector
    def _(dve):
        link = make_chain(dve, dve_chain)
        v = nc.vector

        nc.vector.memset(c_st[:].rearrange("p k n -> p (k n)").bitcast(F32), 0.0).then_inc(setup_dve, 1)
        v.memset(ss2[:], 1.0)
        v.memset(wbd[:], 0.0).then_inc(setup_dve, 1)
        dve.wait_ge(setup_act, 2)
        v.tensor_tensor(rw_lo[:], rwf[:], rw_hi[:].bitcast(F32), ALU.subtract).then_inc(setup_dve, 1)
        v.tensor_copy(cstb[:], cb_raw[:]).then_inc(setup_dve, 1)
        v.tensor_tensor(c_st[:, :, 2:4], c_act[:], c_st[:, :, 0:2].bitcast(F32), ALU.subtract).then_inc(setup_dve, 1)

        def ada(l, g0, i, col):
            for j in range(ADA_BODY):
                g = g0 + j
                for kh in range(2):
                    split_lo(dve, 2 * g + kh, i)
                if g >= 2:
                    add_bias(g - 2, i)

        def add_bias(g, i):
            dve.wait_ge(ada_comb, plus(g + 1, ADA_BODY, i))
            dve.wait_ge(ada_bias_in[g % 2], plus(16 * (g // 2 + 1), 48, i))
            if g >= 2:
                dve.wait_ge(ada_stored[g % 2], plus(16 * (g // 2), 48, i))
            v.tensor_tensor(row2[:, g % 2, :], ps[0:2, 2 + g % 2, :], bias2[:, g % 2, :], ALU.add).then_inc(ada_row, 1)

        ada_pass(dve, ada)
        add_bias(2 * ADA_CHUNKS - 2, None)
        add_bias(2 * ADA_CHUNKS - 1, None)

        def norm(l, w):
            tiles = norm_tiles(l, w)
            dve.wait_ge(ab_in, 80 * (ab_ready.after((l, w))))
            for s in range(2):
                r = v.scalar_tensor_tensor(out=ab[:, s, 0, :], in0=ab[:, s, 0, :], scalar=1.0, in1=gb[:, 0, :],
                                           op0=ALU.add, op1=ALU.mult)
            r.then_inc(ab_ready.sem, 1)
            dve.wait_ge(ab_ready.sem, ab_ready.after((l, w)))
            for t in tiles:
                dve.wait_ge(sumsq.sem, sumsq.after((l, w, t)))
                v.tensor_scalar(ms[:, t:t + 1], ss[:, t:t + 1], 1.0 / D, EPS, ALU.mult, ALU.add).then_inc(mean_ready.sem, 1)
            if (l, w) == (0, 1):
                for p_ in range(2):
                    dve.wait_ge(ada_stored[p_], 16 * ADA_CHUNKS)
            elif w == 2:
                dve.wait_ge(op_scaled.sem, op_scaled.after((l, 1, tiles[-1])))

            def scaled(n):
                t = tiles[n]
                dve.wait_ge(rstd_ready.sem, rstd_ready.after((l, w, t)))
                if n >= 2:
                    dve.wait_ge(ht_full.sem, ht_full.after((l, w, tiles[n - 2])))
                    if w == 2:
                        dve.wait_ge(h2_stored[n % 2], 16 * ((h2_items.index((l, w, t))) // 2))
                s = stream(t)
                link(v.scalar_tensor_tensor(out=xn[:, n % 2, :], in0=xs[:, t, :], scalar=rstd[:, t:t + 1],
                                            in1=ab[:, s, 0, :], op0=ALU.mult, op1=ALU.mult))
                v.tensor_tensor(xn[:, n % 2, :], xn[:, n % 2, :], ab[:, s, 1, :], ALU.add).then_inc(h_ready.sem, 1)

            def rest(n):
                t = tiles[n]
                b = 2 * (n % 2)
                dve.wait_ge(ht_hi.sem, ht_hi.after((l, w, t)))
                sl = slice(t * P, (t + 1) * P)
                v.tensor_tensor(t_lo[:, :, sl], ps[:, b:b + 2, :].rearrange("p b (k t) -> p (b k) t", t=P),
                                t_hi[:, :, sl].bitcast(F32), ALU.subtract).then_inc(ht_split.sem, 1)

            for n in range(len(tiles) + 1):
                if n < len(tiles):
                    scaled(n)
                if n:
                    rest(n - 1)

        def in_proj(l):
            if l:
                dve.wait_ge(x_stored, 32)
            for ch in range(3):
                for kh in range(2):
                    split_lo(dve, u_in(l) + 2 * ch + kh, width=IN_WIDTH[ch])
                    if kh == 0 and ch:
                        evacuate(l, ch - 1)
            split_lo(dve, u_out(l))
            evacuate(l, 2)
            dve.wait_ge(p_act.sem, p_act.after((l, 2, 3)))

        def evacuate(l, ch):
            n = IN_WIDTH[ch]
            for t in in_tiles(l, ch):
                if t < XT:
                    await_p(dve, l, ch, t)
                    v.tensor_copy(pr[:, t, ch * 512:ch * 512 + n], ps[:, (4 if ch % 2 == 0 else 0) + t, 0:n]).then_inc(p_dve.sem, 1)

        def heads_view(ap, n):
            return ap.rearrange("p (h d) -> p h d", h=n)

        def rotate(x_, nh, w, cos, sin):
            q4 = w // 4
            t1 = sq[:, 0:nh * w].rearrange("p (h d) -> p h d", h=nh)
            t2 = sq[:, 576:576 + nh * w].rearrange("p (h d) -> p h d", h=nh)
            v.tensor_tensor(t1, x_, cos.unsqueeze(1).to_broadcast([P, nh, w]), ALU.mult)
            for a in range(4):
                o0, i0 = a * q4, (a ^ 1) * q4
                r = v.tensor_tensor(t2[:, :, o0:o0 + q4], x_[:, :, i0:i0 + q4],
                                    sin[:, o0:o0 + q4].unsqueeze(1).to_broadcast([P, nh, q4]), ALU.mult)
            link(r)
            return v.tensor_tensor(x_, t1, t2, ALU.add)

        def prep(l, t):
            q = l == 0 or t < XT
            i_ = prep_items.index((l, t))
            a0 = CQ if q else CKV
            if i_:
                dve.wait_ge(qk_done.sem, i_)
            link(v.tensor_tensor(sq[:, 0:VS - a0], pr[:, t, a0:VS], pr[:, t, a0:VS], ALU.mult))
            if q:
                v.tensor_reduce(ss2[:, 0:1], sq[:, 0:256], AX.X, ALU.add)
            v.tensor_reduce(ss2[:, 1:2], sq[:, CKV - a0:CKV - a0 + 128], AX.X, ALU.add)
            link(v.tensor_reduce(ss2[:, 2:10], heads_view(sq[:, QS - a0:VS - a0], 8), AX.X, ALU.add))
            link(v.tensor_tensor(ss2[:, 0:10], ss2[:, 0:10], cst[:, C_INVN:C_INVN + 10], ALU.mult))
            v.tensor_scalar(ss2[:, 0:10], ss2[:, 0:10], EPS, None, ALU.add).then_inc(c_mean.sem, 1)
            dve.wait_ge(c_rstd.sem, c_rstd.after((l, t)))
            if i_:
                dve.wait_ge(ring_full.sem, ring_full.after((*prep_items[i_ - 1], "c")))
            if q:
                v.scalar_tensor_tensor(out=cn[:, 0:256], in0=pr[:, t, CQ:CKV], scalar=rs2[:, 0:1], in1=gains[:, G_CQ:G_CKV],
                                       op0=ALU.mult, op1=ALU.mult)
            v.scalar_tensor_tensor(out=cn[:, 256:384], in0=pr[:, t, CKV:KR], scalar=rs2[:, 1:2], in1=gains[:, G_CKV:G_MQ],
                                   op0=ALU.mult, op1=ALU.mult).then_inc(cn_ready.sem, 1)
            sw = heads_view(pr[:, t, QS:VS], 8)
            link(v.tensor_tensor(sw, sw, rs2[:, 2:10].unsqueeze(2).to_broadcast([P, 8, HD]), ALU.mult))
            v.tensor_tensor(sw[:, 0:6, :], sw[:, 0:6, :], gains[:, G_SQ:G_SK].unsqueeze(1).to_broadcast([P, 6, HD]), ALU.mult)
            link(v.tensor_tensor(sw[:, 6:8, :], sw[:, 6:8, :], gains[:, G_SK:G_W].unsqueeze(1).to_broadcast([P, 2, HD]), ALU.mult))
            if t < XT:
                link(rotate(sw, 8, HD, rope[:, t, 64:128], rope[:, t, 128:192]))
            if i_:
                dve.wait_ge(ring_full.sem, ring_full.after((*prep_items[i_ - 1], "sk")))
            v.tensor_copy(kdup[:], sw[:, 6:8, :].unsqueeze(2).to_broadcast([P, 2, 2, HD])).then_inc(sw_done.sem, 1)
            h0 = 0 if q else NH
            nh = 2 * NH - h0
            dve.wait_ge(ring_free.sem, ring_free.after((l, t, "k")))
            qkv_ = qk[:, h0:, :]
            link(v.tensor_tensor(sq[:, 0:nh * QKD].rearrange("p (h d) -> p h d", h=nh), qkv_, qkv_, ALU.mult))
            link(v.tensor_reduce(ss2[:, h0:2 * NH], sq[:, 0:nh * QKD].rearrange("p (h d) -> p h d", h=nh), AX.X, ALU.add))
            v.tensor_scalar(ss2[:, h0:2 * NH], ss2[:, h0:2 * NH], 1.0 / QKD, EPS, ALU.mult, ALU.add).then_inc(qk_mean.sem, 1)
            dve.wait_ge(qk_rstd.sem, qk_rstd.after((l, t)))
            link(v.tensor_tensor(qkv_, qkv_, rs2[:, h0:2 * NH].unsqueeze(2).to_broadcast([P, nh, QKD]), ALU.mult))
            if q:
                v.tensor_tensor(qk[:, 0:NH, :], qk[:, 0:NH, :], gains[:, G_MQ:G_MK].unsqueeze(1).to_broadcast([P, NH, QKD]), ALU.mult)
            r = v.tensor_tensor(qk[:, NH:, :], qk[:, NH:, :], gains[:, G_MK:G_SQ].unsqueeze(1).to_broadcast([P, NH, QKD]), ALU.mult)
            if t < XT:
                link(r)
                r = rotate(qk[:, :, HD:QKD], 12, 32, rope[:, t, 0:32], rope[:, t, 32:64])
            r.then_inc(qk_done.sem, 1)

        def fourier(l, s):
            dve.wait_ge(fmix_hi.sem, fmix_hi.after((l, s)))
            dve.wait_ge(ring_free.sem, ring_free.after((l, s, "fy")))
            sl = slice(s * 256, (s + 1) * 256)
            v.tensor_tensor(t_lo[:, 0:2, sl], fab[:, 0, :, :], t_hi[:, 0:2, sl].bitcast(F32), ALU.subtract).then_inc(fmix_lo.sem, 1)

        def attend(l, s):
            us = [(l, s, h, q) for h in range(2 * NH) for q in range(2)]
            nk = 4 if s == 0 else 2

            def biggest(n):
                _, _, h, q = u = us[n]
                par = unit_pos[u] % 2
                dve.wait_ge(s_full.sem, s_full.after(u))
                if unit_pos[u] >= 2:
                    dve.wait_ge(exp_done.sem, unit_pos[u] - 1)
                link(v.tensor_reduce(mx[:, par:par + 1], ps[:, 4 + par, 0:nk * P], AX.X, ALU.max))
                if h < NH:
                    r = v.tensor_scalar(nb[:, par:par + 1], mx[:, par:par + 1], -QKD ** -0.5, None, ALU.mult)
                else:
                    r = v.tensor_scalar(nb[:, par:par + 1], mx[:, par:par + 1], -HD ** -0.5, sinks[:, 1, h - NH:h - NH + 1], ALU.mult, ALU.min)
                r.then_inc(nb_ready.sem, 1)

            def invert(n):
                _, _, h, q = u = us[n]
                par = unit_pos[u] % 2
                dve.wait_ge(exp_done.sem, exp_done.after(u))
                if unit_pos[u] >= 2:
                    dve.wait_ge(p_norm.sem, unit_pos[u] - 1)
                if h >= NH:
                    link(v.tensor_tensor(sm[:, par:par + 1], sm[:, par:par + 1], esk[:, par:par + 1], ALU.add))
                v.reciprocal(ri[:, par:par + 1], sm[:, par:par + 1]).then_inc(r_ready.sem, 1)

            def copy_probs(n):
                _, _, h, q = u = us[n]
                dve.wait_ge(pt_full.sem, pt_full.after(u))
                hn = heads.index((l, s, h))
                if hn >= 2:
                    dve.wait_ge(o_full.sem, hn - 1)
                v.tensor_copy(ptb[:, h % 2, 0:nk, q * P:(q + 1) * P],
                              ps[:, 6 + unit_pos[u] % 2, 0:nk * P].rearrange("p (k t) -> p k t", t=P)).then_inc(pt_copied.sem, 1)

            def mixed(h):
                dve.wait_ge(mix_hi.sem, mix_hi.after((l, s, h)))
                row = 256 + HD * h
                r = row % P
                sl = slice(s * 256, (s + 1) * 256)
                v.tensor_tensor(t_lo[r:r + 64, row // P, sl], ps[r:r + 64, 3, 0:256],
                                t_hi[r:r + 64, row // P, sl].bitcast(F32), ALU.subtract).then_inc(mix_lo.sem, 1)

            for n in range(len(us) + 3):
                if n < len(us):
                    biggest(n)
                if 1 <= n < len(us) + 1:
                    invert(n - 1)
                if 2 <= n < len(us) + 2:
                    copy_probs(n - 2)
                if n >= 4 and n % 2 == 0:
                    mixed((n - 4) // 2)

        def out_proj(l):
            def scale(ch):
                for t in out_tiles(l):
                    n = out_items.index((l, ch, t))
                    await_op(dve, l, ch, t)
                    if n >= 2:
                        dve.wait_ge(x_upd.sem, n - 1)
                    v.tensor_tensor(otmp[:, n % 2, :], ps[:, (4 if ch == 0 else 0) + t, :],
                                    gb[:, stream(t), ch * 512:(ch + 1) * 512], ALU.mult).then_inc(op_scaled.sem, 1)
            for n in range(1, OUT_UNITS):
                split_lo(dve, u_out(l) + n)
                if n == 2:
                    dve.wait_ge(gb_in, 32 * (2 * l + 1))
                    scale(0)
            scale(1)

        def route(l):
            nt = len(out_tiles(l))
            ng = nt * 4
            dve.wait_ge(aff_ready, l + 1)
            if l:
                dve.wait_ge(y_ready, NE * l)
            af, se, cn_, mk = (a[:, 0:nt, :] for a in (aff, sel, cnt, msk))

            def flat(a):
                return a.rearrange("p t e -> p (t e)")

            def ranks(vals, n, out_):
                vi = vals.rearrange("p (g i) -> p g i", i=4)
                a_i = vi.unsqueeze(2).to_broadcast([P, n, 4, 4])
                a_j = vi.unsqueeze(3).to_broadcast([P, n, 4, 4])
                lt = cst[:, C_LT:C_LT + 16]
                v.tensor_tensor(pair[:, 0:n], a_i, a_j, ALU.is_gt)
                link(v.tensor_tensor(pair2[:, 0:n], a_i, a_j, ALU.is_ge))
                p2 = pair2[:, 0:n].rearrange("p g j i -> p g (j i)")
                p1 = pair[:, 0:n].rearrange("p g j i -> p g (j i)")
                link(v.tensor_tensor(p2, p2, lt.unsqueeze(1).to_broadcast([P, n, 16]), ALU.mult))
                link(v.tensor_tensor(p1, p1, p2, ALU.max))
                link(v.tensor_reduce(out_, pair[:, 0:n], AX.X, ALU.add))

            link(v.tensor_tensor(se, af, rb[:].unsqueeze(1).to_broadcast([P, nt, NE]), ALU.add))
            vi = flat(se).rearrange("p (g i) -> p g i", i=4)
            link(v.tensor_tensor(pair[:, 0:ng], vi.unsqueeze(2).to_broadcast([P, ng, 4, 4]),
                                 vi.unsqueeze(3).to_broadcast([P, ng, 4, 4]), ALU.add))
            p1 = pair[:, 0:ng].rearrange("p g j i -> p g (j i)")
            link(v.tensor_tensor(p1, p1, cst[:, C_DIAG:C_DIAG + 16].unsqueeze(1).to_broadcast([P, ng, 16]), ALU.add))
            gs = flat(gsc[:, 0:nt, :])
            link(v.tensor_reduce(gs, p1, AX.X, ALU.max))
            ranks(gs, nt, gcnt[:, 0:nt, :])
            link(v.tensor_scalar(best[:, 0:nt, :], gcnt[:, 0:nt, :], 0.0, None, ALU.is_equal))
            ranks(flat(se), ng, flat(cn_).rearrange("p (g i) -> p g i", i=4))
            link(v.tensor_scalar(flat(mk), flat(cn_), 2.0, None, ALU.is_lt))
            m4 = flat(mk).rearrange("p (g i) -> p g i", i=4)
            link(v.tensor_tensor(m4, m4, flat(best[:, 0:nt, :]).unsqueeze(2).to_broadcast([P, ng, 4]), ALU.mult))
            v.tensor_copy(mskb[:, 0:nt, :], mk).then_inc(msk_ready, 1)
            ga, gr = gate[:, 0:nt, :], gres[:, 0:nt, :]
            link(v.tensor_tensor(ga, af, mk, ALU.mult))
            link(v.tensor_reduce(den[:, 0:nt], ga, AX.X, ALU.add))
            link(v.reciprocal(den[:, 4:4 + nt], den[:, 0:nt]))
            link(v.tensor_tensor(ga, ga, den[:, 4:4 + nt].unsqueeze(2).to_broadcast([P, nt, NE]), ALU.mult))
            py = pay[:, 0:nt]
            v.tensor_copy(py[:, :, :, 4], ga)
            v.tensor_copy(py[:, :, :, 2], cn_)
            link(v.memset(py[:, :, :, 3], 1.0))
            link(v.tensor_tensor(gr, ga, py[:, :, :, 4], ALU.subtract))
            link(v.tensor_copy(py[:, :, :, 5], gr))
            link(v.tensor_tensor(gr, gr, py[:, :, :, 5], ALU.subtract))
            v.tensor_copy(py[:, :, :, 6], gr)
            v.memset(py[:, :, :, 7], 0.0)
            for t in range(nt):
                v.memset(py[:, t, :, 0], float(t))
            v.tensor_copy(py[:, :, :, 1].rearrange("p t e -> p t e"),
                          cst[:, C_TOK:C_TOK + 1].unsqueeze(2).to_broadcast([P, nt, NE]))
            link(v.tensor_copy(iota16[:], cst[:, C_IOTA:C_IOTA + P]))
            dve.wait_ge(pos_full, l + 1)
            link(v.tensor_reduce(den[:, 0:1], ps[:, 5, nt * NE:(nt + 1) * NE], AX.X, ALU.max))
            v.tensor_copy(most[:], den[:, 0:1])
            po = posf[:, 0:nt, :]
            link(v.scalar_tensor_tensor(out=flat(po), in0=ps[:, 5, 0:nt * NE], scalar=1.0, in1=flat(mk), op0=ALU.add, op1=ALU.mult))
            link(v.tensor_scalar(flat(posm[:, 0:nt, :]), flat(po), -1.0, None, ALU.add))
            for e in range(NE):
                if e >= 2:
                    dve.wait_ge(oh_used, l * NE + e - 1)
                v.tensor_tensor(oh[:, e % 2, 0:nt, :], iota16[:].unsqueeze(1).to_broadcast([P, nt, P]),
                                posm[:, 0:nt, e].unsqueeze(2).to_broadcast([P, nt, P]), ALU.is_equal).then_inc(oh_ready, 1)
            dve.wait_ge(oh_used, (l + 1) * NE)
            link(v.tensor_copy(info[:].rearrange("p e n -> p (e n)"), ps[:, 6, 0:NE * 8]))
            v.tensor_scalar(oobf[:], info[:, :, 3], -float(BIG), float(BIG), ALU.mult, ALU.add)
            v.tensor_tensor(gate_s[:], info[:, :, 6], info[:, :, 5], ALU.add)
            link(v.scalar_tensor_tensor(out=tokf[:], in0=info[:, :, 0], scalar=float(P), in1=info[:, :, 1], op0=ALU.mult, op1=ALU.add))
            v.tensor_tensor(gate_s[:], gate_s[:], info[:, :, 4], ALU.add)
            v.tensor_tensor(idxg[:], tokf[:], oobf[:], ALU.add)
            link(v.scalar_tensor_tensor(out=tokf[:], in0=tokf[:], scalar=2.0, in1=info[:, :, 2], op0=ALU.mult, op1=ALU.add))
            v.tensor_tensor(idxs[:], tokf[:], oobf[:], ALU.add).then_inc(idx_ready, 1)

        def experts(l):
            def rows_lo(e, par, i):
                dve.wait_ge(hgt_hi_done, plus(l * NE + e + 1, 2, i))
                v.tensor_tensor(hgt_lo[:, par, :, :], ps[:, 0:2, :].rearrange("p b (k t) -> p (b k) t", t=P),
                                hgt_hi[:, par, :, :].bitcast(F32), ALU.subtract).then_inc(hgt_split, 1)

            def act_lo(e, i):
                dve.wait_ge(at_hi_done, plus(l * NE + e + 1, 2, i))
                v.tensor_tensor(at_lo[:], ps[:, 4, :].rearrange("p (k t) -> p k t", t=P), at_hi[:].bitcast(F32),
                                ALU.subtract).then_inc(at_split, 1)

            def swiglu(e, b, i):
                dve.wait_ge(w_used, plus(b, 12, i))
                dve.wait_ge(silu_done, plus(l * NE + e + 1, 2, i))
                if l or e or i is not None:
                    dve.wait_ge(ta_full, plus(l * NE + e, 2, i))
                v.tensor_tensor(a_act[:], s_act[:], ps[:, 3, :], ALU.mult).then_inc(a_ready, 1)

            def turn(e, i):
                b = e_base(l, e)
                par = e % 2
                split_lo(dve, b, i)
                if e:
                    swiglu(e - 1, b, i)
                split_lo(dve, b + 1, i)
                if e:
                    act_lo(e - 1, i)
                    split_lo(dve, b + 2, i)
                    split_lo(dve, b + 3, i)
                if e < NE - 1:
                    rows_lo(e + 1, 1 - par, i)
                b = b + (4 if e else 2)
                split_lo(dve, b, i)
                split_lo(dve, b + 1, i)

            rows_lo(0, 0, None)
            turn(0, None)
            with dve.Fori(0, 7) as i:
                turn(1, i)
                turn(2, i)
            turn(NE - 1, None)
            b = e_base(l, NE)
            split_lo(dve, b)
            swiglu(NE - 1, b, None)
            split_lo(dve, b + 1)
            act_lo(NE - 1, None)

            nt = len(out_tiles(l))
            STEPS = 4

            def further(c):
                dve.wait_ge(v_turn[l], c * NE + 1)
                v.tensor_scalar(posm[:, 0:nt, :].rearrange("p t e -> p (t e)"), posm[:, 0:nt, :].rearrange("p t e -> p (t e)"),
                                -float(SLOTS), None, ALU.add).then_inc(v_shift[l], 1)

            def one_round(e, n):
                def step(ins, k):
                    ins.then_inc(v_step[l], 1)
                    dve.wait_ge(v_step[l], n * STEPS + k)

                def lo(j):
                    dve.wait_ge(v_hi[l], n * EXP_UNITS + (j + 1))
                    v.tensor_tensor(wlo[j % SPL][:], raw[j % SPL][:], whi[j % SPL][:].bitcast(F32), ALU.subtract).then_inc(v_lo[l], 1)

                v.tensor_tensor(oh[:, 0, 0:nt, :], iota16[:].unsqueeze(1).to_broadcast([P, nt, P]),
                                posm[:, 0:nt, bass.ds(e, 1)].to_broadcast([P, nt, P]), ALU.is_equal).then_inc(v_oh[l], 1)
                dve.wait_ge(v_info[l], n + 1)
                step(v.tensor_copy(info_o[:], ps[:, 7, 0:8]), 1)
                v.tensor_scalar(calc_o[:, 0:1], info_o[:, 3:4], -float(BIG), float(BIG), ALU.mult, ALU.add)
                v.tensor_tensor(calc_o[:, 3:4], info_o[:, 6:7], info_o[:, 5:6], ALU.add)
                step(v.scalar_tensor_tensor(out=calc_o[:, 1:2], in0=info_o[:, 0:1], scalar=float(P), in1=info_o[:, 1:2],
                                            op0=ALU.mult, op1=ALU.add), 2)
                v.tensor_tensor(calc_o[:, 2:3], calc_o[:, 3:4], info_o[:, 4:5], ALU.add)
                step(v.tensor_tensor(idx_o[:, 0:1], calc_o[:, 1:2], calc_o[:, 0:1], ALU.add), 3)
                step(v.scalar_tensor_tensor(out=calc_o[:, 1:2], in0=calc_o[:, 1:2], scalar=2.0, in1=info_o[:, 2:3],
                                            op0=ALU.mult, op1=ALU.add), 4)
                v.tensor_tensor(idx_o[:, 1:2], calc_o[:, 1:2], calc_o[:, 0:1], ALU.add).then_inc(v_idx[l], 1)
                for j in range(SPL):
                    lo(j)
                dve.wait_ge(v_rows_hi[l], n + 1)
                v.tensor_tensor(hgt_lo[:, 0, :, :], ps[:, 0:2, :].rearrange("p b (k t) -> p (b k) t", t=P),
                                hgt_hi[:, 0, :, :].bitcast(F32), ALU.subtract).then_inc(v_rows_lo[l], 1)
                for j in range(SPL, EXP_UNITS):
                    lo(j)
                dve.wait_ge(v_silu[l], n + 1)
                dve.wait_ge(v_used[l], n * EXP_UNITS + 4)
                v.tensor_tensor(a_act[:], s_act[:], ps[:, 3, :], ALU.mult).then_inc(v_act[l], 1)
                dve.wait_ge(v_act_hi[l], n + 1)
                v.tensor_tensor(at_lo[:], ps[:, 4, :].rearrange("p (k t) -> p k t", t=P), at_hi[:].bitcast(F32),
                                ALU.subtract).then_inc(v_act_lo[l], 1)
            overflow(dve, l, one_round, further)

        def finish(l):
            dve.wait_ge(gb_in, 32 * (2 * l + 2))
            for n, t in enumerate(out_tiles(l)):
                f = fin_items.index((l, t))
                dve.wait_ge(y_in[f % 2], 16 * (f // 2 + 1))
                link(v.tensor_tensor(yy[:, f % 2, 0, :], yy[:, f % 2, 0, :], yy[:, f % 2, 1, :], ALU.add))
                v.tensor_tensor(yy[:, f % 2, 0, :], yy[:, f % 2, 0, :], gb[:, stream(t), :], ALU.mult).then_inc(y_sum.sem, 1)

        for l in L:
            norm(l, 1)
            in_proj(l)
            dve.wait_ge(small_in, 16 * N_SMALL * (l + 1))
            link(v.tensor_scalar(sinks[:, 1, :], sinks[:, 0, :], -1.0, None, ALU.mult))
            for s in [1, 0]:
                for t in (2 * s, 2 * s + 1):
                    prep(l, t)
                if s in jobs(l):
                    fourier(l, s)
                    attend(l, s)
            out_proj(l)
            norm(l, 2)
            route(l)
            experts(l)
            finish(l)

    @block.gpsimd
    def _(pool):
        link = make_chain(pool, pool_chain)
        g_ = nc.gpsimd
        def bound(last, e, i):
            return last if i is None else plus(e, 2, i) | last


        pool.dma_start(xs[:, 0:XT, :], x[0].rearrange("(t p) d -> p t d", p=P)).then_inc(x_in, 16)
        pool.dma_start(xs[:, XT:, :], ctx[0].rearrange("(t p) d -> p t d", p=P)).then_inc(x_in, 16)

        def load_small(l):
            def get(dst, src):
                pool.dma_start(dst, src).then_inc(small_in, 16)
            get(w_uq[:], mla_w_uq[l].rearrange("(k p) n -> p k n", p=P))
            get(w_ukv[:, 0, :], mla_w_uk[l])
            get(w_ukv[:, 1, :], mla_w_uv[l])
            for g0, g1, src in ((G_CQ, G_CKV, mla_cq_g), (G_CKV, G_MQ, mla_ckv_g), (G_MQ, G_MK, mla_q_g),
                                (G_MK, G_SQ, mla_k_g), (G_SQ, G_SK, swa_q_g), (G_SK, G_W, swa_k_g)):
                get(gains[:, g0:g1], row_bc(src, l, g1 - g0))
            get(sinks[:, 0, :], row_bc(swa_sink, l, NH))
            for n in range(4):
                r = 64 * (n % 2)
                get(wbd[r:r + 64, n // 2, r:r + 64], fnet_w[l, n])

        pool.wait_ge(setup_dve, 2)
        load_small(0)

        bias_src = ada_b.rearrange("l n -> (l n)")

        def load_bias(par, n, i):
            off = plus((par + 2 * n) * CHUNK, 2 * CHUNK, i)
            pool.dma_start(bias2[:, par, :], bias_src[bass.ds(off, CHUNK)].partition_broadcast(2)).then_inc(ada_bias_in[par], 16)

        def store_rows(par, n, i):
            pool.wait_ge(ada_row, plus(par + 2 * n + 1, 2, i))
            pool.dma_start(ada_d[:, bass.ds(plus((par + 2 * n) * CHUNK, 2 * CHUNK, i), CHUNK)], row2[:, par, :]).then_inc(ada_stored[par], 16)

        for par in range(2):
            load_bias(par, 0, None)
        with pool.Fori(0, ADA_CHUNKS - 1) as i:
            for par in range(2):
                store_rows(par, 0, i)
                load_bias(par, 1, i)
        for par in range(2):
            store_rows(par, ADA_CHUNKS - 1, None)

        def load_ab(l, w):
            k = 3 * (w - 1)
            for s in range(2):
                pool.dma_start(ab[:, s, 0, :], ab_src(s, l, k + 1)).then_inc(ab_in, 16)
                pool.dma_start(ab[:, s, 1, :], ab_src(s, l, k)).then_inc(ab_in, 16)

        def load_gain(l, w):
            pool.dma_start(gb[:, 0, :], row_bc(norm1_g if w == 1 else norm2_g, l, D)).then_inc(ab_in, 16)

        def load_gates(l, w):
            for s in range(2):
                pool.dma_start(gb[:, s, :], ab_src(s, l, 3 * w - 1)).then_inc(gb_in, 16)

        def norm(l, w):
            for n, t in enumerate(norm_tiles(l, w)):
                pool.wait_ge(mean_ready.sem, mean_ready.after((l, w, t)))
                g_.tensor_tensor(rstd[:, t:t + 1], ms[:, t:t + 1], half[:, 0:1], ALU.pow).then_inc(rstd_ready.sem, 1)
            if w == 2:
                for n, t in enumerate(norm_tiles(l, w)):
                    pool.wait_ge(h_ready.sem, h_ready.after((l, w, t)))
                    pool.dma_start(h2_d[t * P:(t + 1) * P, :], xn[:, n % 2, :]).then_inc(h2_stored[n % 2], 16)

        def prep(l, t):
            q = l == 0 or t < XT
            pool.wait_ge(c_mean.sem, c_mean.after((l, t)))
            g_.tensor_tensor(rs2[:, 0:10], ss2[:, 0:10], half[:, 0:10], ALU.pow).then_inc(c_rstd.sem, 1)
            h0 = 0 if q else NH
            pool.wait_ge(qk_mean.sem, qk_mean.after((l, t)))
            g_.tensor_tensor(rs2[:, h0:12], ss2[:, h0:12], half[:, h0:12], ALU.pow).then_inc(qk_rstd.sem, 1)

        def attend(l, s):
            nk = 4 if s == 0 else 2
            for h in range(2 * NH):
                for q in range(2):
                    u = (l, s, h, q)
                    par = unit_pos[u] % 2
                    pool.wait_ge(r_ready.sem, r_ready.after(u))
                    g_.tensor_scalar(pb[:, par, 0:nk * P], pb[:, par, 0:nk * P], ri[:, par:par + 1], None, ALU.mult).then_inc(p_norm.sem, 1)

        def gather(l, e, i, first=False):
            par = e % 2
            if not first:
                pool.wait_ge(tg_full, plus(l * NE + e - 1, 2, i))
            if l or not first:
                pool.wait_ge(gathered[par], plus(16 * (l * 8 + e // 2), 16, i))
            g_.tensor_copy(cur_g[:, par:par + 1], idxg[:, bass.ds(plus(e, 2, i), 1)]).then_inc(cur_g_ready, 1)
            pool.wait_ge(cur_g_ready, plus(l * NE + e + 1, 2, i))
            g_.indirect_dma_start(out=hg[:, par, :], out_offset=None, in_=h2_d,
                                  in_offset=bass.IndirectOffsetOnAxis(ap=cur_g[:, par:par + 1], axis=0),
                                  bounds_check=bound(NTILES * P - 1, e, i), oob_is_err=False).then_inc(gathered[par], 16)

        def scatter(l, e, i):
            par = e % 2
            pool.wait_ge(y_ready, plus(l * NE + e + 1, 2, i))
            if l or e >= 2 or i is not None:
                pool.wait_ge(scattered[par], plus(16 * (l * 8 + e // 2), 16, i))
            g_.tensor_copy(cur_s[:, par:par + 1], idxs[:, bass.ds(plus(e, 2, i), 1)]).then_inc(cur_s_ready, 1)
            pool.wait_ge(cur_s_ready, plus(l * NE + e + 1, 2, i))
            g_.indirect_dma_start(out=y_d, out_offset=bass.IndirectOffsetOnAxis(ap=cur_s[:, par:par + 1], axis=0),
                                  in_=yb[:, par, :], in_offset=None,
                                  bounds_check=bound(2 * NTILES * P - 1, e, i), oob_is_err=False).then_inc(scattered[par], 16)

        for l in L:
            for par in range(2):
                pool.wait_ge(ada_stored[par], 16 * ADA_CHUNKS)
            if l:
                pool.wait_ge(y_sum.sem, y_sum.after((l - 1, 1)))
            load_ab(l, 1)
            load_gain(l, 1)
            norm(l, 1)
            for s in [1, 0]:
                for t in (2 * s, 2 * s + 1):
                    prep(l, t)
                if s in jobs(l):
                    attend(l, s)
            pool.wait_ge(mix_lo.sem, mix_lo.after((l, 0, 2 * NH - 1)))
            if l == 0:
                load_small(1)
                pool.dma_start(xs[:, XT:, :], ctx[0].rearrange("(t p) d -> p t d", p=P)).then_inc(x_in, 16)
                pool.dma_start(xs[:, 0:XT, :], x[0].rearrange("(t p) d -> p t d", p=P)).then_inc(x_in, 16)
            else:
                pool.dma_start(xs[:, 0:XT, :], x_d.rearrange("(t p) d -> p t d", p=P)).then_inc(x_in, 16)
            load_gates(l, 1)
            load_ab(l, 2)
            pool.wait_ge(x_in, (64, 80)[l])
            for ch in range(2):
                for t in out_tiles(l):
                    n = out_items.index((l, ch, t))
                    pool.wait_ge(op_scaled.sem, n + 1)
                    sl = slice(ch * 512, (ch + 1) * 512)
                    g_.tensor_tensor(xs[:, t, sl], xs[:, t, sl], otmp[:, n % 2, :], ALU.add).then_inc(x_upd.sem, 1)
            load_gain(l, 2)
            norm(l, 2)
            pool.wait_ge(ab_ready.sem, ab_ready.after((l, 2)))
            load_gates(l, 2)
            stored = [h2_items.index(it) for it in h2_items if it[0] == l]
            for par in range(2):
                pool.wait_ge(h2_stored[par], 16 * (max(stored) // 2 + 1))
            pool.wait_ge(ht_full.sem, ht_full.after((l, 2, out_tiles(l)[-1])))
            pool.wait_ge(idx_ready, l + 1)
            gather(l, 0, None, True)
            gather(l, 1, None, True)
            with pool.Fori(0, 7) as i:
                for e in range(2):
                    gather(l, e + 2, i)
                    scatter(l, e, i)
            scatter(l, NE - 2, None)
            scatter(l, NE - 1, None)
            for par in range(2):
                pool.wait_ge(scattered[par], 16 * 8 * (l + 1))
            pool.wait_ge(w_used, u_exp(l) + NE * EXP_UNITS)
            g_.tensor_tensor(tick[:], half[:, 0:1], half[:, 0:1], ALU.mult).then_inc(v_turn[l], 1)

            def one_round(e, n):
                pool.wait_ge(v_idx[l], n + 1)
                g_.indirect_dma_start(out=hg[:, 0, :], out_offset=None, in_=h2_d,
                                      in_offset=bass.IndirectOffsetOnAxis(ap=idx_o[:, 0:1], axis=0),
                                      bounds_check=e | NTILES * P - 1, oob_is_err=False).then_inc(v_gathered[l], 16)
                pool.wait_ge(v_y[l], n + 1)
                g_.indirect_dma_start(out=y_d, out_offset=bass.IndirectOffsetOnAxis(ap=idx_o[:, 1:2], axis=0),
                                      in_=yb[:, 0, :], in_offset=None,
                                      bounds_check=e | 2 * NTILES * P - 1, oob_is_err=False).then_inc(v_scattered[l], 16)
                pool.wait_ge(v_scattered[l], n * 16 + 16)
                g_.tensor_tensor(tick[:], half[:, 0:1], half[:, 0:1], ALU.mult).then_inc(v_turn[l], 1)
            overflow(pool, l, one_round)

            def load_y(t):
                f = fin_items.index((l, t))
                pool.dma_start(yy[:, f % 2, :, :].rearrange("p a d -> p (a d)"),
                               y_d[t * 2 * P:(t + 1) * 2 * P, :].rearrange("(p k) d -> p (k d)", k=2)).then_inc(y_in[f % 2], 16)

            tiles = out_tiles(l)
            load_y(tiles[0])
            load_y(tiles[1])
            for n, t in enumerate(tiles):
                f = fin_items.index((l, t))
                pool.wait_ge(y_sum.sem, f + 1)
                g_.tensor_tensor(xs[:, t, :], xs[:, t, :], yy[:, f % 2, 0, :], ALU.add).then_inc(x_fin.sem, 1)
                pool.wait_ge(x_fin.sem, f + 1)
                if n + 2 < len(tiles):
                    load_y(tiles[n + 2])
                if t < XT:
                    dst = (x_d if l == 0 else out[0])[t * P:(t + 1) * P, :]
                    pool.dma_start(dst, xs[:, t, :]).then_inc(x_stored, 16)
        pool.wait_ge(x_stored, 64)

    es.close()


def shape_constants():
    import numpy as np

    def dft_pair(n):
        k = np.arange(n)
        a = 2 * np.pi * ((k[:, None] * k[None, :]) % n) / n
        return np.cos(a), np.sin(a)

    cst = np.zeros((P, CONST_W + P), np.float32)
    cst[:, C_ID:C_ID + P] = np.eye(P)
    ct_, st_ = dft_pair(SEQ)
    both = np.concatenate([ct_, st_], 1).reshape(2, P, 512)
    cst[:, C_DFT:C_DFT + 1024] = both.transpose(1, 0, 2).reshape(P, 1024)
    cc, sc = dft_pair(64)
    norm = 1.0 / np.sqrt(SEQ * 64)
    for n, m in enumerate((cc * norm, -sc * norm)):
        for g in range(2):
            cst[64 * g:64 * g + 64, C_CHAN + n * P + 64 * g:C_CHAN + n * P + 64 * g + 64] = m
    tok = np.arange(SEQ)
    col = C_ROPE
    parts = []
    for w in (32, 64):
        inv = np.float32(10000.0) ** (-np.arange(0, w // 2, 2, dtype=np.float32) / np.float32(w // 2))
        ar = (tok // 64).astype(np.float32)[:, None] * inv
        ac = (tok % 64).astype(np.float32)[:, None] * inv
        ang = np.concatenate([ar, ar, ac, ac], 1)
        sign = np.tile(np.repeat([-1.0, 1.0], w // 4), 2)
        parts += [np.cos(ang), np.sin(ang) * sign]
    rope_ = np.concatenate(parts, 1).reshape(2, P, 192)
    cst[:, C_ROPE:C_ROPE + 384] = rope_.transpose(1, 0, 2).reshape(P, 384)
    cst[:, C_IOTA:C_IOTA + P] = np.arange(P)
    j, i = np.meshgrid(np.arange(4), np.arange(4), indexing="ij")
    cst[:, C_LT:C_LT + 16] = (i < j).reshape(-1)
    cst[:, C_DIAG:C_DIAG + 16] = np.where(i == j, -1e30, 0.0).reshape(-1)
    cst[:, C_INVN:C_INVN + 10] = [1 / 256, 1 / 128] + [1 / 64] * 8
    cst[:, C_HALF:C_HALF + 12] = -0.5
    cst[0:4, CONST_W:CONST_W + 2] = [[1, 0], [0, 1], [1, 0], [0, 1]]
    cst[:, C_TOK] = np.arange(P)
    cb = np.zeros((P, CONST_B), np.float32)
    cb[:, B_ID:B_ID + P] = np.eye(P)
    keys = np.arange(SEQ)
    for q in range(2):
        rel = keys[None, :] - (q * P + np.arange(P))[:, None]
        cb[:, B_MASK + q * 256:B_MASK + (q + 1) * 256] = np.where(np.abs(rel) <= 128, 0.0, -1e30)
    cb[:, B_TRI:B_TRI + P] = np.arange(P)[:, None] < np.arange(P)[None, :]
    cb[:, B_ONE:B_ONE + P] = 1.0
    return cst, cb


_INS = ["x", "c", "ctx", "c_ctx", "ada_w", "ada_b", "norm1_g", "norm2_g", "w_in", "fnet_w", "mla_cq_g", "mla_ckv_g",
        "mla_w_uq", "mla_w_uk", "mla_w_uv", "mla_q_g", "mla_k_g", "swa_q_g", "swa_k_g", "swa_sink", "w_out",
        "router_w", "router_b", "exp_w_gate", "exp_w_up", "exp_w_down"]


def kernel(**inputs):
    import numpy as np
    import concourse.bacc as bacc
    from concourse.bass_utils import run_bass_kernel_spmd

    nc = bacc.Bacc("TRN2", target_bir_lowering=False, num_devices=1)
    cst, cb = shape_constants()
    arrays, args = {}, []
    for name in _INS + ["consts", "consts_b"]:
        a = np.ascontiguousarray({"consts": cst, "consts_b": cb}.get(name, inputs.get(name)))
        arrays[f"in_{name}"] = a
        args.append(nc.dram_tensor(f"in_{name}", a.shape, mybir.dt.from_np(a.dtype), kind="ExternalInput").ap())
    out = nc.dram_tensor("out_0", (1, SEQ, D), F32, kind="ExternalOutput").ap()
    build(nc, *args, out)
    r = run_bass_kernel_spmd(nc, [arrays], core_ids=[0])
    return r.results[0]["out_0"]
```

```python
from contextlib import ExitStack

import concourse.bass as bass
from concourse import mybir

F32 = mybir.dt.float32
F32R = mybir.dt.float32r
BF16 = mybir.dt.bfloat16
F16 = mybir.dt.float16
I32 = mybir.dt.int32
ALU = mybir.AluOpType
ACT = mybir.ActivationFunctionType
AX = mybir.AxisListType

P = 128
D = 1024
KT = D // P
DEPTH = 2
SEQ = 256
XT = SEQ // P
NTILES = 4
CQ, CKV, KR, QS, KS, VS, D_IN = 256, 512, 640, 672, 1056, 1184, 1312
NH, QKD, HD, KVH = 6, 96, 64, 2
VM = CQ
NE, GROUP = 16, 4
EPS = 1e-6
BIG = 1 << 20
SLOTS = 128

ROWS = 3
EARLY = 11
RAW = 4
SPL = 3
CHUNK = 512
ADA_CHUNKS = 6 * D // CHUNK
ADA_BODY = 6
IN_UNITS, OUT_UNITS, EXP_UNITS = 6, 4, 6
LAYER_UNITS = IN_UNITS + OUT_UNITS + NE * EXP_UNITS
IN_WIDTH = (512, 512, 288)

C_ID, C_DFT, C_CHAN, C_ROPE, C_IOTA, C_LT, C_DIAG, C_INVN, C_HALF = (
    0, 128, 1152, 1408, 1792, 1920, 1936, 1952, 1996)
C_TOK = 2000
CONST_W = 2001
N_SMALL = 14
B_ID, B_MASK, B_TRI, B_ONE = 0, 128, 640, 768
CONST_B = 896
G_CQ, G_CKV, G_MQ, G_MK, G_SQ, G_SK, G_W = 0, 256, 384, 480, 576, 640, 704


class Stage:

    def __init__(self, sem, items=()):
        self.sem = sem
        self.count = {item: n + 1 for n, item in enumerate(items)}

    def after(self, item):
        return self.count[item]


def u_in(l):
    return DEPTH * 2 * ADA_CHUNKS + l * LAYER_UNITS


def u_out(l):
    return u_in(l) + IN_UNITS


def u_exp(l):
    return u_out(l) + OUT_UNITS


def stream(t):
    return 0 if t < XT else 1


def plus(n, times, i):
    return n if i is None else i * times + n


def in_tiles(l, chunk):
    return [2, 3, 0, 1] if l == 0 or chunk else [0, 1]


def out_tiles(l):
    return [2, 3, 0, 1] if l == 0 else [0, 1]


def jobs(l):
    return [1, 0] if l == 0 else [0]


def queries(l, t):
    return l == 0 or t < XT


def first_uses(l, t):
    return ["c"] + ["q0", "q1"] * queries(l, t) + ["k", "v"]


def last_uses(l, t):
    q = queries(l, t)
    return ["tq0", "tq1"] * q + ["tk0", "tk1"] + ["sq"] * q + ["sk"]


def build(nc, x, c, ctx, c_ctx, ada_w, ada_b, norm1_g, norm2_g, w_in, fnet_w, mla_cq_g, mla_ckv_g,
          mla_w_uq, mla_w_uk, mla_w_uv, mla_q_g, mla_k_g, swa_q_g, swa_k_g, swa_sink, w_out, router_w,
          router_b, exp_w_gate, exp_w_up, exp_w_down, consts, consts_b, out):
    es = ExitStack()

    def sem(name):
        return es.enter_context(nc.semaphore(name))

    def sb(name, shape, dt=F32):
        return es.enter_context(nc.sbuf_tensor(name, shape, dt))

    ps = es.enter_context(nc.psum_tensor("ps", [P, 8, 512], F32))

    raw = [sb(f"raw{i}", [P, 4, 512]) for i in range(RAW)]
    whi = [sb(f"whi{i}", [P, 4, 512], F32R) for i in range(SPL)]
    wlo = [sb(f"wlo{i}", [P, 4, 512], F32R) for i in range(SPL)]
    t_hi = sb("t_hi", [P, KT, NTILES * P], F32R)
    t_lo = sb("t_lo", [P, KT, NTILES * P], F32R)
    cst = sb("cst", [P, CONST_W])
    cstb = sb("cstb", [P, CONST_B], BF16)
    w_uq = sb("w_uq", [P, 2, NH * QKD])
    w_ukv = sb("w_ukv", [P, 2, NH * HD])
    gains = sb("gains", [P, G_W])
    sinks = sb("sinks", [P, 2, NH])
    wbd = sb("wbd", [P, 2, P])
    mch = sb("mch", [P, 2, 2, P])
    rwf = sb("rwf", [P, KT, NE])
    rw = sb("rw", [P, KT, 2, NE], F32R)
    rb = sb("rb", [P, NE])
    ss = sb("ss", [P, 4])
    ms = sb("ms", [P, 4])
    rstd = sb("rstd", [P, 4])
    ss2 = sb("ss2", [P, 2, 22])
    rs2 = sb("rs2", [P, 2, 22])
    nr2 = sb("nr2", [P, 2, 22])

    KIB = 1024
    REGION = 72384
    region = es.enter_context(nc.sbuf_tensor("region", [P, REGION // 4], F32))
    r_base = nc.lookup_mloc(region).addr

    def at(name, off, shape, dt=F32):
        return nc.alloc_sbuf_tensor_at(name, shape, dt, offset=r_base + off)

    xs = at("xs", 0, [P, NTILES, D])
    gb = at("gb", 16 * KIB, [P, 2, D])
    xn = at("xn", 24 * KIB, [P, 2, D])
    hg = at("hg", 24 * KIB, [P, 2, D])
    s_act = at("s_act", 32 * KIB, [P, 512])
    a_act = at("a_act", 34 * KIB, [P, 512])
    at_hi = at("at_hi", 36 * KIB, [P, 4, P], F32R)
    at_lo = at("at_lo", 38 * KIB, [P, 4, P], F32R)
    yb = at("yb", 40 * KIB, [P, 2, D])
    otmp = at("otmp", 40 * KIB, [P, 2, CHUNK])
    junk = at("junk", 44 * KIB, [P, D])
    gain = at("gain", 64 * KIB, [P, D])
    hgt_hi = at("hgt_hi", 48 * KIB, [P, 2, KT, P], F32R)
    hgt_lo = at("hgt_lo", 56 * KIB, [P, 2, KT, P], F32R)
    ab = at("ab", 48 * KIB, [P, 2, 2, D])
    yy = [at(f"yy{n}", kib * KIB, [P, 2, D]) for n, kib in enumerate((24, 32, 40))]
    rt_off = 64 * KIB
    rt_names = {}

    def rt(name, shape, dt=F32, size=4):
        nonlocal rt_off
        n = 1
        for s in shape[1:]:
            n *= s
        t = at(name, rt_off, shape, dt)
        rt_off += (n * size + 31) // 32 * 32
        assert rt_off <= REGION
        return t

    aff = rt("aff", [P, 4, NE])
    sel = rt("sel", [P, 4, NE])
    pair = at("pair", 34 * KIB, [P, 16, 4, 4])
    pair2 = at("pair2", 35 * KIB, [P, 16, 4, 4])
    gsc = rt("gsc", [P, 4, 4])
    gcnt = rt("gcnt", [P, 4, 4])
    best = rt("best", [P, 4, 4])
    cnt = rt("cnt", [P, 4, NE])
    msk = rt("msk", [P, 4, NE])
    mskb = rt("mskb", [P, 4, NE], BF16, 2)
    den = rt("den", [P, 8])
    gate = rt("gate", [P, 4, NE])
    gres = rt("gres", [P, 4, NE])
    posm = rt("posm", [P, 4, NE], F16, 2)
    posf = rt("posf", [P, 4, NE])
    iota16 = rt("iota16", [P, P], F16, 2)
    pay = rt("pay", [P, 4, NE, 8], BF16, 2)
    oh = at("oh", 32 * KIB, [P, 2, 4, P], BF16)
    info = rt("info", [P, NE, 8])
    tokf = rt("tokf", [P, NE])
    oobf = rt("oobf", [P, NE])
    gate_s = rt("gate_s", [P, NE])
    idxg = rt("idxg", [P, NE], I32)
    idxs = rt("idxs", [P, NE], I32)
    cur_g = rt("cur_g", [P, 2], I32)
    cur_s = rt("cur_s", [P, 2], I32)
    most = rt("most", [P, 1], I32)
    info_o = rt("info_o", [P, 8])
    calc_o = rt("calc_o", [P, 4])
    idx_o = rt("idx_o", [P, 2], I32)
    tick = rt("tick", [P, 1])

    c_raw = at("c_raw", 64 * KIB, [P, KT, 2])
    c_act = at("c_act", 64 * KIB + 64, [P, KT, 2])
    comb = at("comb", 64 * KIB + 128, [4, P])
    c_st = at("c_st", 65 * KIB, [P, KT, P], F32R)
    rowp = at("rowp", 32 * KIB, [4, 2, 512])
    row2 = at("row2", 36 * KIB, [2, ROWS, 512])
    cb_raw = at("cb_raw", 24 * KIB, [P, CONST_B])

    pr = at("pr", 0, [P, NTILES, D_IN])
    o = NTILES * D_IN * 4
    qk0 = at("qk0", o, [P, 2 * NH, QKD]); o += 2 * NH * QKD * 4
    sq = at("sq", o, [P, 2 * NH * QKD]); o += 2 * NH * QKD * 4
    cn0 = at("cn0", o, [P, 384])
    o += 384 * 4
    ct0 = at("ct0", o, [P, 3, P]); o += 384 * 4
    kdup = at("kdup", o, [P, 2, 2, HD]); o += 256 * 4
    qt_m = at("qt_m", o, [QKD, NH, 256]); o += NH * 256 * 4
    qt_s = at("qt_s", o, [P, 3, 256]); o += 3 * 256 * 4
    kt_m = at("kt_m", o, [QKD, NH, 512]); o += NH * 512 * 4
    kt_s = at("kt_s", o, [P, KVH, 512]); o += KVH * 512 * 4
    qk = [qk0, at("qk1", o, [P, 2 * NH, QKD])]
    cn = [cn0, at("cn1", o + 4608, [P, 384])]
    ct = [ct0, at("ct1", o + 6144, [P, 3, P])]
    pb = at("pb", o, [P, 2, 512]); o += 1024 * 4
    ptb = at("ptb", o, [P, 2, 4, 256]); o += 2048 * 4
    fab = at("fab", o - 4096, [P, 2, 2, 256])
    mx = at("mx", o, [P, 2]); o += 32
    nb = at("nb", o, [P, 2]); o += 32
    sm = at("sm", o, [P, 2]); o += 32
    esk = at("esk", o, [P, 2]); o += 32
    assert o <= REGION, o

    ada_d = nc.dram_tensor("ada_rows", (2, DEPTH * 6 * D), F32).ap()
    h2_d = nc.dram_tensor("h2_rows", (NTILES * P, D), F32).ap()
    y_d = nc.dram_tensor("y_rows", (NTILES * P * 2, D), F32).ap()
    x_d = nc.dram_tensor("x_rows", (SEQ, D), F32).ap()

    identf = cst[:, C_ID:C_ID + P]
    identb = cstb[:, B_ID:B_ID + P]
    dft = cst[:, C_DFT:C_DFT + 1024].rearrange("p (k n) -> p k n", k=2)
    chan = cst[:, C_CHAN:C_CHAN + 256].rearrange("p (s n) -> p s n", s=2)
    rope = cst[:, C_ROPE:C_ROPE + 384].rearrange("p (t n) -> p t n", t=2)
    half = cst[:, C_HALF:C_HALF + 4]
    maskb = cstb[:, B_MASK:B_MASK + 512].rearrange("p (t n) -> p t n", t=2)

    L = range(DEPTH)
    c_in = sem("c_in")
    const_in, small_in, x_in = sem("const_in"), sem("small_in"), sem("x_in")
    w_landed = [sem(f"w_landed{i}") for i in range(RAW)]
    w_hi, w_lo, w_used = sem("w_hi"), sem("w_lo"), sem("w_used")
    setup_dve, setup_act = sem("setup_dve"), sem("setup_act")
    dve_chain, act_chain, pool_chain = sem("dve_chain"), sem("act_chain"), sem("pool_chain")
    ada_copied, ada_comb, ada_row = sem("ada_copied"), sem("ada_comb"), sem("ada_row")
    ada_bias_in = sem("ada_bias_in")
    ada_stored = [sem(f"ada_stored{i}") for i in range(ROWS)]
    gb_in = sem("gb_in")
    norms = [(l, w) for l in L for w in (1, 2)]
    ab_in = {norm: sem("ab_in_%d_%d" % norm) for norm in norms}

    def norm_bank(l, w):
        return 4 if (l, w) == (0, 1) else 0

    def norm_tiles(l, w):
        return [2, 3, 0, 1] if w == 1 else out_tiles(l)

    tile_items = [(l, w, t) for l, w in norms for t in norm_tiles(l, w)]
    ab_ready = Stage(sem("ab_ready"), norms)
    sumsq = Stage(sem("sumsq"), tile_items)
    mean_ready = Stage(sem("mean_ready"), tile_items)
    rstd_ready = Stage(sem("rstd_ready"), tile_items)
    h_scaled = Stage(sem("h_scaled"), tile_items)
    h_ready = Stage(sem("h_ready"), tile_items)
    ht_full = Stage(sem("ht_full"), tile_items)
    ht_hi = Stage(sem("ht_hi"), tile_items)
    ht_split = Stage(sem("ht_split"), tile_items)
    h2_items = [i for i in tile_items if i[1] == 2]
    h2_stored = [sem(f"h2_stored{i}") for i in range(2)]

    p_items = [(l, ch, t) for l in L for ch in range(3) for t in in_tiles(l, ch)]
    p_full = Stage(sem("p_full"), [i for i in p_items if i[2] != in_tiles(i[0], i[1])[-1]])
    p_act = Stage(sem("p_act"), [i for i in p_items if i[2] >= XT])
    p_dve = Stage(sem("p_dve"), [i for i in p_items if i[2] < XT])

    ring_items = []
    for l in L:
        ring_items.append((l, "m"))
        for s in jobs(l) if l == 0 else [1, 0]:
            for t in (2 * s, 2 * s + 1):
                ring_items += [(l, t, u) for u in first_uses(l, t)]
            if s in jobs(l):
                ring_items += [(l, s, "f0"), (l, s, "f1"), (l, s, "fy")]
            for t in (2 * s, 2 * s + 1):
                ring_items += [(l, t, u) for u in last_uses(l, t)]
    ring_pos = {it: n for n, it in enumerate(ring_items)}
    ring_full = Stage(sem("ring_full"), ring_items)
    ring_free = Stage(sem("ring_free"), ring_items)
    fm_items = [(l, s) for l in L for s in jobs(l)]
    fmix_hi = Stage(sem("fmix_hi"), fm_items)
    fmix_lo = Stage(sem("fmix_lo"), fm_items)
    prep_items = [(l, t) for l in L for t in (2, 3, 0, 1)]
    c_squares, c_mean, c_root, cn_ready, sw_done = (Stage(sem(n), prep_items) for n in (
        "c_squares", "c_mean", "c_root", "cn_ready", "sw_done"))
    qk_squares, qk_reduced, qk_mean, qk_root, qk_done = (Stage(sem(n), prep_items) for n in (
        "qk_squares", "qk_reduced", "qk_mean", "qk_root", "qk_done"))
    m_ready = sem("m_ready")

    units = [(l, s, h, q) for l in L for s in jobs(l) for h in range(2 * NH) for q in range(2)]
    unit_pos = {u: n for n, u in enumerate(units)}
    heads = [(l, s, h) for l in L for s in jobs(l) for h in range(2 * NH)]
    s_full, nb_ready, exp_done, p_norm, pt_full, pt_copied = (
        Stage(sem(n), units) for n in ("s_full", "nb_ready", "exp_done", "p_norm", "pt_full", "pt_copied"))
    o_full, mix_hi, mix_lo = (Stage(sem(n), heads) for n in ("o_full", "mix_hi", "mix_lo"))

    out_items = [(l, ch, t) for l in L for ch in range(2) for t in out_tiles(l)]
    op_scaled, x_upd = (Stage(sem(n), out_items) for n in ("op_scaled", "x_upd"))
    op_full = Stage(sem("op_full"), [i for i in out_items if i[2] != out_tiles(i[0])[-1]])

    def await_p(eng, l, ch, t):
        if t == in_tiles(l, ch)[-1]:
            eng.wait_ge(w_used, u_in(l) + 2 * ch + 2)
        else:
            eng.wait_ge(p_full.sem, p_full.after((l, ch, t)))

    def await_ada(eng, l):
        if l == 0:
            for r in range(ROWS):
                eng.wait_ge(ada_stored[r], 16 * DEPTH * ADA_CHUNKS // ROWS)

    def await_op(eng, l, ch, t):
        if t == out_tiles(l)[-1]:
            eng.wait_ge(w_used, u_out(l) + 2 * ch + 2)
        else:
            eng.wait_ge(op_full.sem, op_full.after((l, ch, t)))

    lg_sum = sem("lg_sum")
    lg_full, aff_ready, msk_ready, pos_full, info_full, idx_ready = (
        sem(n) for n in ("lg_full", "aff_ready", "msk_ready", "pos_full", "info_full", "idx_ready"))
    oh_ready, oh_used = sem("oh_ready"), sem("oh_used")
    gathered = [sem(f"gathered{i}") for i in range(2)]
    scattered = [sem(f"scattered{i}") for i in range(2)]
    silu_done, a_ready, ta_full, at_hi_done, at_split = (
        sem(n) for n in ("silu_done", "a_ready", "ta_full", "at_hi_done", "at_split"))
    y_ready, tg_full, hgt_hi_done, hgt_split, cur_g_ready, cur_s_ready = (
        sem(n) for n in ("y_ready", "tg_full", "hgt_hi_done", "hgt_split", "cur_g_ready", "cur_s_ready"))
    y_in = [sem(f"y_in{i}") for i in range(4)]
    fin_items = [(l, t) for l in L for t in out_tiles(l)]
    y_sum = Stage(sem("y_sum"), fin_items)

    def y_buf(f):
        return (0, 1, 2, 1)[f % 4]

    x_fin = Stage(sem("x_fin"), fin_items)
    x_stored = sem("x_stored")

    def layer_sems(name):
        return [sem(f"{name}_{l}") for l in L]

    v_turn, v_oh, v_info, v_idx, v_step, v_gathered, v_scattered = (layer_sems(n) for n in (
        "v_turn", "v_oh", "v_info", "v_idx", "v_step", "v_gathered", "v_scattered"))
    v_rows_full, v_rows_hi, v_rows_lo, v_silu, v_act, v_act_full, v_act_hi, v_act_lo, v_y = (layer_sems(n) for n in (
        "v_rows_full", "v_rows_hi", "v_rows_lo", "v_silu", "v_act", "v_act_full", "v_act_hi", "v_act_lo", "v_y"))
    v_landed = [[sem(f"v_landed{j}_{l}") for j in range(SPL)] for l in L]
    v_hi, v_lo, v_used, v_shift = (layer_sems(n) for n in ("v_hi", "v_lo", "v_used", "v_shift"))

    def more_rounds(l):
        return len(out_tiles(l)) * P // SLOTS - 1

    def overflow(eng, l, one_round, each=None):
        eng.wait_ge(idx_ready, 2 * l + 2)
        biggest = eng.value_load(most[0:1, 0:1], min_val=0, max_val=NTILES * P)
        with eng.If(biggest > SLOTS):
            with eng.Fori(0, more_rounds(l)) as c:
                if each is not None:
                    each(c)
                with eng.Fori(0, NE) as e:
                    n = c * NE + e
                    eng.wait_ge(v_turn[l], n + 1)
                    if each is not None:
                        eng.wait_ge(v_shift[l], c + 1)
                    one_round(e, n)
            eng.wait_ge(v_turn[l], more_rounds(l) * NE + 1)

    N_CONST = 5

    def make_chain(eng, s):
        n = [0]

        def link(ins):
            n[0] += 1
            ins.then_inc(s, 1)
            eng.wait_ge(s, n[0])
        return link

    def load_unit(sp, u, src, i=None, width=512):
        if u >= RAW:
            sp.wait_ge(w_lo, plus(u - RAW + 1, 12, i))
        sp.dma_start(raw[u % RAW][:, :, 0:width], src).then_inc(w_landed[u % RAW], 16)

    def split_hi(act, u, i=None, width=512):
        act.wait_ge(w_landed[u % RAW], plus(16 * (u // RAW + 1), 48, i))
        if u >= SPL:
            act.wait_ge(w_used, plus(u - SPL + 1, 12, i))
        nc.scalar.activation(whi[u % SPL][:, :, 0:width], raw[u % RAW][:, :, 0:width], ACT.Copy).then_inc(w_hi, 1)

    def split_lo(dve, u, i=None, width=512):
        dve.wait_ge(w_hi, plus(u + 1, 12, i))
        nc.vector.tensor_tensor(wlo[u % SPL][:, :, 0:width], raw[u % RAW][:, :, 0:width],
                                whi[u % SPL][:, :, 0:width].bitcast(F32), ALU.subtract).then_inc(w_lo, 1)

    def await_unit(pe, u, i=None):
        pe.wait_ge(w_lo, plus(u + 1, 12, i))

    def product3(out_, hi, lo, whi_, wlo_, first, last):
        nc.tensor.matmul(out_, hi, whi_, start=first, stop=False)
        nc.tensor.matmul(out_, hi, wlo_, start=False, stop=False)
        return nc.tensor.matmul(out_, lo, whi_, start=False, stop=last)

    def ada_src(g, i, kh):
        layer, col = g // ADA_CHUNKS, g % ADA_CHUNKS * CHUNK
        v = ada_w[layer:layer + 1] if i is None else ada_w[bass.ds(i, 1)]
        col = col if i is None else i * (-ADA_BODY * CHUNK) + col
        return v.rearrange("l (kh kk p) n -> kh p (l kk) n", kh=2, p=P)[kh][:, :, bass.ds(col, CHUNK)]

    def in_src(l, ch, kh):
        return w_in[l].rearrange("(kh kk p) n -> kh p kk n", kh=2, p=P)[kh][:, :, ch * 512:ch * 512 + IN_WIDTH[ch]]

    def out_src(l, ch, kh):
        return w_out[l].rearrange("(kh kk p) n -> kh p kk n", kh=2, p=P)[kh][:, :, ch * 512:(ch + 1) * 512]

    def e_src(w, l, e, part):
        we = w[l][bass.ds(e, 1)]
        if part < 2:
            return we.rearrange("e (kh kk p) n -> kh p (e kk) n", kh=2, p=P)[part]
        return we.rearrange("e (kk p) n -> p (e kk) n", p=P)[:, :, (part - 2) * 512:(part - 1) * 512]

    def after_turn(l, e):
        return u_exp(l) + 6 * e + 4

    def e_base(l, e_s):
        return u_exp(l) + (0 if e_s == 0 else 4 + 6 * (e_s - 1))

    def ada_first(eng, body):
        body(0, None)
        with eng.Fori(0, 2) as i:
            body(ADA_BODY, i)

    def ada_last(eng, body):
        body(3 * ADA_BODY, None)

    def ab_src(s, l, k):
        off = (l * 6 + k) * D
        return ada_d[s, off:off + D].partition_broadcast(P)

    def row_bc(v, l, n):
        return v[l, 0:n].partition_broadcast(P)

    def load_ab(eng, l, w):
        k = 3 * (w - 1)
        for s in range(2):
            eng.dma_start(ab[:, s, 0, :], ab_src(s, l, k + 1)).then_inc(ab_in[l, w], 16)
            eng.dma_start(ab[:, s, 1, :], ab_src(s, l, k)).then_inc(ab_in[l, w], 16)
        eng.dma_start(gb[:, 0, :] if (l, w) == (0, 1) else gain[:], row_bc(norm1_g if w == 1 else norm2_g, l, D)).then_inc(ab_in[l, w], 16)

    block = es.enter_context(nc.Block())

    @block.sync
    def _(sp):
        with nc.allow_non_contiguous_dma(reason="two vectors, once"):
            sp.dma_start(c_raw[:, :, 0:1], c.rearrange("a (k p) -> p k a", p=P)).then_inc(c_in, 16)
            sp.dma_start(c_raw[:, :, 1:2], c_ctx.rearrange("(k p a) -> p k a", p=P, a=1)).then_inc(c_in, 16)

        def load_constants():
            for dst, src in ((cst[:], consts[:, 0:CONST_W]), (comb[:], consts[0:4, CONST_W:CONST_W + P]), (cb_raw[:], consts_b),
                             (rwf[:], router_w.rearrange("(k p) e -> p k e", p=P)), (rb[:], router_b.partition_broadcast(P))):
                sp.dma_start(dst, src).then_inc(const_in, 16)

        def ada_loads(g, i):
            for j in range(ADA_BODY):
                for kh in range(2):
                    load_unit(sp, 2 * (g + j) + kh, ada_src(g + j, i, kh), i)
                if g + j == 0:
                    load_constants()
        ada_first(sp, ada_loads)
        ada_last(sp, ada_loads)
        for l in L:
            for ch in range(3):
                for kh in range(2):
                    load_unit(sp, u_in(l) + 2 * ch + kh, in_src(l, ch, kh), width=IN_WIDTH[ch])
            for ch in range(2):
                for kh in range(2):
                    load_unit(sp, u_out(l) + 2 * ch + kh, out_src(l, ch, kh))

            def turn(e, e_s, i, first=False):
                b = e_base(l, e_s)
                for kh in range(2):
                    load_unit(sp, b + kh, e_src(exp_w_gate, l, e, kh), i)
                n = 2
                if not first:
                    for ch in range(2):
                        load_unit(sp, b + 2 + ch, e_src(exp_w_down, l, e - 1, 2 + ch), i)
                    n = 4
                for kh in range(2):
                    load_unit(sp, b + n + kh, e_src(exp_w_up, l, e, kh), i)

            turn(0, 0, None, True)
            for n, t in enumerate(out_tiles(l)):
                sp.wait_ge(h_ready.sem, h_ready.after((l, 2, t)))
                sp.dma_start(h2_d[t * P:(t + 1) * P, :], xn[:, n % 2, :]).then_inc(h2_stored[n % 2], 16)
            with sp.Fori(0, 7) as i:
                turn(i * 2 + 1, 1, i)
                turn(i * 2 + 2, 2, i)
            turn(15, 15, None)
            for ch in range(2):
                load_unit(sp, e_base(l, 16) + ch, e_src(exp_w_down, l, 15, 2 + ch))

            def one_round(e, n):
                for j in range(EXP_UNITS):
                    if j >= SPL:
                        sp.wait_ge(v_lo[l], n * EXP_UNITS + (j - SPL + 1))
                    w = (exp_w_gate, exp_w_up, exp_w_down)[j // 2]
                    sp.dma_start(raw[j % SPL][:], e_src(w, l, e, j % 2 + 2 * (j >= 4))).then_inc(v_landed[l][j % SPL], 16)
            overflow(sp, l, one_round)

            for par in range(2):
                sp.wait_ge(scattered[par], 16 * 8 * (l + 1))
            sp.wait_ge(w_used, u_exp(l) + NE * EXP_UNITS)

            def load_y(t):
                f = fin_items.index((l, t))
                sp.dma_start(yy[y_buf(f)][:].rearrange("p a d -> p (a d)"),
                             y_d[t * 2 * P:(t + 1) * 2 * P, :].rearrange("(p k) d -> p (k d)", k=2)).then_inc(y_in[f % 4], 16)

            tiles = out_tiles(l)
            for t in tiles[:3]:
                load_y(t)
            if l == 0:
                load_ab(sp, 1, 1)
                sp.wait_ge(x_fin.sem, x_fin.after((l, tiles[1])))
                load_y(tiles[3])

    @block.tensor
    def _(pe):
        def ada(g0, i):
            for j in range(ADA_BODY):
                g = g0 + j
                if g >= 2:
                    pe.wait_ge(ada_copied, plus(g - 1, ADA_BODY, i))
                for kh in range(2):
                    u = 2 * g + kh
                    await_unit(pe, u, i)
                    for kk in range(4):
                        k = 4 * kh + kk
                        nc.tensor.matmul(ps[:, g % 2, :], c_st[:, k, :], whi[u % SPL][:, kk, :], start=k == 0, stop=False)
                        mm = nc.tensor.matmul(ps[:, g % 2, :], c_st[:, k, :], wlo[u % SPL][:, kk, :], start=False, stop=k == KT - 1)
                    mm.then_inc(w_used, 1)
                if g:
                    combine(g - 1, i)

        def combine(g, i):
            if g == 0:
                pe.wait_ge(const_in, 16 * N_CONST)
            pe.wait_ge(ada_copied, plus(g + 1, ADA_BODY, i))
            if g >= 2:
                pe.wait_ge(ada_row, plus(g - 1, ADA_BODY, i))
            nc.tensor.matmul(ps[:, 2 + g % 2, :], comb[:], rowp[0:4, g % 2, :],
                             start=True, stop=True).then_inc(ada_comb, 1)

        def norm(l, w):
            tiles = norm_tiles(l, w)
            if w == 2:
                pe.wait_ge(op_scaled.sem, op_scaled.after((l, 1, tiles[-1])))
            elif l:
                pe.wait_ge(y_ready, NE * l)
            for n, t in enumerate(tiles):
                pe.wait_ge(h_ready.sem, h_ready.after((l, w, t)))
                if n >= 2:
                    pe.wait_ge(ht_split.sem, ht_split.after((l, w, tiles[n - 2])))
                for k in range(KT):
                    mm = nc.tensor.transpose(ps[:, norm_bank(l, w) + 2 * (n % 2) + k // 4, k % 4 * P:(k % 4 + 1) * P],
                                             xn[:, n % 2, k * P:(k + 1) * P], identf)
                mm.then_inc(ht_full.sem, 1)
                if w == 2 and n:
                    logits(l, tiles[n - 1])
            if w == 2:
                logits(l, tiles[-1]).then_inc(lg_full, 1)

        def logits(l, t):
            pe.wait_ge(ht_split.sem, ht_split.after((l, 2, t)))
            for k in range(KT):
                for part in (t_hi, t_lo):
                    mm = nc.tensor.matmul(ps[:, 4, t * 2 * NE:(t + 1) * 2 * NE], part[:, k, t * P:(t + 1) * P],
                                          rw[:, k, :, :].rearrange("p a e -> p (a e)"), start=k == 0 and part is t_hi,
                                          stop=k == KT - 1 and part is t_lo)
            return mm

        def in_proj(l):
            pe.wait_ge(ht_split.sem, ht_split.after((l, 1, norm_tiles(l, 1)[-1])))
            for ch in range(3):
                n = IN_WIDTH[ch]
                bank = 4 if ch % 2 == 0 else 0
                if ch == 1 and l == 0:
                    pe.wait_ge(ada_row, 2 * ADA_CHUNKS)
                if ch == 2:
                    pe.wait_ge(p_dve.sem, p_dve.after((l, 0, 1)))
                    if l == 0:
                        pe.wait_ge(p_act.sem, p_act.after((l, 0, 3)))
                tiles = in_tiles(l, ch)
                for kh in range(2):
                    u = u_in(l) + 2 * ch + kh
                    await_unit(pe, u)
                    for t in tiles:
                        for kk in range(4):
                            k = 4 * kh + kk
                            mm = product3(ps[:, bank + t, 0:n], t_hi[:, k, t * P:(t + 1) * P], t_lo[:, k, t * P:(t + 1) * P],
                                          whi[u % SPL][:, kk, 0:n], wlo[u % SPL][:, kk, 0:n], k == 0, k == KT - 1)
                        if kh == 1 and t != tiles[-1]:
                            mm.then_inc(p_full.sem, 1)
                    mm.then_inc(w_used, 1)

        def ring(item):
            n = ring_pos[item]
            if n >= 3:
                pe.wait_ge(ring_free.sem, n - 2)
            return n % 3

        def channel_mix(l):
            pe.wait_ge(small_in, 16 * N_SMALL * (l + 1))
            b = ring((l, "m"))
            for pr_ in range(2):
                for cs in range(2):
                    o_ = (2 * pr_ + cs) * P
                    mm = nc.tensor.matmul(ps[:, b, o_:o_ + P], chan[:, cs, :], wbd[:, pr_, :], start=True, stop=True)
            mm.then_inc(ring_full.sem, 1)

        def prep_first(l, t):
            q, par = queries(l, t), t % 2
            pe.wait_ge(cn_ready.sem, cn_ready.after((l, t)))
            b = ring((l, t, "c"))
            for n in range(3) if q else [2]:
                mm = nc.tensor.transpose(ps[:, b, n * P:(n + 1) * P], cn[par][:, n * P:(n + 1) * P], identf)
            mm.then_inc(ring_full.sem, 1)
            pe.wait_ge(ring_free.sem, ring_free.after((l, t, "c")))
            if q:
                for n in range(2):
                    b = ring((l, t, f"q{n}"))
                    for k in range(2):
                        mm = nc.tensor.matmul(ps[:, b, 0:288], ct[par][:, k, :], w_uq[:, k, n * 288:(n + 1) * 288],
                                              start=k == 0, stop=k == 1)
                    mm.then_inc(ring_full.sem, 1)
            for n, what in enumerate("kv"):
                b = ring((l, t, what))
                nc.tensor.matmul(ps[:, b, 0:384], ct[par][:, 2, :], w_ukv[:, n, :], start=True, stop=True).then_inc(ring_full.sem, 1)

        def prep_last(l, t):
            q, par = queries(l, t), t % 2
            pe.wait_ge(qk_done.sem, qk_done.after((l, t)))
            for what, h0 in (("tq", 0), ("tk", NH)):
                if what == "tq" and not q:
                    continue
                for n in range(2):
                    b = ring((l, t, f"{what}{n}"))
                    for h in range(4 * n, min(4 * n + 4, NH)):
                        mm = nc.tensor.transpose(ps[0:QKD, b, (h - 4 * n) * P:(h - 4 * n + 1) * P], qk[par][:, h0 + h, :], identf)
                    mm.then_inc(ring_full.sem, 1)
            pe.wait_ge(sw_done.sem, sw_done.after((l, t)))
            if q:
                b = ring((l, t, "sq"))
                for n in range(3):
                    mm = nc.tensor.transpose(ps[:, b, n * P:(n + 1) * P], pr[:, t, QS + n * P:QS + (n + 1) * P], identf)
                mm.then_inc(ring_full.sem, 1)
            b = ring((l, t, "sk"))
            for n in range(KVH):
                mm = nc.tensor.transpose(ps[:, b, n * P:(n + 1) * P], kdup[:, n, :, :].rearrange("p a d -> p (a d)"), identf)
            mm.then_inc(ring_full.sem, 1)

        def fourier(l, s):
            for ch in range(2):
                b = ring((l, s, f"f{ch}"))
                for k in range(XT):
                    mm = nc.tensor.matmul(ps[:, b, :], pr[:, 2 * s + k, ch * P:(ch + 1) * P], dft[:, k, :],
                                          start=k == 0, stop=k == XT - 1)
                mm.then_inc(ring_full.sem, 1)
            pe.wait_ge(ring_free.sem, ring_free.after((l, s, "f1")))
            b = ring((l, s, "fy"))
            for ch in range(2):
                for cs in range(2):
                    mm = nc.tensor.matmul(ps[:, b, ch * 256:(ch + 1) * 256], mch[:, ch, cs, :], fab[:, ch, cs, :],
                                          start=cs == 0, stop=cs == 1)
            mm.then_inc(ring_full.sem, 1)

        def attend(l, s):
            us = [(l, s, h, q) for h in range(2 * NH) for q in range(2)]
            nk = 4 if s == 0 else 2
            key0 = 0 if s == 0 else 256
            pe.wait_ge(ring_free.sem, ring_free.after((l, 2 * s + 1, "sk")))

            def scores(n):
                _, _, h, q = u = us[n]
                g = unit_pos[u]
                if g >= 2:
                    pe.wait_ge(exp_done.sem, g - 1)
                b = 4 + g % 2
                cols = slice(q * P, (q + 1) * P)
                if h < NH:
                    mm = nc.tensor.matmul(ps[:, b, 0:nk * P], qt_m[:, h, cols], kt_m[:, h, key0:key0 + nk * P],
                                          start=True, stop=True)
                else:
                    r = 64 * ((h - NH) % 2)
                    for k0 in range(0, nk * P, 256):
                        masked = s == 0 and k0 == 0
                        mm = nc.tensor.matmul(ps[:, b, k0:k0 + 256], qt_s[r:r + 64, (h - NH) // 2, cols],
                                              kt_s[r:r + 64, (h - NH) // 3, key0 + k0:key0 + k0 + 256],
                                              start=True, stop=not masked)
                        if masked:
                            mm = nc.tensor.matmul(ps[:, b, 0:256], identb, maskb[:, q, :], start=False, stop=True)
                mm.then_inc(s_full.sem, 1)

            def turn_probs(n):
                u = us[n]
                g = unit_pos[u]
                pe.wait_ge(p_norm.sem, p_norm.after(u))
                if g >= 2:
                    pe.wait_ge(pt_copied.sem, g - 1)
                for j in range(nk):
                    mm = nc.tensor.transpose(ps[:, 6 + g % 2, j * P:(j + 1) * P], pb[:, g % 2, j * P:(j + 1) * P], identf)
                mm.then_inc(pt_full.sem, 1)

            def values(h, part):
                pe.wait_ge(pt_copied.sem, pt_copied.after((l, s, h, 1)))
                hn = heads.index((l, s, h))
                if part == 0 and hn >= 2:
                    pe.wait_ge(mix_lo.sem, hn - 1)
                r = (256 + HD * h) % P
                for j in range(part * nk // 2, (part + 1) * nk // 2):
                    kt = j if s == 0 else 2 + j
                    v0 = VM + HD * h if h < NH else VS + HD * ((h - NH) // 3)
                    mm = nc.tensor.matmul(ps[r:r + 64, 2 + h % 2, 0:256], pr[:, kt, v0:v0 + HD], ptb[:, h % 2, j, :],
                                          start=j == 0, stop=j == nk - 1)
                if part:
                    mm.then_inc(o_full.sem, 1)

            for n in range(len(us) + 4):
                if n < len(us):
                    scores(n)
                if 2 <= n < len(us) + 2:
                    turn_probs(n - 2)
                if n >= 4:
                    values((n - 4) // 2, n % 2)

        def out_proj(l):
            pe.wait_ge(mix_lo.sem, mix_lo.after((l, 0, 2 * NH - 1)))
            pe.wait_ge(fmix_lo.sem, fmix_lo.after((l, 0)))
            for ch in range(2):
                bank = 4 if ch == 0 else 0
                tiles = out_tiles(l)
                for kh in range(2):
                    u = u_out(l) + 2 * ch + kh
                    await_unit(pe, u)
                    for t in tiles:
                        for kk in range(4):
                            k = 4 * kh + kk
                            mm = product3(ps[:, bank + t, :], t_hi[:, k, t * P:(t + 1) * P], t_lo[:, k, t * P:(t + 1) * P],
                                          whi[u % SPL][:, kk, :], wlo[u % SPL][:, kk, :], k == 0, k == KT - 1)
                        if kh == 1 and t != tiles[-1]:
                            mm.then_inc(op_full.sem, 1)
                    mm.then_inc(w_used, 1)

        def route(l):
            tiles = out_tiles(l)
            nt = len(tiles)
            pe.wait_ge(msk_ready, l + 1)
            for t in range(nt + 1):
                last = min(t, nt - 1)
                for t2 in range(last + 1):
                    mm = nc.tensor.matmul(ps[:, 5, t * NE:(t + 1) * NE], cstb[:, (B_TRI if t2 == t else B_ONE):][:, 0:P],
                                          mskb[:, t2, :], start=t2 == 0, stop=t2 == last)
            mm.then_inc(pos_full, 1)
            for e in range(NE):
                if e == EARLY:
                    turn_rows(l, 0, 0, None)
                pe.wait_ge(oh_ready, l * NE + e + 1)
                for t in range(nt):
                    mm = nc.tensor.matmul(ps[:, 6, e * 8:(e + 1) * 8], oh[:, e % 2, t, :], pay[:, t, e, :],
                                          start=t == 0, stop=t == nt - 1)
                mm.then_inc(oh_used, 1)

        def turn_rows(l, e, par, i):
            pe.wait_ge(gathered[par], plus(16 * (l * 8 + e // 2 + 1), 16, i))
            if l or e:
                pe.wait_ge(hgt_split, plus(l * NE + e, 2, i))
            for k in range(KT):
                mm = nc.tensor.transpose(ps[:, k // 4, k % 4 * P:(k % 4 + 1) * P], hg[:, par, k * P:(k + 1) * P], identf)
            mm.then_inc(tg_full, 1)

        def experts_half(bank, par, kh, u, i):
            await_unit(pe, u, i)
            for kk in range(4):
                k = 4 * kh + kk
                mm = product3(ps[:, bank, :], hgt_hi[:, par, k, :], hgt_lo[:, par, k, :],
                              whi[u % SPL][:, kk, :], wlo[u % SPL][:, kk, :], k == 0, k == KT - 1)
            mm.then_inc(w_used, 1)

        def turn_act(l, e, i):
            pe.wait_ge(a_ready, plus(l * NE + e + 1, 2, i))
            if l or e or i is not None:
                pe.wait_ge(at_split, plus(l * NE + e, 2, i))
            for k in range(4):
                mm = nc.tensor.transpose(ps[:, 4, k * P:(k + 1) * P], a_act[:, k * P:(k + 1) * P], identf)
            mm.then_inc(ta_full, 1)

        def down(l, e, b, i):
            pe.wait_ge(at_split, plus(l * NE + e + 1, 2, i))
            for ch in range(2):
                u = b + ch
                await_unit(pe, u, i)
                if ch == 0 and (l or e or i is not None):
                    pe.wait_ge(y_ready, plus(l * NE + e, 2, i))
                for k in range(4):
                    mm = product3(ps[:, 5 + ch, :], at_hi[:, k, :], at_lo[:, k, :],
                                  whi[u % SPL][:, k, :], wlo[u % SPL][:, k, :], k == 0, k == 3)
                mm.then_inc(w_used, 1)

        def experts(l):
            def turn(e, i):
                b = e_base(l, e)
                par = e % 2
                pe.wait_ge(hgt_split, plus(l * NE + e + 1, 2, i))
                if e:
                    pe.wait_ge(silu_done, plus(l * NE + e, 2, i))
                experts_half(2, par, 0, b, i)
                if e:
                    turn_act(l, e - 1, i)
                experts_half(2, par, 1, b + 1, i)
                if e:
                    down(l, e - 1, b + 2, i)
                if e < NE - 1:
                    turn_rows(l, e + 1, 1 - par, i)
                b = b + (4 if e else 2)
                experts_half(3, par, 0, b, i)
                experts_half(3, par, 1, b + 1, i)

            turn(0, None)
            with pe.Fori(0, 7) as i:
                turn(1, i)
                turn(2, i)
            turn(NE - 1, None)
            turn_act(l, NE - 1, None)
            down(l, NE - 1, e_base(l, NE), None)

            def one_round(e, n):
                nt = len(out_tiles(l))
                pe.wait_ge(v_oh[l], n + 1)
                for t in range(nt):
                    mm = nc.tensor.matmul(ps[:, 7, 0:8], oh[:, 0, t, :], pay[:, t, bass.ds(e, 1), :].rearrange("p a n -> p (a n)"),
                                          start=t == 0, stop=t == nt - 1)
                mm.then_inc(v_info[l], 1)
                pe.wait_ge(v_gathered[l], n * 16 + 16)
                for k in range(KT):
                    mm = nc.tensor.transpose(ps[:, k // 4, k % 4 * P:(k % 4 + 1) * P], hg[:, 0, k * P:(k + 1) * P], identf)
                mm.then_inc(v_rows_full[l], 1)
                pe.wait_ge(v_rows_lo[l], n + 1)
                for j in range(4):
                    pe.wait_ge(v_lo[l], n * EXP_UNITS + (j + 1))
                    for kk in range(4):
                        k = 4 * (j % 2) + kk
                        mm = product3(ps[:, 2 + j // 2, :], hgt_hi[:, 0, k, :], hgt_lo[:, 0, k, :],
                                      whi[j % SPL][:, kk, :], wlo[j % SPL][:, kk, :], k == 0, k == KT - 1)
                    mm.then_inc(v_used[l], 1)
                pe.wait_ge(v_act[l], n + 1)
                for k in range(4):
                    mm = nc.tensor.transpose(ps[:, 4, k * P:(k + 1) * P], a_act[:, k * P:(k + 1) * P], identf)
                mm.then_inc(v_act_full[l], 1)
                pe.wait_ge(v_act_lo[l], n + 1)
                for j in range(4, EXP_UNITS):
                    pe.wait_ge(v_lo[l], n * EXP_UNITS + (j + 1))
                    for k in range(4):
                        mm = product3(ps[:, 1 + j, :], at_hi[:, k, :], at_lo[:, k, :],
                                      whi[j % SPL][:, k, :], wlo[j % SPL][:, k, :], k == 0, k == 3)
                    mm.then_inc(v_used[l], 1)
            overflow(pe, l, one_round)

        pe.wait_ge(setup_dve, 3)
        ada_first(pe, ada)
        norm(0, 1)
        pe.wait_ge(setup_dve, 5)
        ada_last(pe, ada)
        combine(2 * ADA_CHUNKS - 1, None)
        for l in L:
            if l:
                norm(l, 1)
            in_proj(l)
            channel_mix(l)
            for s in [1, 0]:
                for t in (2 * s, 2 * s + 1):
                    prep_first(l, t)
                if s in jobs(l):
                    fourier(l, s)
                for t in (2 * s, 2 * s + 1):
                    prep_last(l, t)
                if s in jobs(l):
                    attend(l, s)
            out_proj(l)
            norm(l, 2)
            route(l)
            experts(l)

    @block.scalar
    def _(act):
        link = make_chain(act, act_chain)

        def ada(g0, i):
            for j in range(ADA_BODY):
                g = g0 + j
                for kh in range(2):
                    split_hi(act, 2 * g + kh, i)
                if g:
                    copy_rows(g - 1, i)

        def copy_rows(g, i):
            act.wait_ge(w_used, plus(2 * g + 2, 12, i))
            if g >= 2:
                act.wait_ge(ada_comb, plus(g - 1, ADA_BODY, i))
            nc.scalar.activation(rowp[0:4, g % 2, :], ps[0:4, g % 2, :], ACT.Copy).then_inc(ada_copied, 1)

        act.wait_ge(c_in, 32)
        link(nc.scalar.activation(c_act[:], c_raw[:], ACT.Silu))
        act.wait_ge(setup_dve, 1)
        nc.scalar.activation(c_st[:, :, 0:2], c_act[:], ACT.Copy).then_inc(setup_act, 1)
        def norm(l, w):
            tiles = norm_tiles(l, w)
            if (l, w) == (0, 1):
                act.wait_ge(x_in, 32)
            for n, t in enumerate(tiles):
                if w == 2:
                    act.wait_ge(x_upd.sem, x_upd.after((l, 1, t)))
                elif l:
                    act.wait_ge(x_fin.sem, x_fin.after((l - 1, t)))
                if n:
                    act.wait_ge(sumsq.sem, sumsq.after((l, w, tiles[n - 1])))
                squares = junk[:] if (l, w) == (0, 1) else ps[:, 6:8, :].rearrange("p b n -> p (b n)")
                nc.scalar.activation(squares, xs[:, t, :], ACT.Square, accum_out=ss[:, t:t + 1]).then_inc(sumsq.sem, 1)
            if w == 2:
                act.wait_ge(w_used, u_out(l) + OUT_UNITS)
            for t in tiles:
                act.wait_ge(ht_full.sem, ht_full.after((l, w, t)))
                b = norm_bank(l, w) + 2 * (tiles.index(t) % 2)
                nc.scalar.activation(t_hi[:, :, t * P:(t + 1) * P],
                                     ps[:, b:b + 2, :].rearrange("p b (k t) -> p (b k) t", t=P), ACT.Copy).then_inc(ht_hi.sem, 1)

        def in_proj(l):
            if l:
                act.wait_ge(x_stored, 32)
            for ch in range(3):
                for kh in range(2):
                    split_hi(act, u_in(l) + 2 * ch + kh, width=IN_WIDTH[ch])
                    if kh == 0 and ch:
                        evacuate(l, ch - 1)
            split_hi(act, u_out(l))
            evacuate(l, 2)
            act.wait_ge(p_act.sem, p_act.after((l, 2, 3)))
            act.wait_ge(p_dve.sem, p_dve.after((l, 2, 1)))
            await_ada(act, l)

        def evacuate(l, ch):
            n = IN_WIDTH[ch]
            for t in in_tiles(l, ch):
                if t >= XT:
                    await_p(act, l, ch, t)
                    nc.scalar.activation(pr[:, t, ch * 512:ch * 512 + n], ps[:, (4 if ch % 2 == 0 else 0) + t, 0:n],
                                         ACT.Copy).then_inc(p_act.sem, 1)

        def take(item):
            act.wait_ge(ring_full.sem, ring_full.after(item))
            return ring_pos[item] % 3

        def copy(out_, in_):
            return nc.scalar.activation(out_, in_, ACT.Copy)

        def square(out_, in_, **kw):
            return nc.scalar.activation(out_, in_, ACT.Square, **kw)

        def prep_squares(l, t):
            par = t % 2
            i_ = prep_items.index((l, t))
            if i_ >= 2:
                act.wait_ge(qk_done.sem, i_ - 1)
            else:
                act.wait_ge(setup_dve, 3)
            if queries(l, t):
                square(sq[:, 384 * par:384 * par + 256], pr[:, t, CQ:CKV], accum_out=ss2[:, par, 0:1])
            square(sq[:, 384 * par + 256:384 * par + 384], pr[:, t, CKV:KR], accum_out=ss2[:, par, 1:2])
            square(ps[:, 4 + par, :], pr[:, t, QS:VS]).then_inc(c_squares.sem, 1)

        def prep_root(l, t):
            act.wait_ge(c_mean.sem, c_mean.after((l, t)))
            nc.scalar.activation(rs2[:, t % 2, 0:10], ss2[:, t % 2, 0:10], ACT.Sqrt).then_inc(c_root.sem, 1)

        def prep_heads(l, t):
            q, par = queries(l, t), t % 2
            c0 = 0 if q else 2
            b = take((l, t, "c"))
            copy(ct[par][:, c0:3, :], ps[:, b, c0 * P:384].rearrange("p (k t) -> p k t", t=P)).then_inc(ring_free.sem, 1)
            i_ = prep_items.index((l, t))
            if i_:
                act.wait_ge(qk_reduced.sem, i_)
            act.wait_ge(c_squares.sem, c_squares.after((l, 2 * (t // 2) + 1)))
            if q:
                for n in range(2):
                    b = take((l, t, f"q{n}"))
                    src = ps[:, b, 0:288]
                    square(sq[:, n * 288:(n + 1) * 288], src)
                    copy(qk[par][:, 3 * n:3 * n + 3, :], src.rearrange("p (h d) -> p h d", d=QKD)).then_inc(ring_free.sem, 1)
            kr = pr[:, t, KR:QS].unsqueeze(1).to_broadcast([P, NH, QKD - HD])
            sqk = sq[:, 576:1152].rearrange("p (h d) -> p h d", d=QKD)
            copy(qk[par][:, NH:2 * NH, HD:QKD], kr)
            square(sqk[:, :, HD:QKD], kr)
            b = take((l, t, "k"))
            src = ps[:, b, 0:384].rearrange("p (h d) -> p h d", d=HD)
            square(sqk[:, :, 0:HD], src).then_inc(qk_squares.sem, 1)
            copy(qk[par][:, NH:2 * NH, 0:HD], src).then_inc(ring_free.sem, 1)
            b = take((l, t, "v"))
            copy(pr[:, t, VM:VM + 384], ps[:, b, 0:384]).then_inc(ring_free.sem, 1)

        def prep_head_root(l, t):
            h0 = 10 if queries(l, t) else 16
            act.wait_ge(qk_mean.sem, qk_mean.after((l, t)))
            nc.scalar.activation(rs2[:, t % 2, h0:22], ss2[:, t % 2, h0:22], ACT.Sqrt).then_inc(qk_root.sem, 1)

        def prep_turned(l, t):
            q = queries(l, t)
            cols = slice((t % 2) * P, (t % 2 + 1) * P)
            keys = slice(t * P, (t + 1) * P)
            for what, dst, at_ in (("tq", qt_m, cols), ("tk", kt_m, keys)):
                if what == "tq" and not q:
                    continue
                for n in range(2):
                    b = take((l, t, f"{what}{n}"))
                    h1 = min(4 * n + 4, NH)
                    copy(dst[:, 4 * n:h1, at_], ps[0:QKD, b, 0:(h1 - 4 * n) * P].rearrange("p (h t) -> p h t", t=P)).then_inc(ring_free.sem, 1)
            if q:
                b = take((l, t, "sq"))
                copy(qt_s[:, :, cols], ps[:, b, 0:384].rearrange("p (h t) -> p h t", t=P)).then_inc(ring_free.sem, 1)
            b = take((l, t, "sk"))
            copy(kt_s[:, :, keys], ps[:, b, 0:256].rearrange("p (h t) -> p h t", t=P)).then_inc(ring_free.sem, 1)

        def fourier(l, s):
            for ch in range(2):
                b = take((l, s, f"f{ch}"))
                nc.scalar.activation(fab[:, ch, :, :].rearrange("p a t -> p (a t)"), ps[:, b, :], ACT.Copy).then_inc(ring_free.sem, 1)
            b = take((l, s, "fy"))
            src = ps[:, b, :].rearrange("p (c t) -> p c t", c=2)
            nc.scalar.activation(t_hi[:, 0:2, s * 256:(s + 1) * 256], src, ACT.Copy).then_inc(fmix_hi.sem, 1)
            nc.scalar.activation(fab[:, 0, :, :], src, ACT.Copy).then_inc(ring_free.sem, 1)

        def attend(l, s):
            us = [(l, s, h, q) for h in range(2 * NH) for q in range(2)]
            nk = 4 if s == 0 else 2
            act.wait_ge(small_in, 16 * N_SMALL * (l + 1))

            def probs(n):
                _, _, h, q = u = us[n]
                g = unit_pos[u]
                act.wait_ge(nb_ready.sem, nb_ready.after(u))
                if n >= 2:
                    act.wait_ge(pt_full.sem, g - 1)
                else:
                    act.wait_ge(fmix_lo.sem, fmix_lo.after((l, s)))
                par = g % 2
                col = 10 + h if h < NH else 2 + h - NH
                e = nc.scalar.activation(pb[:, par, 0:nk * P], ps[:, 4 + par, 0:nk * P], ACT.Exp, bias=nb[:, par:par + 1],
                                         scale=rs2[:, q, col:col + 1], accum_out=sm[:, par:par + 1])
                if h >= NH:
                    e = nc.scalar.activation(esk[:, par:par + 1], sinks[:, 0, h - NH:h - NH + 1], ACT.Exp, bias=nb[:, par:par + 1])
                e.then_inc(exp_done.sem, 1)

            def copy_probs(n):
                _, _, h, q = u = us[n]
                act.wait_ge(pt_full.sem, pt_full.after(u))
                hn = heads.index((l, s, h))
                if hn >= 2:
                    act.wait_ge(o_full.sem, hn - 1)
                nc.scalar.activation(ptb[:, h % 2, 0:nk, q * P:(q + 1) * P],
                                     ps[:, 6 + unit_pos[u] % 2, 0:nk * P].rearrange("p (k t) -> p k t", t=P),
                                     ACT.Copy).then_inc(pt_copied.sem, 1)

            def mixed(h):
                act.wait_ge(o_full.sem, o_full.after((l, s, h)))
                row = 256 + HD * h
                r = row % P
                nc.scalar.activation(t_hi[r:r + 64, row // P, s * 256:(s + 1) * 256], ps[r:r + 64, 2 + h % 2, 0:256], ACT.Copy).then_inc(mix_hi.sem, 1)

            for n in range(len(us) + 5):
                if n < len(us):
                    probs(n)
                if 2 <= n < len(us) + 2:
                    copy_probs(n - 2)
                if n >= 6 and n % 2 == 0:
                    mixed((n - 6) // 2)

        def out_proj(l):
            for u in range(u_out(l) + 1, u_out(l) + OUT_UNITS):
                split_hi(act, u)

        def route(l):
            nt = len(out_tiles(l))
            split_hi(act, e_base(l, 0))
            split_hi(act, e_base(l, 0) + 1)
            act.wait_ge(lg_sum, l + 1)
            nc.scalar.activation(aff[:, 0:nt, :], gres[:, 0:nt, :], ACT.Sigmoid).then_inc(aff_ready, 1)

        def experts(l):
            def rows_hi(e, par, i):
                act.wait_ge(tg_full, plus(l * NE + e + 1, 2, i))
                if e >= 2:
                    act.wait_ge(w_used, plus(after_turn(l, e - 2), 12, i))
                nc.scalar.activation(hgt_hi[:, par, :, :], ps[:, 0:2, :].rearrange("p b (k t) -> p (b k) t", t=P),
                                     ACT.Copy).then_inc(hgt_hi_done, 1)

            def act_hi(e, i):
                act.wait_ge(ta_full, plus(l * NE + e + 1, 2, i))
                act.wait_ge(w_used, plus(after_turn(l, e) - 2, 12, i))
                nc.scalar.activation(at_hi[:], ps[:, 4, :].rearrange("p (k t) -> p k t", t=P), ACT.Copy).then_inc(at_hi_done, 1)

            def silu(e, i):
                act.wait_ge(w_used, plus(e_base(l, e) + 2, 12, i))
                if l or e:
                    act.wait_ge(a_ready, plus(l * NE + e, 2, i))
                nc.scalar.activation(s_act[:], ps[:, 2, :], ACT.Silu).then_inc(silu_done, 1)

            def gated(e, par, b, i, ei):
                act.wait_ge(w_used, plus(b + 2, 12, i))
                if l or e >= 2 or i is not None:
                    act.wait_ge(scattered[par], plus(16 * (l * 8 + e // 2), 16, i))
                for ch in range(2):
                    y = nc.scalar.activation(yb[:, par, ch * 512:(ch + 1) * 512], ps[:, 5 + ch, :], ACT.Copy,
                                             scale=gate_s[:, bass.ds(ei, 1)])
                y.then_inc(y_ready, 1)

            def turn(e, i):
                b = e_base(l, e)
                par = e % 2
                n = 6 if e else 4
                split_hi(act, b + 2, i)
                if e:
                    act_hi(e - 1, i)
                    split_hi(act, b + 3, i)
                    split_hi(act, b + 4, i)
                    silu(e, i)
                    split_hi(act, b + n - 1, i)
                else:
                    split_hi(act, b + n - 1, i)
                    silu(e, i)
                split_hi(act, b + n, i)
                if e < NE - 1:
                    rows_hi(e + 1, 1 - par, i)
                if e:
                    gated(e - 1, 1 - par, b + 2, i, plus(e - 1, 2, i))
                split_hi(act, b + n + 1, i)

            rows_hi(0, 0, None)
            turn(0, None)
            act.wait_ge(idx_ready, 2 * l + 2)
            with act.Fori(0, 7) as i:
                turn(1, i)
                turn(2, i)
            turn(NE - 1, None)
            b = e_base(l, NE)
            act_hi(NE - 1, None)
            gated(NE - 1, 1, b, None, NE - 1)

            def one_round(e, n):
                def hi(j):
                    act.wait_ge(v_landed[l][j % SPL], n * 32 + (16 + 16 * (j // SPL)))
                    if j >= SPL:
                        act.wait_ge(v_used[l], n * EXP_UNITS + (j - SPL + 1))
                    nc.scalar.activation(whi[j % SPL][:], raw[j % SPL][:], ACT.Copy).then_inc(v_hi[l], 1)

                for j in range(SPL):
                    hi(j)
                act.wait_ge(v_rows_full[l], n + 1)
                nc.scalar.activation(hgt_hi[:, 0, :, :], ps[:, 0:2, :].rearrange("p b (k t) -> p (b k) t", t=P),
                                     ACT.Copy).then_inc(v_rows_hi[l], 1)
                act.wait_ge(v_used[l], n * EXP_UNITS + 2)
                nc.scalar.activation(s_act[:], ps[:, 2, :], ACT.Silu).then_inc(v_silu[l], 1)
                for j in range(SPL, EXP_UNITS):
                    hi(j)
                act.wait_ge(v_act_full[l], n + 1)
                nc.scalar.activation(at_hi[:], ps[:, 4, :].rearrange("p (k t) -> p k t", t=P), ACT.Copy).then_inc(v_act_hi[l], 1)
                act.wait_ge(v_used[l], n * EXP_UNITS + EXP_UNITS)
                for ch in range(2):
                    y = nc.scalar.activation(yb[:, 0, ch * 512:(ch + 1) * 512], ps[:, 5 + ch, :], ACT.Copy, scale=calc_o[:, 2:3])
                y.then_inc(v_y[l], 1)
            overflow(act, l, one_round)

        ada_first(act, ada)
        act.wait_ge(const_in, 16 * N_CONST)
        nc.scalar.activation(rw[:, :, 0, :], rwf[:], ACT.Copy).then_inc(setup_act, 1)
        norm(0, 1)
        ada_last(act, ada)
        copy_rows(2 * ADA_CHUNKS - 1, None)
        for l in L:
            if l:
                norm(l, 1)
            in_proj(l)
            act.wait_ge(ring_full.sem, ring_full.after((l, "m")))
            nc.scalar.activation(mch[:].rearrange("p a b n -> p (a b n)"), ps[:, ring_pos[(l, "m")] % 3, :], ACT.Copy).then_inc(ring_free.sem, 1)
            for s in [1, 0]:
                ta, tb = 2 * s, 2 * s + 1
                for part, t in ((prep_squares, ta), (prep_squares, tb), (prep_root, ta), (prep_root, tb),
                                (prep_heads, ta), (prep_head_root, ta), (prep_heads, tb)):
                    part(l, t)
                if s in jobs(l):
                    fourier(l, s)
                for part, t in ((prep_head_root, tb), (prep_turned, ta), (prep_turned, tb)):
                    part(l, t)
                if s in jobs(l):
                    attend(l, s)
            out_proj(l)
            norm(l, 2)
            route(l)
            experts(l)

    @block.vector
    def _(dve):
        link = make_chain(dve, dve_chain)
        v = nc.vector

        nc.vector.memset(c_st[:].rearrange("p k n -> p (k n)").bitcast(F32), 0.0).then_inc(setup_dve, 1)
        v.memset(ss2[:], 1.0)
        v.memset(wbd[:], 0.0).then_inc(setup_dve, 1)
        dve.wait_ge(setup_act, 1)
        v.tensor_tensor(c_st[:, :, 2:4], c_act[:], c_st[:, :, 0:2].bitcast(F32), ALU.subtract).then_inc(setup_dve, 1)

        def ada(g0, i):
            for j in range(ADA_BODY):
                g = g0 + j
                for kh in range(2):
                    split_lo(dve, 2 * g + kh, i)
                if g >= 2:
                    take_row(g - 2, i)

        def take_row(g, i):
            dve.wait_ge(ada_comb, plus(g + 1, ADA_BODY, i))
            if g >= ROWS:
                dve.wait_ge(ada_stored[g % ROWS], plus(16 * (g // ROWS), 16 * ADA_BODY // ROWS, i))
            v.tensor_copy(row2[:, g % ROWS, :], ps[0:2, 2 + g % 2, :]).then_inc(ada_row, 1)

        def norm(l, w):
            tiles = norm_tiles(l, w)
            dve.wait_ge(ab_in[l, w], 80)
            for s in range(2):
                r = v.scalar_tensor_tensor(out=ab[:, s, 0, :], in0=ab[:, s, 0, :], scalar=1.0, in1=gb[:, 0, :] if (l, w) == (0, 1) else gain[:],
                                           op0=ALU.add, op1=ALU.mult)
            r.then_inc(ab_ready.sem, 1)
            dve.wait_ge(ab_ready.sem, ab_ready.after((l, w)))
            for t in tiles:
                dve.wait_ge(sumsq.sem, sumsq.after((l, w, t)))
                v.tensor_scalar(ms[:, t:t + 1], ss[:, t:t + 1], 1.0 / D, EPS, ALU.mult, ALU.add).then_inc(mean_ready.sem, 1)
            if w == 2:
                dve.wait_ge(op_scaled.sem, op_scaled.after((l, 1, tiles[-1])))

            def scaled(n):
                t = tiles[n]
                dve.wait_ge(rstd_ready.sem, rstd_ready.after((l, w, t)))
                if n >= 2:
                    dve.wait_ge(ht_full.sem, ht_full.after((l, w, tiles[n - 2])))
                    if w == 2:
                        dve.wait_ge(h2_stored[n % 2], 16 * ((h2_items.index((l, w, t))) // 2))
                s = stream(t)
                v.scalar_tensor_tensor(out=xn[:, n % 2, :], in0=xs[:, t, :], scalar=rstd[:, t:t + 1],
                                       in1=ab[:, s, 0, :], op0=ALU.mult, op1=ALU.mult).then_inc(h_scaled.sem, 1)

            def rest(n):
                t = tiles[n]
                b = norm_bank(l, w) + 2 * (n % 2)
                dve.wait_ge(ht_hi.sem, ht_hi.after((l, w, t)))
                sl = slice(t * P, (t + 1) * P)
                v.tensor_tensor(t_lo[:, :, sl], ps[:, b:b + 2, :].rearrange("p b (k t) -> p (b k) t", t=P),
                                t_hi[:, :, sl].bitcast(F32), ALU.subtract).then_inc(ht_split.sem, 1)

            for n in range(len(tiles) + 2):
                if n < len(tiles):
                    scaled(n)
                if n >= 2:
                    rest(n - 2)

        def in_proj(l):
            if l:
                dve.wait_ge(x_stored, 32)
            for ch in range(3):
                for kh in range(2):
                    split_lo(dve, u_in(l) + 2 * ch + kh, width=IN_WIDTH[ch])
                    if kh == 0 and ch:
                        evacuate(l, ch - 1)
            split_lo(dve, u_out(l))
            evacuate(l, 2)
            dve.wait_ge(p_act.sem, p_act.after((l, 2, 3)))
            await_ada(dve, l)

        def evacuate(l, ch):
            n = IN_WIDTH[ch]
            for t in in_tiles(l, ch):
                if t < XT:
                    await_p(dve, l, ch, t)
                    v.tensor_copy(pr[:, t, ch * 512:ch * 512 + n], ps[:, (4 if ch % 2 == 0 else 0) + t, 0:n]).then_inc(p_dve.sem, 1)

        def heads_view(ap, n):
            return ap.rearrange("p (h d) -> p h d", h=n)

        def rotate(x_, nh, w, cos, sin):
            q4 = w // 4
            swapped = ps[:, 6, 0:nh * w].rearrange("p (h d) -> p h d", h=nh)
            for a in range(4):
                o0, i0 = a * q4, (a ^ 1) * q4
                r = v.tensor_tensor(swapped[:, :, o0:o0 + q4], x_[:, :, i0:i0 + q4],
                                    sin[:, o0:o0 + q4].unsqueeze(1).to_broadcast([P, nh, q4]), ALU.mult)
            link(r)
            link(v.tensor_tensor(x_, x_, cos.unsqueeze(1).to_broadcast([P, nh, w]), ALU.mult))
            return v.tensor_tensor(x_, x_, swapped, ALU.add)

        def mean(par, c0, c1):
            a = ss2[:, par, c0:c1]
            link(v.tensor_tensor(a, a, cst[:, C_INVN + c0:C_INVN + c1], ALU.mult))
            return v.tensor_tensor(a, a, cst[:, C_INVN + 22 + c0:C_INVN + 22 + c1], ALU.add)

        def invert_roots(par, c0, c1):
            r, t, x_ = rs2[:, par, c0:c1], nr2[:, par, c0:c1], ss2[:, par, c0:c1]
            link(v.reciprocal(r, r))
            link(v.scalar_tensor_tensor(out=t, in0=r, scalar=-0.5, in1=r, op0=ALU.mult, op1=ALU.mult))
            link(v.tensor_tensor(t, t, x_, ALU.mult))
            link(v.scalar_tensor_tensor(out=r, in0=t, scalar=1.5, in1=r, op0=ALU.add, op1=ALU.mult))
            v.tensor_scalar(nr2[:, par, c0:c1], rs2[:, par, c0:c1], -1.0, None, ALU.mult)

        def prep_mean(l, t):
            par = t % 2
            dve.wait_ge(c_squares.sem, c_squares.after((l, t)))
            link(v.tensor_reduce(ss2[:, par, 2:10], heads_view(ps[:, 4 + par, :], 8), AX.X, ALU.add))
            mean(par, 0, 10).then_inc(c_mean.sem, 1)

        def prep_latents(l, t):
            q, par = queries(l, t), t % 2
            i_ = prep_items.index((l, t))
            dve.wait_ge(c_root.sem, c_root.after((l, t)))
            invert_roots(par, 0, 10)
            if i_ >= 2:
                dve.wait_ge(ring_full.sem, ring_full.after((*prep_items[i_ - 2], "c")))
            if q:
                v.scalar_tensor_tensor(out=cn[par][:, 0:256], in0=pr[:, t, CQ:CKV], scalar=rs2[:, par, 0:1], in1=gains[:, G_CQ:G_CKV],
                                       op0=ALU.mult, op1=ALU.mult)
            v.scalar_tensor_tensor(out=cn[par][:, 256:384], in0=pr[:, t, CKV:KR], scalar=rs2[:, par, 1:2], in1=gains[:, G_CKV:G_MQ],
                                   op0=ALU.mult, op1=ALU.mult).then_inc(cn_ready.sem, 1)

        def prep_windowed(l, t):
            par = t % 2
            sw = heads_view(pr[:, t, QS:VS], 8)
            link(v.tensor_tensor(sw[:, 6:8, :], sw[:, 6:8, :], rs2[:, par, 8:10].unsqueeze(2).to_broadcast([P, 2, HD]), ALU.mult))
            r = v.tensor_tensor(sw[:, 6:8, :], sw[:, 6:8, :], gains[:, G_SK:G_W].unsqueeze(1).to_broadcast([P, 2, HD]), ALU.mult)
            if queries(l, t):
                r = v.tensor_tensor(sw[:, 0:6, :], sw[:, 0:6, :], gains[:, G_SQ:G_SK].unsqueeze(1).to_broadcast([P, 6, HD]), ALU.mult)
            link(r)
            if t < XT:
                link(rotate(sw, 8, HD, rope[:, t, 64:128], rope[:, t, 128:192]))

        def prep_twice(l, t):
            i_ = prep_items.index((l, t))
            sw = heads_view(pr[:, t, QS:VS], 8)
            if i_:
                dve.wait_ge(ring_full.sem, ring_full.after((*prep_items[i_ - 1], "sk")))
            v.tensor_copy(kdup[:], sw[:, 6:8, :].unsqueeze(2).to_broadcast([P, 2, 2, HD])).then_inc(sw_done.sem, 1)

        def prep_head_mean(l, t):
            q, par = queries(l, t), t % 2
            h0 = 0 if q else NH
            dve.wait_ge(qk_squares.sem, qk_squares.after((l, t)))
            v.tensor_reduce(ss2[:, par, 10 + h0:22], heads_view(sq[:, h0 * QKD:], 2 * NH - h0), AX.X, ALU.add).then_inc(qk_reduced.sem, 1)
            dve.wait_ge(qk_reduced.sem, qk_reduced.after((l, t)))
            mean(par, 10 + h0, 22).then_inc(qk_mean.sem, 1)

        def prep_heads(l, t):
            q, par = queries(l, t), t % 2
            h0 = 0 if q else NH
            dve.wait_ge(qk_root.sem, qk_root.after((l, t)))
            invert_roots(par, 10 + h0, 22)
            dve.wait_ge(ring_free.sem, ring_free.after((l, t, "k")))
            kk = qk[par][:, NH:, :]
            link(v.tensor_tensor(kk, kk, rs2[:, par, 16:22].unsqueeze(2).to_broadcast([P, NH, QKD]), ALU.mult))
            if q:
                qr = qk[par][:, 0:NH, HD:QKD]
                v.tensor_tensor(qr, qr, gains[:, G_MQ + HD:G_MK].unsqueeze(1).to_broadcast([P, NH, QKD - HD]), ALU.mult)
            r = v.tensor_tensor(kk, kk, gains[:, G_MK:G_SQ].unsqueeze(1).to_broadcast([P, NH, QKD]), ALU.mult)
            if t < XT:
                link(r)
                r = rotate(qk[par][:, :, HD:QKD], 12, 32, rope[:, t, 0:32], rope[:, t, 32:64])
            r.then_inc(qk_done.sem, 1)

        def fourier(l, s):
            dve.wait_ge(fmix_hi.sem, fmix_hi.after((l, s)))
            dve.wait_ge(ring_free.sem, ring_free.after((l, s, "fy")))
            sl = slice(s * 256, (s + 1) * 256)
            v.tensor_tensor(t_lo[:, 0:2, sl], fab[:, 0, :, :], t_hi[:, 0:2, sl].bitcast(F32), ALU.subtract).then_inc(fmix_lo.sem, 1)

        def attend(l, s):
            us = [(l, s, h, q) for h in range(2 * NH) for q in range(2)]
            nk = 4 if s == 0 else 2

            def biggest(n):
                _, _, h, q = u = us[n]
                par = unit_pos[u] % 2
                dve.wait_ge(s_full.sem, s_full.after(u))
                if unit_pos[u] >= 2:
                    dve.wait_ge(exp_done.sem, unit_pos[u] - 1)
                link(v.tensor_reduce(mx[:, par:par + 1], ps[:, 4 + par, 0:nk * P], AX.X, ALU.max))
                if h < NH:
                    r = v.tensor_scalar(nb[:, par:par + 1], mx[:, par:par + 1], nr2[:, q, 10 + h:11 + h], None, ALU.mult)
                else:
                    r = v.tensor_scalar(nb[:, par:par + 1], mx[:, par:par + 1], nr2[:, q, h - 4:h - 3],
                                        sinks[:, 1, h - NH:h - NH + 1], ALU.mult, ALU.min)
                r.then_inc(nb_ready.sem, 1)

            def invert(n):
                _, _, h, q = u = us[n]
                par = unit_pos[u] % 2
                dve.wait_ge(exp_done.sem, exp_done.after(u))
                if h >= NH:
                    link(v.tensor_tensor(sm[:, par:par + 1], sm[:, par:par + 1], esk[:, par:par + 1], ALU.add))
                link(v.reciprocal(sm[:, par:par + 1], sm[:, par:par + 1]))
                v.tensor_scalar(pb[:, par, 0:nk * P], pb[:, par, 0:nk * P], sm[:, par:par + 1], None, ALU.mult).then_inc(p_norm.sem, 1)

            def mixed(h):
                dve.wait_ge(mix_hi.sem, mix_hi.after((l, s, h)))
                row = 256 + HD * h
                r = row % P
                sl = slice(s * 256, (s + 1) * 256)
                v.tensor_tensor(t_lo[r:r + 64, row // P, sl], ps[r:r + 64, 2 + h % 2, 0:256],
                                t_hi[r:r + 64, row // P, sl].bitcast(F32), ALU.subtract).then_inc(mix_lo.sem, 1)

            for n in range(len(us) + 5):
                if n < len(us):
                    biggest(n)
                if 1 <= n < len(us) + 1:
                    invert(n - 1)
                if n >= 6 and n % 2 == 0:
                    mixed((n - 6) // 2)

        def out_proj(l):
            def scale(ch):
                for t in out_tiles(l):
                    n = out_items.index((l, ch, t))
                    await_op(dve, l, ch, t)
                    if n >= 2:
                        dve.wait_ge(x_upd.sem, n - 1)
                    v.tensor_tensor(otmp[:, n % 2, :], ps[:, (4 if ch == 0 else 0) + t, :],
                                    gb[:, stream(t), ch * 512:(ch + 1) * 512], ALU.mult).then_inc(op_scaled.sem, 1)
            for n in range(1, OUT_UNITS):
                split_lo(dve, u_out(l) + n)
                if n == 2:
                    dve.wait_ge(gb_in, 32 * (2 * l + 1))
                    scale(0)
            scale(1)

        def route(l):
            nt = len(out_tiles(l))
            ng = nt * 4
            split_lo(dve, e_base(l, 0))
            split_lo(dve, e_base(l, 0) + 1)
            dve.wait_ge(lg_full, l + 1)
            lg = ps[:, 4, 0:nt * 2 * NE].rearrange("p (t a e) -> p t a e", a=2, e=NE)
            link(v.tensor_copy(gate[:, 0:nt, :], lg[:, :, 1, :]))
            v.tensor_tensor(gres[:, 0:nt, :], gate[:, 0:nt, :], lg[:, :, 0, :], ALU.add).then_inc(lg_sum, 1)
            dve.wait_ge(aff_ready, l + 1)
            if l:
                dve.wait_ge(y_ready, NE * l)
            af, se, cn_, mk = (a[:, 0:nt, :] for a in (aff, sel, cnt, msk))

            def flat(a):
                return a.rearrange("p t e -> p (t e)")

            def ranks(vals, n, out_):
                vi = vals.rearrange("p (g i) -> p g i", i=4)
                a_i = vi.unsqueeze(2).to_broadcast([P, n, 4, 4])
                a_j = vi.unsqueeze(3).to_broadcast([P, n, 4, 4])
                lt = cst[:, C_LT:C_LT + 16]
                v.tensor_tensor(pair[:, 0:n], a_i, a_j, ALU.is_gt)
                link(v.tensor_tensor(pair2[:, 0:n], a_i, a_j, ALU.is_ge))
                p2 = pair2[:, 0:n].rearrange("p g j i -> p g (j i)")
                p1 = pair[:, 0:n].rearrange("p g j i -> p g (j i)")
                link(v.tensor_tensor(p2, p2, lt.unsqueeze(1).to_broadcast([P, n, 16]), ALU.mult))
                link(v.tensor_tensor(p1, p1, p2, ALU.max))
                link(v.tensor_reduce(out_, pair[:, 0:n], AX.X, ALU.add))

            link(v.tensor_tensor(se, af, rb[:].unsqueeze(1).to_broadcast([P, nt, NE]), ALU.add))
            vi = flat(se).rearrange("p (g i) -> p g i", i=4)
            link(v.tensor_tensor(pair[:, 0:ng], vi.unsqueeze(2).to_broadcast([P, ng, 4, 4]),
                                 vi.unsqueeze(3).to_broadcast([P, ng, 4, 4]), ALU.add))
            p1 = pair[:, 0:ng].rearrange("p g j i -> p g (j i)")
            link(v.tensor_tensor(p1, p1, cst[:, C_DIAG:C_DIAG + 16].unsqueeze(1).to_broadcast([P, ng, 16]), ALU.add))
            gs = flat(gsc[:, 0:nt, :])
            link(v.tensor_reduce(gs, p1, AX.X, ALU.max))
            ranks(gs, nt, gcnt[:, 0:nt, :])
            link(v.tensor_scalar(best[:, 0:nt, :], gcnt[:, 0:nt, :], 0.0, None, ALU.is_equal))
            ranks(flat(se), ng, flat(cn_).rearrange("p (g i) -> p g i", i=4))
            link(v.tensor_scalar(flat(mk), flat(cn_), 2.0, None, ALU.is_lt))
            m4 = flat(mk).rearrange("p (g i) -> p g i", i=4)
            link(v.tensor_tensor(m4, m4, flat(best[:, 0:nt, :]).unsqueeze(2).to_broadcast([P, ng, 4]), ALU.mult))
            v.tensor_copy(mskb[:, 0:nt, :], mk).then_inc(msk_ready, 1)
            ga, gr = gate[:, 0:nt, :], gres[:, 0:nt, :]
            link(v.tensor_tensor(ga, af, mk, ALU.mult))
            link(v.tensor_reduce(den[:, 0:nt], ga, AX.X, ALU.add))
            link(v.reciprocal(den[:, 4:4 + nt], den[:, 0:nt]))
            link(v.tensor_tensor(ga, ga, den[:, 4:4 + nt].unsqueeze(2).to_broadcast([P, nt, NE]), ALU.mult))
            py = pay[:, 0:nt]
            v.tensor_copy(py[:, :, :, 4], ga)
            v.tensor_copy(py[:, :, :, 2], cn_)
            link(v.memset(py[:, :, :, 3], 1.0))
            link(v.tensor_tensor(gr, ga, py[:, :, :, 4], ALU.subtract))
            link(v.tensor_copy(py[:, :, :, 5], gr))
            link(v.tensor_tensor(gr, gr, py[:, :, :, 5], ALU.subtract))
            v.tensor_copy(py[:, :, :, 6], gr)
            v.memset(py[:, :, :, 7], 0.0)
            for t in range(nt):
                v.memset(py[:, t, :, 0], float(t))
            v.tensor_copy(py[:, :, :, 1].rearrange("p t e -> p t e"),
                          cst[:, C_TOK:C_TOK + 1].unsqueeze(2).to_broadcast([P, nt, NE]))
            link(v.tensor_copy(iota16[:], cst[:, C_IOTA:C_IOTA + P]))
            dve.wait_ge(pos_full, l + 1)
            link(v.tensor_reduce(den[:, 0:1], ps[:, 5, nt * NE:(nt + 1) * NE], AX.X, ALU.max))
            v.tensor_copy(most[:], den[:, 0:1])
            po = posf[:, 0:nt, :]
            link(v.scalar_tensor_tensor(out=flat(po), in0=ps[:, 5, 0:nt * NE], scalar=1.0, in1=flat(mk), op0=ALU.add, op1=ALU.mult))
            link(v.tensor_scalar(flat(posm[:, 0:nt, :]), flat(po), -1.0, None, ALU.add))
            for e in range(NE):
                if e >= 2:
                    dve.wait_ge(oh_used, l * NE + e - 1)
                if e == 2:
                    slots(l, 0, 2)
                if e == EARLY + 2:
                    rows_lo(l, 0, 0, None)
                v.tensor_tensor(oh[:, e % 2, 0:nt, :], iota16[:].unsqueeze(1).to_broadcast([P, nt, P]),
                                posm[:, 0:nt, e].unsqueeze(2).to_broadcast([P, nt, P]), ALU.is_equal).then_inc(oh_ready, 1)
            slots(l, 2, NE)

        def slots(l, e0, e1):
            dve.wait_ge(oh_used, l * NE + e1)
            es_ = slice(e0, e1)
            link(v.tensor_copy(info[:, es_, :].rearrange("p e n -> p (e n)"), ps[:, 6, e0 * 8:e1 * 8]))
            v.tensor_scalar(oobf[:, es_], info[:, es_, 3], -float(BIG), float(BIG), ALU.mult, ALU.add)
            v.tensor_tensor(gate_s[:, es_], info[:, es_, 6], info[:, es_, 5], ALU.add)
            link(v.scalar_tensor_tensor(out=tokf[:, es_], in0=info[:, es_, 0], scalar=float(P), in1=info[:, es_, 1], op0=ALU.mult, op1=ALU.add))
            v.tensor_tensor(gate_s[:, es_], gate_s[:, es_], info[:, es_, 4], ALU.add)
            v.tensor_tensor(idxg[:, es_], tokf[:, es_], oobf[:, es_], ALU.add)
            link(v.scalar_tensor_tensor(out=tokf[:, es_], in0=tokf[:, es_], scalar=2.0, in1=info[:, es_, 2], op0=ALU.mult, op1=ALU.add))
            v.tensor_tensor(idxs[:, es_], tokf[:, es_], oobf[:, es_], ALU.add).then_inc(idx_ready, 1)

        def rows_lo(l, e, par, i):
            dve.wait_ge(hgt_hi_done, plus(l * NE + e + 1, 2, i))
            v.tensor_tensor(hgt_lo[:, par, :, :], ps[:, 0:2, :].rearrange("p b (k t) -> p (b k) t", t=P),
                            hgt_hi[:, par, :, :].bitcast(F32), ALU.subtract).then_inc(hgt_split, 1)

        def experts(l):
            def act_lo(e, i):
                dve.wait_ge(at_hi_done, plus(l * NE + e + 1, 2, i))
                v.tensor_tensor(at_lo[:], ps[:, 4, :].rearrange("p (k t) -> p k t", t=P), at_hi[:].bitcast(F32),
                                ALU.subtract).then_inc(at_split, 1)

            def swiglu(e, b, i):
                dve.wait_ge(w_used, plus(b, 12, i))
                dve.wait_ge(silu_done, plus(l * NE + e + 1, 2, i))
                if l or e or i is not None:
                    dve.wait_ge(ta_full, plus(l * NE + e, 2, i))
                v.tensor_tensor(a_act[:], s_act[:], ps[:, 3, :], ALU.mult).then_inc(a_ready, 1)

            def turn(e, i):
                b = e_base(l, e)
                par = e % 2
                if e:
                    swiglu(e - 1, b, i)
                split_lo(dve, b + 2, i)
                if e:
                    act_lo(e - 1, i)
                    split_lo(dve, b + 3, i)
                    split_lo(dve, b + 4, i)
                n = 6 if e else 4
                split_lo(dve, b + n - 1, i)
                split_lo(dve, b + n, i)
                if e < NE - 1:
                    rows_lo(l, e + 1, 1 - par, i)
                split_lo(dve, b + n + 1, i)

            turn(0, None)
            with dve.Fori(0, 7) as i:
                turn(1, i)
                turn(2, i)
            turn(NE - 1, None)
            b = e_base(l, NE)
            swiglu(NE - 1, b, None)
            act_lo(NE - 1, None)

            nt = len(out_tiles(l))
            STEPS = 4

            def further(c):
                dve.wait_ge(v_turn[l], c * NE + 1)
                v.tensor_scalar(posm[:, 0:nt, :].rearrange("p t e -> p (t e)"), posm[:, 0:nt, :].rearrange("p t e -> p (t e)"),
                                -float(SLOTS), None, ALU.add).then_inc(v_shift[l], 1)

            def one_round(e, n):
                def step(ins, k):
                    ins.then_inc(v_step[l], 1)
                    dve.wait_ge(v_step[l], n * STEPS + k)

                def lo(j):
                    dve.wait_ge(v_hi[l], n * EXP_UNITS + (j + 1))
                    v.tensor_tensor(wlo[j % SPL][:], raw[j % SPL][:], whi[j % SPL][:].bitcast(F32), ALU.subtract).then_inc(v_lo[l], 1)

                v.tensor_tensor(oh[:, 0, 0:nt, :], iota16[:].unsqueeze(1).to_broadcast([P, nt, P]),
                                posm[:, 0:nt, bass.ds(e, 1)].to_broadcast([P, nt, P]), ALU.is_equal).then_inc(v_oh[l], 1)
                dve.wait_ge(v_info[l], n + 1)
                step(v.tensor_copy(info_o[:], ps[:, 7, 0:8]), 1)
                v.tensor_scalar(calc_o[:, 0:1], info_o[:, 3:4], -float(BIG), float(BIG), ALU.mult, ALU.add)
                v.tensor_tensor(calc_o[:, 3:4], info_o[:, 6:7], info_o[:, 5:6], ALU.add)
                step(v.scalar_tensor_tensor(out=calc_o[:, 1:2], in0=info_o[:, 0:1], scalar=float(P), in1=info_o[:, 1:2],
                                            op0=ALU.mult, op1=ALU.add), 2)
                v.tensor_tensor(calc_o[:, 2:3], calc_o[:, 3:4], info_o[:, 4:5], ALU.add)
                step(v.tensor_tensor(idx_o[:, 0:1], calc_o[:, 1:2], calc_o[:, 0:1], ALU.add), 3)
                step(v.scalar_tensor_tensor(out=calc_o[:, 1:2], in0=calc_o[:, 1:2], scalar=2.0, in1=info_o[:, 2:3],
                                            op0=ALU.mult, op1=ALU.add), 4)
                v.tensor_tensor(idx_o[:, 1:2], calc_o[:, 1:2], calc_o[:, 0:1], ALU.add).then_inc(v_idx[l], 1)
                for j in range(SPL):
                    lo(j)
                dve.wait_ge(v_rows_hi[l], n + 1)
                v.tensor_tensor(hgt_lo[:, 0, :, :], ps[:, 0:2, :].rearrange("p b (k t) -> p (b k) t", t=P),
                                hgt_hi[:, 0, :, :].bitcast(F32), ALU.subtract).then_inc(v_rows_lo[l], 1)
                for j in range(SPL, EXP_UNITS):
                    lo(j)
                dve.wait_ge(v_silu[l], n + 1)
                dve.wait_ge(v_used[l], n * EXP_UNITS + 4)
                v.tensor_tensor(a_act[:], s_act[:], ps[:, 3, :], ALU.mult).then_inc(v_act[l], 1)
                dve.wait_ge(v_act_hi[l], n + 1)
                v.tensor_tensor(at_lo[:], ps[:, 4, :].rearrange("p (k t) -> p k t", t=P), at_hi[:].bitcast(F32),
                                ALU.subtract).then_inc(v_act_lo[l], 1)
            overflow(dve, l, one_round, further)

        def finish(l):
            dve.wait_ge(gb_in, 32 * (2 * l + 2))
            for n, t in enumerate(out_tiles(l)):
                f = fin_items.index((l, t))
                dve.wait_ge(y_in[f % 4], 16 * (f // 4 + 1))
                y0, y1 = (yy[y_buf(f)][:, n, :] for n in range(2))
                link(v.tensor_tensor(y0, y0, y1, ALU.add))
                v.tensor_tensor(y0, y0, gb[:, stream(t), :], ALU.mult).then_inc(y_sum.sem, 1)

        ada_first(dve, ada)
        dve.wait_ge(setup_act, 2)
        v.tensor_tensor(rw[:, :, 1, :], rwf[:], rw[:, :, 0, :].bitcast(F32), ALU.subtract).then_inc(setup_dve, 1)
        v.tensor_copy(cstb[:], cb_raw[:]).then_inc(setup_dve, 1)
        norm(0, 1)
        ada_last(dve, ada)
        take_row(2 * ADA_CHUNKS - 2, None)
        take_row(2 * ADA_CHUNKS - 1, None)
        for l in L:
            if l:
                norm(l, 1)
            in_proj(l)
            dve.wait_ge(small_in, 16 * N_SMALL * (l + 1))
            link(v.tensor_scalar(sinks[:, 1, :], sinks[:, 0, :], -1.0, None, ALU.mult))
            kg = gains[:, G_MK:G_MK + HD]
            link(v.tensor_tensor(kg, kg, gains[:, G_MQ:G_MQ + HD], ALU.mult))
            for s in [1, 0]:
                ta, tb = 2 * s, 2 * s + 1
                for part, t in ((prep_mean, ta), (prep_mean, tb), (prep_latents, ta), (prep_latents, tb),
                                (prep_windowed, ta), (prep_twice, ta), (prep_head_mean, ta), (prep_heads, ta),
                                (prep_head_mean, tb), (prep_windowed, tb)):
                    part(l, t)
                if s in jobs(l):
                    fourier(l, s)
                prep_heads(l, tb)
                prep_twice(l, tb)
                if s in jobs(l):
                    attend(l, s)
            out_proj(l)
            norm(l, 2)
            route(l)
            experts(l)
            finish(l)

    @block.gpsimd
    def _(pool):
        link = make_chain(pool, pool_chain)
        g_ = nc.gpsimd
        def bound(last, e, i):
            return last if i is None else plus(e, 2, i) | last


        pool.dma_start(xs[:, 0:XT, :], x[0].rearrange("(t p) d -> p t d", p=P)).then_inc(x_in, 16)
        pool.dma_start(xs[:, XT:, :], ctx[0].rearrange("(t p) d -> p t d", p=P)).then_inc(x_in, 16)

        def load_small(l):
            def get(dst, src):
                pool.dma_start(dst, src).then_inc(small_in, 16)
            get(w_uq[:], mla_w_uq[l].rearrange("(k p) n -> p k n", p=P))
            get(w_ukv[:, 0, :], mla_w_uk[l])
            get(w_ukv[:, 1, :], mla_w_uv[l])
            for g0, g1, src in ((G_CQ, G_CKV, mla_cq_g), (G_CKV, G_MQ, mla_ckv_g), (G_MQ, G_MK, mla_q_g),
                                (G_MK, G_SQ, mla_k_g), (G_SQ, G_SK, swa_q_g), (G_SK, G_W, swa_k_g)):
                get(gains[:, g0:g1], row_bc(src, l, g1 - g0))
            get(sinks[:, 0, :], row_bc(swa_sink, l, NH))
            for n in range(4):
                r = 64 * (n % 2)
                get(wbd[r:r + 64, n // 2, r:r + 64], fnet_w[l, n])


        for n in range(2):
            pool.dma_start(ada_d[n:n + 1, :], ada_b.rearrange("(a l) n -> a (l n)", a=1)).then_inc(ada_bias_in, 16)

        def ada_rows(n, count):
            with pool.Fori(0, count) as i:
                for r in range(ROWS):
                    g = r + ROWS * n
                    pool.wait_ge(ada_row, plus(g + 1, ROWS, i))
                    pool.dma_start(ada_d[:, bass.ds(plus(g * CHUNK, ROWS * CHUNK, i), CHUNK)], row2[:, r, :],
                                   accum_op=ALU.add).then_inc(ada_stored[r], 16)

        def load_gates(l, w):
            for s in range(2):
                pool.dma_start(gb[:, s, :], ab_src(s, l, 3 * w - 1)).then_inc(gb_in, 16)

        def norm(l, w):
            tiles = norm_tiles(l, w)

            def inverse_root(n):
                t = tiles[n]
                pool.wait_ge(mean_ready.sem, mean_ready.after((l, w, t)))
                g_.tensor_tensor(rstd[:, t:t + 1], ms[:, t:t + 1], half[:, 0:1], ALU.pow).then_inc(rstd_ready.sem, 1)

            inverse_root(0)
            for n, t in enumerate(tiles):
                if n + 1 < len(tiles):
                    inverse_root(n + 1)
                pool.wait_ge(h_scaled.sem, h_scaled.after((l, w, t)))
                g_.tensor_tensor(xn[:, n % 2, :], xn[:, n % 2, :], ab[:, stream(t), 1, :], ALU.add).then_inc(h_ready.sem, 1)

        def gather(l, e, i, first=False):
            par = e % 2
            if not first:
                pool.wait_ge(tg_full, plus(l * NE + e - 1, 2, i))
            if l or not first:
                pool.wait_ge(gathered[par], plus(16 * (l * 8 + e // 2), 16, i))
            g_.tensor_copy(cur_g[:, par:par + 1], idxg[:, bass.ds(plus(e, 2, i), 1)]).then_inc(cur_g_ready, 1)
            pool.wait_ge(cur_g_ready, plus(l * NE + e + 1, 2, i))
            g_.indirect_dma_start(out=hg[:, par, :], out_offset=None, in_=h2_d,
                                  in_offset=bass.IndirectOffsetOnAxis(ap=cur_g[:, par:par + 1], axis=0),
                                  bounds_check=bound(NTILES * P - 1, e, i), oob_is_err=False).then_inc(gathered[par], 16)

        def scatter(l, e, i):
            par = e % 2
            pool.wait_ge(y_ready, plus(l * NE + e + 1, 2, i))
            if l or e >= 2 or i is not None:
                pool.wait_ge(scattered[par], plus(16 * (l * 8 + e // 2), 16, i))
            g_.tensor_copy(cur_s[:, par:par + 1], idxs[:, bass.ds(plus(e, 2, i), 1)]).then_inc(cur_s_ready, 1)
            pool.wait_ge(cur_s_ready, plus(l * NE + e + 1, 2, i))
            g_.indirect_dma_start(out=y_d, out_offset=bass.IndirectOffsetOnAxis(ap=cur_s[:, par:par + 1], axis=0),
                                  in_=yb[:, par, :], in_offset=None,
                                  bounds_check=bound(2 * NTILES * P - 1, e, i), oob_is_err=False).then_inc(scattered[par], 16)

        rounds = ADA_CHUNKS // ROWS
        done = (3 * ADA_BODY - 2) // ROWS
        pool.wait_ge(ada_bias_in, 32)
        ada_rows(0, rounds)
        for r in range(ROWS):
            pool.wait_ge(ada_stored[r], 16 * rounds)
        load_ab(pool, 0, 1)
        ada_rows(rounds, done - rounds)
        norm(0, 1)
        ada_rows(done, 2 * rounds - done)
        pool.wait_ge(setup_dve, 2)
        load_small(0)
        for l in L:
            for r in range(ROWS):
                pool.wait_ge(ada_stored[r], 32 * rounds)
            if l:
                norm(l, 1)
            pool.wait_ge(mix_lo.sem, mix_lo.after((l, 0, 2 * NH - 1)))
            if l == 0:
                load_small(1)
                pool.dma_start(xs[:, XT:, :], ctx[0].rearrange("(t p) d -> p t d", p=P)).then_inc(x_in, 16)
                pool.dma_start(xs[:, 0:XT, :], x[0].rearrange("(t p) d -> p t d", p=P)).then_inc(x_in, 16)
            else:
                pool.dma_start(xs[:, 0:XT, :], x_d.rearrange("(t p) d -> p t d", p=P)).then_inc(x_in, 16)
            load_gates(l, 1)
            load_ab(pool, l, 2)
            pool.wait_ge(x_in, (64, 80)[l])
            for ch in range(2):
                for t in out_tiles(l):
                    n = out_items.index((l, ch, t))
                    pool.wait_ge(op_scaled.sem, n + 1)
                    sl = slice(ch * 512, (ch + 1) * 512)
                    g_.tensor_tensor(xs[:, t, sl], xs[:, t, sl], otmp[:, n % 2, :], ALU.add).then_inc(x_upd.sem, 1)
            load_gates(l, 2)
            norm(l, 2)
            stored = [h2_items.index(it) for it in h2_items if it[0] == l]
            for par in range(2):
                pool.wait_ge(h2_stored[par], 16 * (max(stored) // 2 + 1))
            pool.wait_ge(ht_full.sem, ht_full.after((l, 2, out_tiles(l)[-1])))
            pool.wait_ge(idx_ready, 2 * l + 1)
            gather(l, 0, None, True)
            gather(l, 1, None, True)
            pool.wait_ge(idx_ready, 2 * l + 2)
            with pool.Fori(0, 7) as i:
                for e in range(2):
                    gather(l, e + 2, i)
                    scatter(l, e, i)
            scatter(l, NE - 2, None)
            scatter(l, NE - 1, None)
            for par in range(2):
                pool.wait_ge(scattered[par], 16 * 8 * (l + 1))
            pool.wait_ge(w_used, u_exp(l) + NE * EXP_UNITS)
            g_.tensor_tensor(tick[:], half[:, 0:1], half[:, 0:1], ALU.mult).then_inc(v_turn[l], 1)

            def one_round(e, n):
                pool.wait_ge(v_idx[l], n + 1)
                g_.indirect_dma_start(out=hg[:, 0, :], out_offset=None, in_=h2_d,
                                      in_offset=bass.IndirectOffsetOnAxis(ap=idx_o[:, 0:1], axis=0),
                                      bounds_check=e | NTILES * P - 1, oob_is_err=False).then_inc(v_gathered[l], 16)
                pool.wait_ge(v_y[l], n + 1)
                g_.indirect_dma_start(out=y_d, out_offset=bass.IndirectOffsetOnAxis(ap=idx_o[:, 1:2], axis=0),
                                      in_=yb[:, 0, :], in_offset=None,
                                      bounds_check=e | 2 * NTILES * P - 1, oob_is_err=False).then_inc(v_scattered[l], 16)
                pool.wait_ge(v_scattered[l], n * 16 + 16)
                g_.tensor_tensor(tick[:], half[:, 0:1], half[:, 0:1], ALU.mult).then_inc(v_turn[l], 1)
            overflow(pool, l, one_round)

            tiles = out_tiles(l)
            for n, t in enumerate(tiles):
                f = fin_items.index((l, t))
                pool.wait_ge(y_sum.sem, f + 1)
                g_.tensor_tensor(xs[:, t, :], xs[:, t, :], yy[y_buf(f)][:, 0, :], ALU.add).then_inc(x_fin.sem, 1)
                pool.wait_ge(x_fin.sem, f + 1)
                if t < XT:
                    dst = (x_d if l == 0 else out[0])[t * P:(t + 1) * P, :]
                    pool.dma_start(dst, xs[:, t, :]).then_inc(x_stored, 16)
        pool.wait_ge(x_stored, 64)

    es.close()


def shape_constants():
    import numpy as np

    def dft_pair(n):
        k = np.arange(n)
        a = 2 * np.pi * ((k[:, None] * k[None, :]) % n) / n
        return np.cos(a), np.sin(a)

    cst = np.zeros((P, CONST_W + P), np.float32)
    cst[:, C_ID:C_ID + P] = np.eye(P)
    ct_, st_ = dft_pair(SEQ)
    both = np.concatenate([ct_, st_], 1).reshape(2, P, 512)
    cst[:, C_DFT:C_DFT + 1024] = both.transpose(1, 0, 2).reshape(P, 1024)
    cc, sc = dft_pair(64)
    norm = 1.0 / np.sqrt(SEQ * 64)
    for n, m in enumerate((cc * norm, -sc * norm)):
        for g in range(2):
            cst[64 * g:64 * g + 64, C_CHAN + n * P + 64 * g:C_CHAN + n * P + 64 * g + 64] = m
    tok = np.arange(SEQ)
    col = C_ROPE
    parts = []
    for w in (32, 64):
        inv = np.float32(10000.0) ** (-np.arange(0, w // 2, 2, dtype=np.float32) / np.float32(w // 2))
        ar = (tok // 64).astype(np.float32)[:, None] * inv
        ac = (tok % 64).astype(np.float32)[:, None] * inv
        ang = np.concatenate([ar, ar, ac, ac], 1)
        sign = np.tile(np.repeat([-1.0, 1.0], w // 4), 2)
        parts += [np.cos(ang), np.sin(ang) * sign]
    rope_ = np.concatenate(parts, 1).reshape(2, P, 192)
    cst[:, C_ROPE:C_ROPE + 384] = rope_.transpose(1, 0, 2).reshape(P, 384)
    cst[:, C_IOTA:C_IOTA + P] = np.arange(P)
    j, i = np.meshgrid(np.arange(4), np.arange(4), indexing="ij")
    cst[:, C_LT:C_LT + 16] = (i < j).reshape(-1)
    cst[:, C_DIAG:C_DIAG + 16] = np.where(i == j, -1e30, 0.0).reshape(-1)
    width = np.array([256, 128] + [HD] * 8 + [QKD] * 12, np.float64)
    query = np.array([False] * 2 + [True] * 6 + [False] * 2 + [True] * 6 + [False] * 6)
    cst[:, C_INVN:C_INVN + 22] = np.where(query, 1, 1 / width)
    cst[:, C_INVN + 22:C_INVN + 44] = np.where(query, width, 1) * EPS
    cst[:, C_HALF:C_HALF + 4] = -0.5
    cst[0:4, CONST_W:CONST_W + 2] = [[1, 0], [0, 1], [1, 0], [0, 1]]
    cst[:, C_TOK] = np.arange(P)
    cb = np.zeros((P, CONST_B), np.float32)
    cb[:, B_ID:B_ID + P] = np.eye(P)
    keys = np.arange(SEQ)
    for q in range(2):
        rel = keys[None, :] - (q * P + np.arange(P))[:, None]
        cb[:, B_MASK + q * 256:B_MASK + (q + 1) * 256] = np.where(np.abs(rel) <= 128, 0.0, -1e30)
    cb[:, B_TRI:B_TRI + P] = np.arange(P)[:, None] < np.arange(P)[None, :]
    cb[:, B_ONE:B_ONE + P] = 1.0
    return cst, cb


_INS = ["x", "c", "ctx", "c_ctx", "ada_w", "ada_b", "norm1_g", "norm2_g", "w_in", "fnet_w", "mla_cq_g", "mla_ckv_g",
        "mla_w_uq", "mla_w_uk", "mla_w_uv", "mla_q_g", "mla_k_g", "swa_q_g", "swa_k_g", "swa_sink", "w_out",
        "router_w", "router_b", "exp_w_gate", "exp_w_up", "exp_w_down"]


def kernel(**inputs):
    import numpy as np
    import concourse.bacc as bacc
    from concourse.bass_utils import run_bass_kernel_spmd

    nc = bacc.Bacc("TRN2", target_bir_lowering=False, num_devices=1)
    cst, cb = shape_constants()
    arrays, args = {}, []
    for name in _INS + ["consts", "consts_b"]:
        a = np.ascontiguousarray({"consts": cst, "consts_b": cb}.get(name, inputs.get(name)))
        arrays[f"in_{name}"] = a
        args.append(nc.dram_tensor(f"in_{name}", a.shape, mybir.dt.from_np(a.dtype), kind="ExternalInput").ap())
    out = nc.dram_tensor("out_0", (1, SEQ, D), F32, kind="ExternalOutput").ap()
    build(nc, *args, out)
    r = run_bass_kernel_spmd(nc, [arrays], core_ids=[0])
    return r.results[0]["out_0"]
```
